# Optimizing a Trainium2 kernel written in Bass

```python
import jax, jax.numpy as jnp
from jax import lax
import numpy as np

D_MODEL = 2048
BATCH = 1
SEQ = 256
DEPTH = 1

MEM_LEN = 256
EPS = 1e-6
D_FF = 5504

RW_HEADS = 16
RW_HEAD_DIM = 64
RW_WIDTH = RW_HEADS * RW_HEAD_DIM
RW_DECAY_LORA = 64
RW_ICLR_LORA = 64
RW_GATE_LORA = 160
RW_GN_EPS = 64e-5
RW_SPLITS = (RW_WIDTH, RW_WIDTH, RW_WIDTH, RW_DECAY_LORA, RW_ICLR_LORA, RW_GATE_LORA)
RW_COLS = 3 * RW_WIDTH + RW_DECAY_LORA + RW_ICLR_LORA + RW_GATE_LORA

NSA_HEADS = 16
NSA_KV_GROUPS = 4
NSA_HPG = NSA_HEADS // NSA_KV_GROUPS
NSA_HEAD_DIM = 64
NSA_WIDTH = NSA_HEADS * NSA_HEAD_DIM
NSA_KV_WIDTH = NSA_KV_GROUPS * NSA_HEAD_DIM
NSA_SPLITS = (NSA_WIDTH, NSA_KV_WIDTH, NSA_KV_WIDTH, NSA_KV_WIDTH, NSA_KV_WIDTH, NSA_KV_WIDTH, NSA_KV_WIDTH, 3 * NSA_HEADS)
NSA_COLS = NSA_WIDTH + 6 * NSA_KV_WIDTH + 3 * NSA_HEADS
CMP_BLOCK = 32
CMP_STRIDE = 16
CMP_HIDDEN = 128
SEL_BLOCK = 64
SEL_TOPK = 16
WINDOW = 512
Q_BLOCK = 128
FORCE_BONUS = 1000.0

ROPE_THETA = 500000.0
ROPE_DIM = NSA_HEAD_DIM // 4

MIX_WIDTH = RW_WIDTH + NSA_WIDTH
IN_COLS = RW_COLS + NSA_COLS

MEM_HEADS = 4
MEM_HEAD_DIM = 128
MEM_WIDTH = MEM_HEADS * MEM_HEAD_DIM

kernel_name = 'hymba_rwkv7_nsa_macaron_memory'

F32 = jnp.float32

def rmsnorm(x, g):
    xf = x.astype(F32)
    y = xf * lax.rsqrt(jnp.mean(xf * xf, axis=-1, keepdims=True) + EPS)
    return (y * g.astype(F32)).astype(x.dtype)

def swiglu(x, w_gate, w_up, w_down):
    return (jax.nn.silu(x @ w_gate) * (x @ w_up)) @ w_down

def split_cols(x, sizes):
    offs = np.cumsum(np.array(sizes))[:-1].tolist()
    return jnp.split(x, offs, axis=-1)

def token_shift(f, mu):
    prev = jnp.pad(f, ((0, 0), (1, 0), (0, 0)))[:, :-1]
    return f + mu * (prev - f)

def partial_rope(x, pos):
    half = ROPE_DIM // 2
    inv_freq = ROPE_THETA ** (-jnp.arange(half, dtype=F32) * 2.0 / ROPE_DIM)
    ang = pos.astype(F32)[:, None] * inv_freq[None, :]
    cos = jnp.cos(ang)[None, :, None, :]
    sin = jnp.sin(ang)[None, :, None, :]
    x1 = x[..., :half].astype(F32)
    x2 = x[..., half:ROPE_DIM].astype(F32)
    rot = jnp.concatenate([x1 * cos - x2 * sin, x2 * cos + x1 * sin], axis=-1).astype(x.dtype)
    return jnp.concatenate([rot, x[..., ROPE_DIM:]], axis=-1)

def masked_softmax(s, mask):
    s = jnp.where(mask, s.astype(F32), -1e30)
    return jax.nn.softmax(s, axis=-1) * mask

def rwkv7_group(f, mu, w0, w_up, a0, a_up, g_up, k_k, k_a, r_k, ln_w, ln_b):
    B, S, _ = f.shape
    H, N = RW_HEADS, RW_HEAD_DIM
    f = token_shift(f, mu)
    r, k, v, wd, ad, gd = split_cols(f, RW_SPLITS)
    w_log = -jax.nn.softplus(-(w0 + jnp.tanh(wd) @ w_up)) - 0.5
    decay = jnp.exp(-jnp.exp(w_log.astype(F32)))
    a = jax.nn.sigmoid(a0 + ad @ a_up)
    g = jax.nn.sigmoid(gd) @ g_up
    heads = lambda t: t.reshape(B, S, H, N)
    kk = heads(k * k_k).astype(F32)
    kk = kk / jnp.maximum(jnp.sqrt(jnp.sum(kk * kk, axis=-1, keepdims=True)), 1e-12)
    k = k * (1.0 + (a - 1.0) * k_a)
    r_h, k_h, v_h, a_h = heads(r), heads(k), heads(v), heads(a)
    xs = tuple(jnp.swapaxes(t.astype(F32), 0, 1) for t in (r_h, heads(decay), k_h, v_h, kk, a_h))

    def step(state, inp):
        r_t, w_t, k_t, v_t, kk_t, a_t = inp
        sa = jnp.einsum('bhvk,bhk->bhv', state, -kk_t)
        state = (state * w_t[:, :, None, :]
                 + sa[..., None] * (kk_t * a_t)[:, :, None, :]
                 + v_t[..., None] * k_t[:, :, None, :])
        return state, jnp.einsum('bhvk,bhk->bhv', state, r_t)

    state0 = jnp.zeros((B, H, N, N), F32)
    _, y = lax.scan(step, state0, xs)
    y = jnp.swapaxes(y, 0, 1)
    mean = jnp.mean(y, axis=-1, keepdims=True)
    var = jnp.mean(jnp.square(y - mean), axis=-1, keepdims=True)
    y = ((y - mean) * lax.rsqrt(var + RW_GN_EPS)).reshape(B, S, RW_WIDTH) * ln_w + ln_b
    bonus = jnp.sum(r_h * k_h * r_k, axis=-1, keepdims=True) * v_h
    y = y + bonus.reshape(B, S, RW_WIDTH)
    return (y * g).astype(f.dtype)

def compress(x, pe, w1, w2):
    B, S, G, Dh = x.shape
    n_chunks = S // CMP_STRIDE
    ratio = CMP_BLOCK // CMP_STRIDE
    n_cmp = n_chunks - ratio + 1
    chunks = x.reshape(B, n_chunks, CMP_STRIDE, G, Dh)
    blocks = jnp.concatenate([chunks[:, i:i + n_cmp] for i in range(ratio)], axis=2)
    blocks = blocks + pe[None, None, :, None, :]
    blocks = blocks.transpose(0, 3, 1, 2, 4).reshape(B, G, n_cmp, CMP_BLOCK * Dh)
    return jax.nn.gelu(blocks @ w1) @ w2

def nsa_group(f, pos, cmp_pe_k, cmp_w1_k, cmp_w2_k, cmp_pe_v, cmp_w1_v, cmp_w2_v):
    B, S, _ = f.shape
    G, HPG, Dh = NSA_KV_GROUPS, NSA_HPG, NSA_HEAD_DIM
    q, kc, vc, ks, vs, kw, vw, gl = split_cols(f, NSA_SPLITS)
    kv = lambda t: t.reshape(B, S, G, Dh)
    q = q.reshape(B, S, NSA_HEADS, Dh)
    to_bghsd = lambda t: t.reshape(B, S, G, HPG, Dh).transpose(0, 2, 3, 1, 4)
    q_nope = to_bghsd(q)
    q_rope = to_bghsd(partial_rope(q, pos))

    k_cmp = compress(kv(kc), cmp_pe_k, cmp_w1_k, cmp_w2_k)
    v_cmp = compress(kv(vc), cmp_pe_v, cmp_w1_v, cmp_w2_v)
    n_cmp = k_cmp.shape[2]
    cmp_start = jnp.arange(n_cmp) * CMP_STRIDE
    cmp_end = cmp_start + (CMP_BLOCK - 1)
    n_sel = S // SEL_BLOCK
    sel_start = jnp.arange(n_sel) * SEL_BLOCK
    overlap = ((cmp_start[:, None] < sel_start[None, :] + SEL_BLOCK)
               & (cmp_end[:, None] >= sel_start[None, :])).astype(F32)

    to_blocks = lambda t: t.reshape(B, n_sel, SEL_BLOCK, G, Dh).transpose(0, 3, 1, 2, 4)
    k_sel_blocks = to_blocks(partial_rope(kv(ks), pos))
    v_sel_blocks = to_blocks(kv(vs))
    pad_front = lambda t: jnp.pad(t, ((0, 0), (WINDOW, 0), (0, 0), (0, 0))).transpose(0, 2, 1, 3)
    k_win = pad_front(partial_rope(kv(kw), pos))
    v_win = pad_front(kv(vw))
    gates = jax.nn.sigmoid(gl.astype(F32)).reshape(B, S, 3, G, HPG).transpose(0, 2, 3, 4, 1)

    top_n = min(SEL_TOPK, n_sel)
    scale = Dh ** -0.5
    gather = jax.vmap(jax.vmap(lambda blk, ix: blk[ix]))

    def query_block(i):
        q0 = i * Q_BLOCK
        t = q0 + jnp.arange(Q_BLOCK)
        qn = lax.dynamic_slice_in_dim(q_nope, q0, Q_BLOCK, axis=3)
        qr = lax.dynamic_slice_in_dim(q_rope, q0, Q_BLOCK, axis=3)
        s_c = jnp.einsum('bghqd,bgnd->bghqn', qn, k_cmp) * scale
        p_c = masked_softmax(s_c, cmp_end[None, :] <= t[:, None])
        o_c = jnp.einsum('bghqn,bgnd->bghqd', p_c, v_cmp)
        imp = jnp.einsum('bghqn,nj->bgqj', p_c, overlap)
        cur = (t // SEL_BLOCK)[:, None]
        jj = jnp.arange(n_sel)[None, :]
        forced = (jj == 0) | (jj == cur) | (jj == cur - 1)
        score = jnp.where(jj <= cur, imp + FORCE_BONUS * forced, -1.0)
        _, idx = lax.top_k(score, top_n)
        k_s = gather(k_sel_blocks, idx).reshape(B, G, Q_BLOCK, top_n * SEL_BLOCK, Dh)
        v_s = gather(v_sel_blocks, idx).reshape(B, G, Q_BLOCK, top_n * SEL_BLOCK, Dh)
        pos_s = (idx[..., None] * SEL_BLOCK + jnp.arange(SEL_BLOCK)).reshape(B, G, Q_BLOCK, top_n * SEL_BLOCK)
        s_s = jnp.einsum('bghqd,bgqkd->bghqk', qr, k_s) * scale
        p_s = masked_softmax(s_s, (pos_s <= t[:, None])[:, :, None])
        o_s = jnp.einsum('bghqk,bgqkd->bghqd', p_s, v_s)
        k_w = lax.dynamic_slice_in_dim(k_win, q0, Q_BLOCK + WINDOW, axis=2)
        v_w = lax.dynamic_slice_in_dim(v_win, q0, Q_BLOCK + WINDOW, axis=2)
        pos_w = q0 - WINDOW + jnp.arange(Q_BLOCK + WINDOW)
        diff = t[:, None] - pos_w[None, :]
        mask_w = (diff >= 0) & (diff < WINDOW) & (pos_w[None, :] >= 0)
        s_w = jnp.einsum('bghqd,bgkd->bghqk', qr, k_w) * scale
        p_w = masked_softmax(s_w, mask_w)
        o_w = jnp.einsum('bghqk,bgkd->bghqd', p_w, v_w)
        g = lax.dynamic_slice_in_dim(gates, q0, Q_BLOCK, axis=4)[..., None]
        o = g[:, 0] * o_c + g[:, 1] * o_s + g[:, 2] * o_w
        return o.transpose(0, 3, 1, 2, 4).reshape(B, Q_BLOCK, NSA_WIDTH)

    out = lax.map(query_block, jnp.arange(S // Q_BLOCK))
    return out.transpose(1, 0, 2, 3).reshape(B, S, NSA_WIDTH).astype(f.dtype)

def memory_cross_attention(h, mem, w_q, w_kv, w_o):
    B, S, _ = h.shape
    M = mem.shape[1]
    q = (h @ w_q).reshape(B, S, MEM_HEADS, MEM_HEAD_DIM)
    k, v = jnp.split(mem @ w_kv, 2, axis=-1)
    k = k.reshape(B, M, MEM_HEADS, MEM_HEAD_DIM)
    v = v.reshape(B, M, MEM_HEADS, MEM_HEAD_DIM)
    s = jnp.einsum('bshd,bmhd->bhsm', q, k).astype(F32) * (MEM_HEAD_DIM ** -0.5)
    p = jax.nn.softmax(s, axis=-1)
    o = jnp.einsum('bhsm,bmhd->bshd', p, v).astype(h.dtype).reshape(B, S, MEM_WIDTH)
    return o @ w_o

def setup_inputs(seed: int = 0) -> dict:
    key = jax.random.key(seed)
    ks = iter(jax.random.split(key, 48))
    nrm = lambda shape, scale: jax.random.normal(next(ks), shape, F32) * scale
    gain = lambda n: 1.0 + nrm((n,), 0.05)
    uni = lambda shape, lo, hi: jax.random.uniform(next(ks), shape, F32, lo, hi)
    d = D_MODEL
    return {
        'x': nrm((BATCH, SEQ, d), 1.0),
        'mem': nrm((BATCH, MEM_LEN, d), 1.0),
        'ffn1_pre_g': gain(d),
        'ffn1_w_gate': nrm((d, D_FF), d ** -0.5),
        'ffn1_w_up': nrm((d, D_FF), d ** -0.5),
        'ffn1_w_down': nrm((D_FF, d), D_FF ** -0.5),
        'ffn1_post_g': gain(d),
        'mix_pre_g': gain(d),
        'w_in': nrm((d, IN_COLS), d ** -0.5),
        'rw_mu': uni((RW_COLS,), 0.0, 1.0),
        'rw_w0': uni((RW_WIDTH,), -6.0, 1.0),
        'rw_w_up': nrm((RW_DECAY_LORA, RW_WIDTH), 0.5 * RW_DECAY_LORA ** -0.5),
        'rw_a0': nrm((RW_WIDTH,), 0.1),
        'rw_a_up': nrm((RW_ICLR_LORA, RW_WIDTH), 0.5 * RW_ICLR_LORA ** -0.5),
        'rw_g_up': nrm((RW_GATE_LORA, RW_WIDTH), RW_GATE_LORA ** -0.5),
        'rw_k_k': 0.85 + nrm((RW_WIDTH,), 0.05),
        'rw_k_a': 1.0 + nrm((RW_WIDTH,), 0.05),
        'rw_r_k': nrm((RW_HEADS, RW_HEAD_DIM), 0.1),
        'rw_ln_w': gain(RW_WIDTH),
        'rw_ln_b': nrm((RW_WIDTH,), 0.01),
        'cmp_pe_k': nrm((CMP_BLOCK, NSA_HEAD_DIM), 0.02),
        'cmp_w1_k': nrm((CMP_BLOCK * NSA_HEAD_DIM, CMP_HIDDEN), (CMP_BLOCK * NSA_HEAD_DIM) ** -0.5),
        'cmp_w2_k': nrm((CMP_HIDDEN, NSA_HEAD_DIM), CMP_HIDDEN ** -0.5),
        'cmp_pe_v': nrm((CMP_BLOCK, NSA_HEAD_DIM), 0.02),
        'cmp_w1_v': nrm((CMP_BLOCK * NSA_HEAD_DIM, CMP_HIDDEN), (CMP_BLOCK * NSA_HEAD_DIM) ** -0.5),
        'cmp_w2_v': nrm((CMP_HIDDEN, NSA_HEAD_DIM), CMP_HIDDEN ** -0.5),
        'w_out': nrm((MIX_WIDTH, d), MIX_WIDTH ** -0.5),
        'mix_post_g': gain(d),
        'mem_pre_g': gain(d),
        'mem_norm_g': gain(d),
        'mem_w_q': nrm((d, MEM_WIDTH), d ** -0.5),
        'mem_w_kv': nrm((d, 2 * MEM_WIDTH), d ** -0.5),
        'mem_w_o': nrm((MEM_WIDTH, d), MEM_WIDTH ** -0.5),
        'mem_post_g': gain(d),
        'ffn2_pre_g': gain(d),
        'ffn2_w_gate': nrm((d, D_FF), d ** -0.5),
        'ffn2_w_up': nrm((d, D_FF), d ** -0.5),
        'ffn2_w_down': nrm((D_FF, d), D_FF ** -0.5),
        'ffn2_post_g': gain(d),
    }

def reference(x, mem,
              ffn1_pre_g, ffn1_w_gate, ffn1_w_up, ffn1_w_down, ffn1_post_g,
              mix_pre_g, w_in,
              rw_mu, rw_w0, rw_w_up, rw_a0, rw_a_up, rw_g_up, rw_k_k, rw_k_a, rw_r_k, rw_ln_w, rw_ln_b,
              cmp_pe_k, cmp_w1_k, cmp_w2_k, cmp_pe_v, cmp_w1_v, cmp_w2_v,
              w_out, mix_post_g,
              mem_pre_g, mem_norm_g, mem_w_q, mem_w_kv, mem_w_o, mem_post_g,
              ffn2_pre_g, ffn2_w_gate, ffn2_w_up, ffn2_w_down, ffn2_post_g):
    S = x.shape[1]
    pos = jnp.arange(S, dtype=jnp.int32)
    mem_n = rmsnorm(mem, mem_norm_g)
    h = x
    for _ in range(DEPTH):
        h = h + 0.5 * rmsnorm(swiglu(rmsnorm(h, ffn1_pre_g), ffn1_w_gate, ffn1_w_up, ffn1_w_down), ffn1_post_g)
        feats = rmsnorm(h, mix_pre_g) @ w_in
        f_rw, f_nsa = jnp.split(feats, [RW_COLS], axis=-1)
        y_rw = rwkv7_group(f_rw, rw_mu, rw_w0, rw_w_up, rw_a0, rw_a_up, rw_g_up,
                           rw_k_k, rw_k_a, rw_r_k, rw_ln_w, rw_ln_b)
        y_nsa = nsa_group(f_nsa, pos, cmp_pe_k, cmp_w1_k, cmp_w2_k,
                          cmp_pe_v, cmp_w1_v, cmp_w2_v)
        y = jnp.concatenate([y_rw, y_nsa], axis=-1) @ w_out
        h = h + rmsnorm(y, mix_post_g)
        m = memory_cross_attention(rmsnorm(h, mem_pre_g), mem_n, mem_w_q, mem_w_kv, mem_w_o)
        h = h + rmsnorm(m, mem_post_g)
        h = h + 0.5 * rmsnorm(swiglu(rmsnorm(h, ffn2_pre_g), ffn2_w_gate, ffn2_w_up, ffn2_w_down), ffn2_post_g)
    return h


_drawn_inputs = setup_inputs


def setup_inputs(seed=0):
    import zlib

    import numpy as np

    out = dict(_drawn_inputs(seed))
    spreads = {}
    factors = {'rw_w_up': 3.591,
     'rw_ln_b': 8.0,
     'cmp_pe_k': 38.197,
     'cmp_pe_v': 8.0,
     'ffn2_pre_g': 2.978,
     'ffn2_post_g': 4.273}
    for name, (base, spread) in spreads.items():
        noise = np.random.default_rng([zlib.crc32(name.encode()), seed]).standard_normal(out[name].shape)
        drawn = base * np.exp(spread * noise) if base else spread * noise
        out[name] = __import__('jax').numpy.asarray(drawn.astype(out[name].dtype))
    for name, factor in factors.items():
        out[name] = (out[name] * factor).astype(out[name].dtype)
    return out
```

```python
from contextlib import ExitStack

import numpy as np
import concourse.bass as bass
from concourse import mybir

F32 = mybir.dt.float32
F32R = mybir.dt.float32r
ALU = mybir.AluOpType
ACT = mybir.ActivationFunctionType
AX = mybir.AxisListType

P = 128
D = 2048
S = 256
TT = S // P
DK = D // P
FF = 5504
FK = FF // P
NCH = 512
EPS = 1e-6

RW_HEADS = 16
RW_W = 1024
RW_T = RW_W // P
GN_EPS = 64e-5
C = 64
NC = S // C
RW_MAIN = 3 * RW_W
LORA = 64 + 64 + 160
HD = 64

G = 4
HPG = 4
N_CMP = 15
NSA_MAIN = 1024 + 6 * 256
NSA_W = NSA_MAIN + 48
OFF_KC, OFF_VC, OFF_KS, OFF_VS, OFF_KW, OFF_VW, OFF_GL = (1024 + 256 * n for n in range(7))
ROPE_H = 8
NEG = -1e30

MH = 4
MEM_W = 512

CREDIT = 1
RING = 4
SLAB = 2 * NCH
TAIL_F = FF - 10 * NCH
TAIL_IN = LORA + 48

FFN_PAIRS = 11
PAIR = 2 * (DK // 2)
DOWN = (FK + 1) // 2

S_KV = 0
S_GU1 = S_KV + PAIR
S_DN1 = S_GU1 + FFN_PAIRS * PAIR
S_IN = S_DN1 + 4 * DOWN
S_OUT = S_IN + 6 * PAIR
S_MQ = S_OUT + 2 * PAIR
S_MO = S_MQ + PAIR // 2
S_GU2 = S_MO + 8
S_DN2 = S_GU2 + FFN_PAIRS * PAIR
S_END = S_DN2 + 4 * DOWN

COLS = {}
_at = 0
for _name, _n in (("mem", 16), ("ffn1", 16), ("mix", 16), ("mattn", 16), ("ffn2", 16), ("pe_k", 16), ("pe_v", 16),
                  ("mu", 27), ("w0", 8), ("a0", 8), ("k_k", 8), ("k_a", 8), ("r_k", 8), ("ln_w", 8), ("ln_b", 8)):
    COLS[_name] = _at
    _at += _n
NCOLS = _at

MC = {}
_at = 0
for _name, _n in (("hsel", 8 * 16), ("bones", 128), ("hselT", 8 * 128), ("neg_up1", 128), ("up2", 128),
                  ("up4", 128), ("up8", 128), ("up16", 128), ("up32", 128), ("strict", 128), ("incl", 64),
                  ("causal", 256), ("cmp_add", 2 * 15), ("cmp_mul", 2 * 15), ("cos", 16), ("sin", 16),
                  ("blk", 4), ("start", 256), ("notstart", 256)):
    MC[_name] = (_at, _n)
    _at += _n
NMC = _at


def shape_constants():
    m = np.zeros((P, NMC), np.float32)

    def put(name, a):
        at, n = MC[name]
        m[:a.shape[0], at:at + n] = a.reshape(a.shape[0], n)

    p = np.arange(P)
    half, loc = p // C, p % C
    put("hsel", (np.arange(16)[None, None, :] == 2 * np.arange(8)[None, :, None] + half[:, None, None]).astype("f"))
    put("hselT", (np.arange(16)[:, None, None] == 2 * np.arange(8)[None, :, None] + half[None, None, :]).astype("f"))
    same = half[:, None] == half[None, :]
    put("bones", same.astype("f"))
    row, col = loc[:, None], loc[None, :]

    def up(b):
        return same & (row < col) & (row // (2 * b) == col // (2 * b)) & (row // b != col // b)

    put("neg_up1", -up(1).astype("f"))
    for b in (2, 4, 8, 16, 32):
        put(f"up{b}", up(b).astype("f"))
    put("strict", (same & (row < col)).astype("f"))
    put("incl", (row <= np.arange(C)[None, :]).astype("f"))
    causal = np.zeros((P, 2 * P), np.float32)
    causal[:, P:] = np.where(np.arange(P)[None, :] <= p[:, None], 0.0, NEG)
    put("causal", causal)
    t = p[:, None, None] + P * np.arange(TT)[None, :, None]
    seen = 16 * np.arange(N_CMP)[None, None, :] + 31 <= t
    put("cmp_add", np.where(seen, 0.0, NEG).astype("f"))
    put("cmp_mul", seen.astype("f"))
    inv = (np.float32(500000.0) ** (-np.arange(ROPE_H, dtype=np.float32) * np.float32(2.0) / np.float32(16))).astype("f")
    ang = (t.astype("f") * inv[None, None, :]).astype("f")
    put("cos", np.cos(ang))
    put("sin", np.sin(ang))
    put("blk", (p[:, None] // 32 == np.arange(4)[None, :]).astype("f"))
    start = np.broadcast_to((np.arange(S) % C == 0).astype("f"), (P, S))
    put("start", start)
    put("notstart", 1 - start)
    return m


def bc(ap, shape):
    return ap.to_broadcast(list(shape))


def mixing(nc, e):
    g_ = e
    (raw, ps, ident, cols, h) = (g_[n] for n in ("raw", "ps", "ident", "cols", "h"))
    (x_hi, x_lo, mc, rkv, yN, lora, nf, shb, dif, fst, w1, w2, vblk) = (g_[n] for n in (
        "x_hi", "x_lo", "mc", "rkv", "yN", "lora", "nf", "shb", "dif", "fst", "w1", "w2", "vblk"))
    (kdup, kc2, hid, hidrep, qn, qr, kk2, vv, qnT, qrT, kT, p0, p1, pc, pcT, vbg, pT0, pT1, kcT, kcg, qrot, rt, gates,
     gg, sm) = (g_[n] for n in (
         "kdup", "kc2", "hid", "hidrep", "qn", "qr", "kk2", "vv", "qnT", "qrT", "kT", "p0", "p1", "pc", "pcT", "vbg",
         "pT0", "pT1", "kcT", "kcg", "qrot", "rt", "gates", "gg", "sm"))
    (kkT, aT, wT, gT, yR, loraw, sq8, nrm, bZ, kZ, vZ, kkZ, Am, Zm, Ym, VtZ, KtZ, BtZ, Xm, Pd, iP, Bm, kp, tmp, rt_, Vt,
     Qb, Qk, Sc, SZ, Wc, Uc, UZ, Pe, vq, Sp) = (g_[n] for n in (
         "kkT", "aT", "wT", "gT", "yR", "loraw", "sq8", "nrm", "bZ", "kZ", "vZ", "kkZ", "Am", "Zm", "Ym", "VtZ", "KtZ",
         "BtZ", "Xm", "Pd", "iP", "Bm", "kp", "tmp", "rt_", "Vt", "Qb", "Qk", "Sc", "SZ", "Wc", "Uc", "UZ", "Pe",
         "vq", "Sp"))
    (sig, col, msk, split_hi, split_lo, slab_products, chunk_products, used, square_y, copy_y) = (g_[n] for n in (
        "sig", "col", "msk", "split_hi", "split_lo", "slab_products", "chunk_products", "used", "square_y", "copy_y"))
    (feat_rows, feat_turned, feat_T, shifted, mc_in, w1_in, loraw_in, y_copied, y_squared, h_ready, slab_used,
     y_hi_ready, y_lo_ready, Y_BASE, y_b) = (g_[n] for n in (
         "feat_rows", "feat_turned", "feat_T", "shifted", "mc_in", "w1_in", "loraw_in", "y_copied", "y_squared",
         "h_ready", "slab_used", "y_hi_ready", "y_lo_ready", "Y_BASE", "y_b"))
    V, A, T = nc.vector, nc.scalar, nc.tensor
    NS0 = S_IN + 3 * PAIR
    TL0 = S_IN + 5 * PAIR
    LEVELS = (2, 4, 8, 16, 32)
    DECAY = -float(np.exp(-0.5))
    cmp_add = msk("cmp_add").rearrange("p (t n) -> p t n", t=TT)
    cmp_mul = msk("cmp_mul").rearrange("p (t n) -> p t n", t=TT)
    cos = msk("cos").rearrange("p (t n) -> p t n", t=TT)
    sin = msk("sin").rearrange("p (t n) -> p t n", t=TT)

    def bank(n, w):
        return ps[:, n, :].rearrange("p (b w) -> p b w", w=w)

    def banks(n, m, w):
        return ps[:, n:n + m, :].rearrange("p a (b w) -> p (a b) w", w=w)

    def settle():
        V.drain()

    def pool_fn(pool):
        pool.wait_ge(sig("loraw_cleared"), 1)
        pool.dma_start(loraw[:, 0, :], e["drams_of"]("loraw_wa")).then_inc(loraw_in, 16)
        pool.dma_start(loraw[:, 1, :], e["drams_of"]("loraw_g")[0:P, :]).then_inc(loraw_in, 16)
        pool.dma_start(loraw[0:32, 2, :], e["drams_of"]("loraw_g")[P:160, :]).then_inc(loraw_in, 16)
        pool.wait_ge(y_lo_ready, 2)

    def in_pe(pe):
        def turn(blocks):
            for m in range(blocks):
                w = P if m < 2 or blocks == 4 else 32
                for tt in range(TT):
                    t = T.transpose(ps[0:w, 4 + m // 2, (m % 2) * S + tt * P:(m % 2) * S + (tt + 1) * P],
                                    fst[:, tt, m * P:m * P + w], ident[:, :])
            t.then_inc(feat_turned, 1)

        with pe.Fori(0, 3) as i:
            for k in range(PAIR):
                if k == PAIR // 2:
                    pe.wait_ge(feat_rows, i * 2 + CREDIT)
                m = k % (PAIR // 2)
                slab_products(pe, S_IN, i, PAIR, k, x_hi, x_lo, (2 * m, 2 * m + 1), NCH, 2 * (k // 8), m == 0, m == 7)
                if k == 12:
                    pe.wait_ge(feat_rows, i * 2 + 1 + CREDIT)
                    pe.wait_ge(feat_T, i * 2 + CREDIT)
                    turn(4)
            pe.wait_ge(feat_rows, i * 2 + 2 + CREDIT)
            pe.wait_ge(feat_T, i * 2 + 1 + CREDIT)
            turn(4)
        with pe.Fori(0, 2) as i:
            for k in range(PAIR):
                if k == PAIR // 2:
                    pe.wait_ge(feat_rows, i * 2 + 6 + CREDIT)
                m = k % (PAIR // 2)
                slab_products(pe, NS0, i, PAIR, k, x_hi, x_lo, (2 * m, 2 * m + 1), NCH, 2 * (k // 8), m == 0, m == 7)
            pe.wait_ge(feat_rows, i * 2 + 7 + CREDIT)
        chunk_products(pe, TL0, None, 0, 0, NCH, 0)
        pe.wait_ge(feat_rows, 10 + CREDIT)
        chunk_products(pe, TL0, None, 0, 8, TAIL_IN, 2)
        pe.wait_ge(feat_rows, 12 + CREDIT)
        pe.wait_ge(feat_T, 6 + CREDIT)
        turn(3)

    def in_act(act):
        def rows(dst, bank0, w=NCH):
            for tt in range(TT):
                a = A.activation(dst(tt), ps[:, bank0 + tt, 0:w], ACT.Copy)
            a.then_inc(feat_rows, 1)

        def turned():
            for b in range(2):
                a = A.activation(shb[:, 2 * b:2 * b + 2, 1:S + 1], bank(4 + b, S), ACT.Copy)
            a.then_inc(feat_T, 1)

        with act.Fori(0, 3) as i:
            for k in range(PAIR):
                split_hi(act, S_IN, i, PAIR, k, SLAB)
                if k == 11:
                    used(act, S_IN, i, PAIR, 7)
                    act.wait_ge(feat_turned, i * 2 + CREDIT)
                    rows(lambda tt: fst[:, tt, :], 0)
            act.wait_ge(feat_turned, i * 2 + 1 + CREDIT)
            act.wait_ge(shifted, i * 2 + CREDIT)
            turned()
            used(act, S_IN, i, PAIR, PAIR - 1)
            rows(lambda tt: fst[:, tt, :], 2)
            act.wait_ge(feat_turned, i * 2 + 2 + CREDIT)
            act.wait_ge(shifted, i * 2 + 1 + CREDIT)
            turned()
        with act.Fori(0, 2) as i:
            for k in range(PAIR):
                split_hi(act, NS0, i, PAIR, k, SLAB)
                if k == 11:
                    used(act, NS0, i, PAIR, 7)
                    rows(lambda tt: nf[:, tt, bass.ds(i * (2 * NCH), NCH)], 0)
            used(act, NS0, i, PAIR, PAIR - 1)
            rows(lambda tt: nf[:, tt, bass.ds(i * (2 * NCH) + NCH, NCH)], 2)
        for k in range(PAIR):
            split_hi(act, TL0, None, 0, k, SLAB if k < 8 else 2 * TAIL_IN)
            if k == 11:
                used(act, TL0, None, 0, 7)
                rows(lambda tt: nf[:, tt, 4 * NCH:5 * NCH], 0)
        used(act, TL0, None, 0, PAIR - 1)
        for tt in range(TT):
            A.activation(fst[:, tt, 0:LORA], ps[:, 2 + tt, 0:LORA], ACT.Copy)
            a = A.activation(nf[:, tt, OFF_GL:OFF_GL + 48], ps[:, 2 + tt, LORA:TAIL_IN], ACT.Copy)
        a.then_inc(feat_rows, 1)
        act.wait_ge(feat_turned, 7 + CREDIT)
        act.wait_ge(shifted, 6 + CREDIT)
        A.activation(shb[:, 0:2, 1:S + 1], bank(4, S), ACT.Copy)
        A.activation(shb[0:32, 2, 1:S + 1], ps[0:32, 5, 0:S], ACT.Copy).then_inc(feat_T, 1)

    def in_dve(dve):
        dve.wait_ge(mc_in, 16)
        V.memset(shb[:, :, 0:1], 0.0)
        V.memset(lora[:, 2, :], 0.0)
        settle()

        def shift(dst, mu0, q, n):
            V.tensor_tensor(dif[0:q, 0:n, :], shb[0:q, 0:n, 0:S], shb[0:q, 0:n, 1:S + 1], ALU.subtract)
            settle()
            mu = cols[0:q, bass.ds(mu0, n)].unsqueeze(2)
            V.tensor_tensor(dif[0:q, 0:n, :], dif[0:q, 0:n, :], bc(mu, [q, n, S]), ALU.mult)
            settle()
            return V.tensor_tensor(dst, dif[0:q, 0:n, :], shb[0:q, 0:n, 1:S + 1], ALU.add)

        MU = COLS["mu"]
        with dve.Fori(0, 3) as i:
            for k in range(PAIR):
                split_lo(dve, S_IN, i, PAIR, k, SLAB)
            for c in range(2):
                dve.wait_ge(feat_T, i * 2 + c + 1 + CREDIT)
                shift(rkv[:, bass.ds(i * 8 + 4 * c, 4), :], i * 8 + (MU + 4 * c), P, 4).then_inc(shifted, 1)
        with dve.Fori(0, 2) as i:
            for k in range(PAIR):
                split_lo(dve, NS0, i, PAIR, k, SLAB)
        for k in range(PAIR):
            split_lo(dve, TL0, None, 0, k, SLAB if k < 8 else 2 * TAIL_IN)
        dve.wait_ge(feat_T, 7 + CREDIT)
        shift(lora[:, 0:2, :], MU + 24, P, 2)
        settle()
        V.tensor_tensor(dif[0:32, 0, :], shb[0:32, 2, 0:S], shb[0:32, 2, 1:S + 1], ALU.subtract)
        settle()
        V.scalar_tensor_tensor(out=lora[0:32, 2, :], in0=dif[0:32, 0, :], scalar=cols[0:32, MU + 26:MU + 27],
                               in1=shb[0:32, 2, 1:S + 1], op0=ALU.mult, op1=ALU.add).then_inc(shifted, 1)

    KV = ("k", "v")

    def nsa_pre_pe(pe):
        for n, kv in enumerate(KV):
            pe.wait_ge(sig("c_dup"), n + 1)
            if n:
                pe.wait_ge(sig("c_T"), n)
            for g in range(G):
                for tt in range(TT):
                    t = T.transpose(ps[:, g // 2, (g % 2) * S + tt * P:(g % 2) * S + (tt + 1) * P],
                                    kdup[:, tt, g].rearrange("p a d -> p (a d)"), ident[:, :])
            t.then_inc(sig("c_turned"), 1)
        pe.wait_ge(w1_in, 80)
        for n, kv in enumerate(KV):
            pe.wait_ge(sig("c_T"), n + 1)
            for j in range(16):
                T.matmul(ps[:, 2 + n, 0:1], w1[:, n, j, :], col("pe_" + kv, j), start=j == 0, stop=j == 15)
            for j in range(16):
                m = T.matmul(ps[:, 4 + n, 0:G * N_CMP], w1[:, n, j, :], kc2[:, n, :, 2 * j:2 * j + 16 * 14 + 1:16],
                             start=j == 0, stop=j == 15)
            m.then_inc(sig("c_hidden"), 1)
        pe.wait_ge(sig("c_gelu"), 1)
        T.matmul(ps[:, 6, 0:G * N_CMP], w2[:, 0:2, :].rearrange("p a d -> p (a d)"), hid[:, 3, 0:G * N_CMP],
                 start=True, stop=True).then_inc(sig("kc_done"), 1)
        pe.wait_ge(sig("c_gelu"), 2)
        for g in range(G):
            m = T.matmul(ps[:, 7, g * HD:(g + 1) * HD], hidrep[:, g].rearrange("p a n -> p (a n)"), w2[:, 2, :],
                         start=True, stop=True)
        m.then_inc(sig("vc_done"), 1)

    def nsa_pre_act(act):
        for n in range(2):
            act.wait_ge(sig("c_turned"), n + 1)
            v = banks(0, 2, S)
            A.activation(kc2[0:HD, n, :, :], v[0:HD], ACT.Copy)
            A.activation(kc2[HD:P, n, :, 0:S - 1], v[HD:P, :, 1:S], ACT.Copy).then_inc(sig("c_T"), 1)
        for n in range(2):
            act.wait_ge(sig("c_hidden"), n + 1)
            if n:
                act.wait_ge(sig("c_gelu"), n)
            A.activation(hid[:, 4, 0:1], ps[:, 2 + n, 0:1], ACT.Copy)
            A.drain()
            A.activation(hid[:, 0, 0:G * N_CMP], ps[:, 4 + n, 0:G * N_CMP], ACT.Identity,
                         bias=hid[:, 4, 0:1]).then_inc(sig("c_x"), 1)
            act.wait_ge(sig("c_inner"), n + 1)
            A.activation(hid[:, 2, 0:G * N_CMP], hid[:, 1, 0:G * N_CMP], ACT.Tanh,
                         scale=0.7978845608028654).then_inc(sig("c_tanh"), 1)
        act.wait_ge(sig("kc_done"), 1)
        A.activation(kcT[:, :, 0:N_CMP], ps[:, 6, 0:G * N_CMP].rearrange("p (g n) -> p g n", g=G),
                     ACT.Copy).then_inc(sig("kcT_ready"), 1)
        act.wait_ge(sig("vc_done"), 1)
        A.activation(gates[:, :, :], nf[:, :, OFF_GL:OFF_GL + 48], ACT.Sigmoid).then_inc(sig("gates_ready"), 1)

    def nsa_pre_dve(dve):
        dve.wait_ge(feat_rows, 12 + CREDIT)
        W = G * N_CMP
        for n, off in enumerate((OFF_KC, OFF_VC)):
            if n:
                dve.wait_ge(sig("c_turned"), n)
            for tt in range(TT):
                src = nf[:, tt, off:off + G * HD].rearrange("p (g d) -> p g d", g=G).unsqueeze(2)
                v = V.tensor_copy(kdup[:, tt], bc(src, [P, G, 2, HD]))
            v.then_inc(sig("c_dup"), 1)
        V.memset(hidrep[:, :, :, :], 0.0)
        for n in range(2):
            dve.wait_ge(sig("c_x"), n + 1)
            x, t, y = hid[:, 0, 0:W], hid[:, 1, 0:W], hid[:, 3, 0:W]
            V.tensor_tensor(t, x, x, ALU.mult)
            settle()
            V.tensor_tensor(t, t, x, ALU.mult)
            settle()
            V.scalar_tensor_tensor(out=t, in0=t, scalar=0.044715, in1=x, op0=ALU.mult,
                                   op1=ALU.add).then_inc(sig("c_inner"), 1)
            dve.wait_ge(sig("c_tanh"), n + 1)
            if n:
                dve.wait_ge(sig("kc_done"), 1)
            V.scalar_tensor_tensor(out=y, in0=hid[:, 2, 0:W], scalar=1.0, in1=x, op0=ALU.add, op1=ALU.mult)
            settle()
            if n == 0:
                V.tensor_scalar(y, y, 0.5, None, ALU.mult).then_inc(sig("c_gelu"), 1)
            else:
                V.tensor_scalar(y, y, 0.5, None, ALU.mult)
                settle()
                V.tensor_copy(hidrep[:, :, :, 0:N_CMP],
                              bc(y.rearrange("p (g n) -> p g n", g=G).unsqueeze(2), [P, G, 4, N_CMP])
                              ).then_inc(sig("c_gelu"), 1)
        dve.wait_ge(sig("vc_done"), 1)
        V.tensor_tensor(vblk[:, :, :, :],
                        bc(ps[:, 7, 0:G * HD].rearrange("p (g d) -> p g d", g=G).unsqueeze(2), [P, G, 4, HD]),
                        bc(msk("blk").unsqueeze(1).unsqueeze(3), [P, G, 4, HD]), ALU.mult)
        for tt in range(TT):
            for kind in ("q", "k"):
                if kind == "q":
                    heads = nf[:, tt, 0:1024].rearrange("p (h d) -> p h d", d=HD)
                    x1, x2, n = heads[:, :, 0:ROPE_H], heads[:, :, ROPE_H:2 * ROPE_H], 16
                    o1, o2 = qrot[:, tt, :, 0:ROPE_H], qrot[:, tt, :, ROPE_H:2 * ROPE_H]
                    shp = [P, 16, ROPE_H]
                    tb = [rt[:, m, 0:16, :] for m in range(4)]
                    cs, sn = (bc(a[:, tt].unsqueeze(1), shp) for a in (cos, sin))
                    views = [(x1, x2, o1, o2, tb)]
                else:
                    views = []
                    for off in (OFF_KS, OFF_KW):
                        heads = nf[:, tt, off:off + 256].rearrange("p (h d) -> p h d", d=HD)
                        x1, x2 = heads[:, :, 0:ROPE_H], heads[:, :, ROPE_H:2 * ROPE_H]
                        views.append((x1, x2, x1, x2, [rt[:, m, 0:4, :] for m in range(4)]))
                    cs, sn = (bc(a[:, tt].unsqueeze(1), [P, 4, ROPE_H]) for a in (cos, sin))
                for x1, x2, o1, o2, tb in views:
                    settle()
                    V.tensor_tensor(tb[0], x1, cs, ALU.mult)
                    V.tensor_tensor(tb[1], x2, sn, ALU.mult)
                    V.tensor_tensor(tb[2], x2, cs, ALU.mult)
                    V.tensor_tensor(tb[3], x1, sn, ALU.mult)
                    settle()
                    V.tensor_tensor(o1, tb[0], tb[1], ALU.subtract)
                    V.tensor_tensor(o2, tb[2], tb[3], ALU.add)
        settle()
        V.memset(pc[:, :, :, :], 0.0)
        settle()
        dve.wait_ge(sig("gates_ready"), 1)
        dve.wait_ge(sig("kcT_ready"), 1)

    def nsa_pe(pe):
        with pe.Fori(0, G) as i:
            pe.wait_ge(sig("g_rows"), i + 1)
            pe.wait_ge(sig("g_o_out"), i + CREDIT)
            for src, b in ((qn, 0), (qr, 1)):
                for j in range(2):
                    for tt in range(TT):
                        T.transpose(ps[:, b, j * S + tt * P:j * S + (tt + 1) * P],
                                    src[:, tt, 2 * j:2 * j + 2, :].rearrange("p a d -> p (a d)"), ident[:, :])
            for b in range(2):
                for tt in range(TT):
                    t = T.transpose(ps[:, 2, b * S + tt * P:b * S + (tt + 1) * P],
                                    kk2[:, b, tt].rearrange("p a d -> p (a d)"), ident[:, :])
            t.then_inc(sig("g_turned"), 1)
            pe.wait_ge(sig("g_T"), i + 1)
            for p in range(2):
                r = slice(64 * p, 64 * p + 64)
                for tt in range(TT):
                    for j in range(2):
                        c0 = (2 * tt + j) * 16
                        T.matmul(ps[:, p, c0:c0 + N_CMP], qnT[r, j, tt * P:(tt + 1) * P], kcg[r, 0:N_CMP],
                                 start=True, stop=True)
                for b in range(2):
                    for j in range(2):
                        T.matmul(ps[:, 2 + p, (2 * b + j) * P:(2 * b + j + 1) * P], qrT[r, j, 0:P], kT[r, b, 0:P],
                                 start=True, stop=True)
                        m = T.matmul(ps[:, 4 + 2 * b + p, j * S:(j + 1) * S], qrT[r, j, P:S], kT[r, b, :],
                                     start=True, stop=True)
            m.then_inc(sig("g_scores"), 1)
            pe.wait_ge(sig("g_probs"), i + 1)
            for tt in range(TT):
                T.transpose(ps[:, 0, tt * P:(tt + 1) * P], pc[:, tt].rearrange("p a n -> p (a n)"), ident[:, :])
            for b in range(2):
                for j in range(2):
                    for p in range(2):
                        T.transpose(ps[:, 2 + 2 * b + j, p * S:p * S + P], p0[:, 4 * p + 2 * b + j, :], ident[:, :])
                        T.transpose(ps[:, 2 + 2 * b + j, p * S + P:(p + 1) * S], p1[:, 4 * b + 2 * p + j, 0:P], ident[:, :])
                        t = T.transpose(ps[:, 6 + b, (2 * j + p) * P:(2 * j + p + 1) * P], p1[:, 4 * b + 2 * p + j, P:S],
                                        ident[:, :])
            t.then_inc(sig("g_p_turned"), 1)
            pe.wait_ge(sig("g_pT_act"), i + 1)
            pe.wait_ge(sig("g_pT_dve"), i + 1)
            for j in range(2):
                T.matmul(ps[:, 1, j * S:(j + 1) * S], vbg[:, 2 * j:2 * j + 2, :].rearrange("p a d -> p (a d)"), pcT[:, :],
                         start=j == 0, stop=False, skip_group_check=True)
            for j in range(2):
                for p in range(2):
                    r = slice(64 * p, 64 * p + 64)
                    for b in range(2):
                        T.matmul(ps[r, 1, j * S:(j + 1) * S], vv[:, b, 0, :], pT0[:, b, 2 * j + p, :],
                                 start=False, stop=False, skip_group_check=True)
                        m = T.matmul(ps[r, 1, j * S + P:(j + 1) * S], vv[:, b, 1, :], pT1[:, b, 2 * j + p, :],
                                     start=False, stop=b == 1, skip_group_check=True)
            m.then_inc(sig("g_o"), 1)

    def nsa_act(act):
        with act.Fori(0, G) as i:
            act.wait_ge(sig("g_turned"), i + 1)
            A.activation(qnT[:, :, :], bank(0, S), ACT.Copy, scale=HD ** -0.5)
            A.activation(qrT[:, :, :], bank(1, S), ACT.Copy, scale=HD ** -0.5)
            A.activation(kT[:, :, :], bank(2, S), ACT.Copy).then_inc(sig("g_T"), 1)
            act.wait_ge(sig("g_max"), i + 1)
            cmp = pc[:, :, :, 0:N_CMP].rearrange("p t a n -> p (t a) n")
            A.activation(cmp, cmp, ACT.Exp)
            for n in range(8):
                A.activation(p0[:, n, :], p0[:, n, :], ACT.Exp, bias=sm[:, 1, n:n + 1], accum_out=sm[:, 2, n:n + 1])
                a = A.activation(p1[:, n, :], p1[:, n, :], ACT.Exp, bias=sm[:, 1, 8 + n:9 + n],
                                 accum_out=sm[:, 2, 8 + n:9 + n])
            a.then_inc(sig("g_exp"), 1)
            act.wait_ge(sig("g_p_turned"), i + 1)
            A.activation(pcT[:, :], ps[:, 0, 0:S], ACT.Copy)
            A.activation(pT0[:, 0], banks(2, 2, S), ACT.Copy)
            A.activation(pT1[:, 0], bank(6, P), ACT.Copy).then_inc(sig("g_pT_act"), 1)
            act.wait_ge(sig("g_o"), i + 1 + CREDIT)
            A.activation(yN[:, bass.ds(i * 2, 2), :], bank(1, S), ACT.Copy).then_inc(sig("g_o_out"), 1)

    def nsa_dve(dve):
        causal = msk("causal")
        with dve.Fori(0, G) as i:
            dve.wait_ge(sig("g_o"), i + CREDIT)
            q = nf[:, :, bass.ds(i * 256, 256)].rearrange("p t (a d) -> p t a d", a=4)
            V.tensor_copy(qn[:, :, :, :], q)
            V.tensor_copy(qr[:, :, :, :], q)
            for b, off in enumerate((OFF_KS, OFF_KW)):
                for tt in range(TT):
                    V.tensor_copy(kk2[:, b, tt], bc(nf[:, tt, bass.ds(i * HD + off, HD)].unsqueeze(1), [P, 2, HD]))
            for b, off in enumerate((OFF_VS, OFF_VW)):
                V.tensor_copy(vv[:, b], nf[:, :, bass.ds(i * HD + off, HD)])
            for tt in range(TT):
                V.tensor_copy(gg[:, tt], gates[:, tt, :].rearrange("p (b h) -> p b h", b=3)[:, :, bass.ds(i * 4, 4)])
            V.tensor_copy(kcg[:, 0:N_CMP], kcT[:, bass.ds(i, 1), 0:N_CMP].rearrange("p a n -> p (a n)"))
            V.tensor_copy(vbg[:, :, :], vblk[:, bass.ds(i, 1)].rearrange("p a b d -> p (a b) d"))
            settle()
            V.tensor_copy(qr[:, :, :, 0:2 * ROPE_H], qrot[:, :, bass.ds(i * 4, 4), :]).then_inc(sig("g_rows"), 1)
            dve.wait_ge(sig("g_scores"), i + 1)
            for p in range(2):
                s = ps[:, p, 0:64].rearrange("p (t j n) -> p t j n", t=TT, j=2)[:, :, :, 0:N_CMP]
                V.tensor_tensor(pc[:, :, :, :].rearrange("q t (j p) n -> q t j p n", p=2)[:, :, :, p, 0:N_CMP], s,
                                bc(cmp_add.unsqueeze(2), [P, TT, 2, N_CMP]), ALU.add)
                V.tensor_tensor(p0[:, 4 * p:4 * p + 4, :], bank(2 + p, P), bc(causal[:, P:2 * P].unsqueeze(1), [P, 4, P]),
                                ALU.add)
                for b in range(2):
                    n = 4 * b + 2 * p
                    V.tensor_tensor(p1[:, n:n + 2, :], bank(4 + 2 * b + p, S), bc(causal.unsqueeze(1), [P, 2, S]), ALU.add)
            settle()
            cmp = pc[:, :, :, 0:N_CMP].rearrange("p t a n -> p (t a) n")
            V.tensor_reduce(sm[:, 0, 0:8], cmp, AX.X, ALU.max, negate=True)
            V.tensor_reduce(sm[:, 1, 0:8], p0[:, :, :], AX.X, ALU.max, negate=True)
            V.tensor_reduce(sm[:, 1, 8:16], p1[:, :, :], AX.X, ALU.max, negate=True)
            settle()
            V.tensor_tensor(cmp, cmp, bc(sm[:, 0, 0:8].unsqueeze(2), [P, 8, N_CMP]), ALU.add).then_inc(sig("g_max"), 1)
            dve.wait_ge(sig("g_exp"), i + 1)
            V.tensor_reduce(sm[:, 3, 0:8], cmp, AX.X, ALU.add)
            V.reciprocal(sm[:, 5, :], sm[:, 2, :])
            settle()
            V.reciprocal(sm[:, 4, 0:8], sm[:, 3, 0:8])
            V.tensor_tensor(sm[:, 6, 0:8].rearrange("q (p b j) -> q p b j", p=2, b=2),
                            sm[:, 5, 0:8].rearrange("q (p b j) -> q p b j", p=2, b=2),
                            gg[:, 0, 1:3, :].rearrange("q b (j p) -> q p b j", p=2), ALU.mult)
            V.tensor_tensor(sm[:, 6, 8:16].rearrange("q (b p j) -> q b p j", p=2, b=2),
                            sm[:, 5, 8:16].rearrange("q (b p j) -> q b p j", p=2, b=2),
                            gg[:, 1, 1:3, :].rearrange("q b (j p) -> q b p j", p=2), ALU.mult)
            V.tensor_tensor(pc[:, :, :, 0:N_CMP], pc[:, :, :, 0:N_CMP], bc(cmp_mul.unsqueeze(2), [P, TT, 4, N_CMP]), ALU.mult)
            settle()
            V.tensor_tensor(sm[:, 7, 0:8].rearrange("p (t a) -> p t a", t=TT),
                            sm[:, 4, 0:8].rearrange("p (t a) -> p t a", t=TT), gg[:, :, 0, :], ALU.mult)
            V.tensor_tensor(p0[:, :, :], p0[:, :, :], bc(sm[:, 6, 0:8].unsqueeze(2), [P, 8, P]), ALU.mult)
            V.tensor_tensor(p1[:, :, :], p1[:, :, :], bc(sm[:, 6, 8:16].unsqueeze(2), [P, 8, S]), ALU.mult)
            settle()
            V.tensor_tensor(cmp, cmp, bc(sm[:, 7, 0:8].unsqueeze(2), [P, 8, N_CMP]), ALU.mult).then_inc(sig("g_probs"), 1)
            dve.wait_ge(sig("g_p_turned"), i + 1)
            V.tensor_copy(pT0[:, 1], banks(4, 2, S))
            V.tensor_copy(pT1[:, 1], bank(7, P)).then_inc(sig("g_pT_dve"), 1)
        dve.wait_ge(sig("g_o_out"), G + CREDIT)
        V.memset(loraw[:, 2, :], 0.0).then_inc(sig("loraw_cleared"), 1)

    def hsum(src, dst):
        for j in range(RW_T):
            m = T.matmul(dst, msk("hsel")[:, 16 * j:16 * j + 16], src[:, j, :], start=j == 0, stop=j == RW_T - 1)
        return m

    def hspread(src, bank0):
        for j in range(RW_T):
            m = T.matmul(ps[:, bank0 + j // 2, (j % 2) * S:(j % 2 + 1) * S], msk("hselT")[0:16, P * j:P * (j + 1)], src,
                         start=True, stop=True)
        return m

    def pre_pe(pe):
        pe.wait_ge(loraw_in, 48)
        pe.wait_ge(sig("lora_act"), 1)
        for j in range(RW_T):
            cs = slice(P * j, P * (j + 1))
            T.matmul(ps[:, j // 2, (j % 2) * S:(j % 2 + 1) * S], loraw[0:64, 0, cs], lora[0:64, 0, :], start=True, stop=True)
            m = T.matmul(ps[:, 4 + j // 2, (j % 2) * S:(j % 2 + 1) * S], loraw[64:P, 0, cs], lora[64:P, 0, :], start=True,
                         stop=True)
        m.then_inc(sig("wa_done"), 1)
        pe.wait_ge(sig("wa_out"), 1)
        for j in range(RW_T):
            cs = slice(P * j, P * (j + 1))
            acc = ps[:, j // 2, (j % 2) * S:(j % 2 + 1) * S]
            T.matmul(acc, loraw[:, 1, cs], lora[:, 1, :], start=True, stop=False)
            m = T.matmul(acc, loraw[:, 2, cs], lora[:, 2, :], start=False, stop=True)
        m.then_inc(sig("g_done"), 1)
        pe.wait_ge(sig("kk_squared"), 1)
        hsum(sq8, ps[0:16, 4, 0:S]).then_inc(sig("kk_summed"), 1)
        pe.wait_ge(sig("kk_rnorm"), 1)
        hspread(nrm[0:16, 1, :], 4).then_inc(sig("kk_spread"), 1)

    def pre_act(act):
        A.activation(lora[0:64, 0, :], lora[0:64, 0, :], ACT.Tanh)
        A.activation(lora[:, 1, :], lora[:, 1, :], ACT.Sigmoid)
        A.activation(lora[0:32, 2, :], lora[0:32, 2, :], ACT.Sigmoid).then_inc(sig("lora_act"), 1)
        act.wait_ge(sig("wa_done"), 1)
        for j in range(RW_T):
            v = ps[:, j // 2, (j % 2) * S:(j % 2 + 1) * S]
            A.activation(wT[:, j, :], v, ACT.Sigmoid, bias=col("w0", j))
        for j in range(RW_T):
            v = ps[:, 4 + j // 2, (j % 2) * S:(j % 2 + 1) * S]
            a = A.activation(aT[:, j, :], v, ACT.Sigmoid, bias=col("a0", j))
        a.then_inc(sig("wa_out"), 1)
        A.drain()
        A.activation(wT[:, :, :], wT[:, :, :], ACT.Exp, scale=DECAY).then_inc(sig("decay_ready"), 1)
        act.wait_ge(sig("g_done"), 1)
        A.activation(gT[:, :, :], banks(0, 4, S), ACT.Copy).then_inc(sig("gT_ready"), 1)
        act.wait_ge(sig("kk_clamped"), 1)
        A.activation(nrm[0:16, 2, :], nrm[0:16, 0, :], ACT.Sqrt).then_inc(sig("kk_root"), 1)

    def pre_dve(dve):
        kT8 = rkv[:, RW_T:2 * RW_T, :]
        V.tensor_tensor(kkT[:, :, :], kT8, bc(col("k_k", 0, 8).unsqueeze(2), [P, RW_T, S]), ALU.mult)
        settle()
        V.tensor_tensor(sq8[:, :, :], kkT[:, :, :], kkT[:, :, :], ALU.mult).then_inc(sig("kk_squared"), 1)
        dve.wait_ge(sig("kk_summed"), 1)
        V.tensor_scalar(nrm[0:16, 0, :], ps[0:16, 4, 0:S], 1e-24, None, ALU.max).then_inc(sig("kk_clamped"), 1)
        dve.wait_ge(sig("kk_root"), 1)
        V.reciprocal(nrm[0:16, 1, :], nrm[0:16, 2, :]).then_inc(sig("kk_rnorm"), 1)
        dve.wait_ge(sig("kk_spread"), 1)
        V.tensor_tensor(kkT[:, :, :], kkT[:, :, :], banks(4, 4, S), ALU.mult)
        for z in (bZ, kZ, vZ, kkZ):
            V.memset(z[:, :, :], 0.0)
        V.memset(SZ[:, :, :], 0.0)
        V.memset(UZ[:, :, :], 0.0)
        settle()
        dve.wait_ge(sig("decay_ready"), 1)
        dve.wait_ge(sig("gT_ready"), 1)

    HALVES = (slice(0, C), slice(C, P))
    UNITS = [(j, c) for j in range(2) for c in range(NC)]

    def blk4(ap):
        return ap.rearrange("p j (c t) -> p (j c) t", t=C)

    def rec_pe(pe):
        with pe.Fori(0, RW_T // 2) as i:
            pe.wait_ge(sig("r_prep"), i + 1)
            pe.wait_ge(sig("r_y_out"), i * NC + CREDIT)
            T.matmul(ps[:, 7, :], msk("bones"), tmp[:, :, :].rearrange("p j t -> p (j t)"), start=True,
                     stop=True).then_inc(sig("r_bonus"), 1)

            def gram(bank0, lhs, rhs, w, name):
                for u in range(8):
                    n = u * w // NCH
                    m = T.matmul(ps[:, bank0 + n, u * w - n * NCH:(u + 1) * w - n * NCH], lhs[:, u, :], rhs(u),
                                 start=True, stop=True)
                m.then_inc(sig(name), 1)

            gram(0, bZ, lambda u: kkZ[:, u, :], P, "r_AT")
            gram(2, kkZ, lambda u: bZ[:, u, :], P, "r_Ap")
            gram(6, bZ, lambda u: rt_[:, u // NC, (u % NC) * C:(u % NC + 1) * C], C, "r_Qbp")
            pe.wait_ge(sig("r_bonus_out"), i + 1)
            gram(7, kZ, lambda u: rt_[:, u // NC, (u % NC) * C:(u % NC + 1) * C], C, "r_Qkp")
            gram(4, kZ, lambda u: kkZ[:, u, :], P, "r_Bmp")

            def turn(src, n):
                if n == 0:
                    pe.wait_ge(sig("r_vZ"), i + 1)
                    pe.wait_ge(sig("r_gram_out"), i + 1)
                else:
                    pe.wait_ge(sig("r_t"), i * 3 + n)
                for u in range(8):
                    t = T.transpose(ps[:, 4 + u // 4, (u % 4) * P:(u % 4 + 1) * P], src[:, u, :], ident[:, :])
                t.then_inc(sig("r_turned"), 1)

            pe.wait_ge(sig("r_A"), i + 1)
            pe.wait_ge(sig("r_Q"), i + 1)
            for n in range(len(LEVELS)):
                for g in range(2):
                    pe.wait_ge(sig("r_x"), i * 12 + 2 * n + g + 1)
                    for u in range(4 * g, 4 * g + 4):
                        m = T.matmul(ps[:, g, (u % 4) * P:(u % 4 + 1) * P], Am[:, u, :], Xm[:, u, :], start=True, stop=True)
                    m.then_inc(sig("r_AX"), 1)
                    for u in range(4 * g, 4 * g + 4):
                        m = T.transpose(ps[:, 6 + g, (u % 4) * P:(u % 4 + 1) * P], Xm[:, u, :], ident[:, :])
                    m.then_inc(sig("r_XT"), 1)
                if 1 <= n <= 3:
                    turn((vZ, kZ, bZ)[n - 1], n - 1)
                for g in range(2):
                    pe.wait_ge(sig("r_Y"), i * 10 + 2 * n + g + 1)
                    pe.wait_ge(sig("r_Z"), i * 10 + 2 * n + g + 1)
                    for u in range(4 * g, 4 * g + 4):
                        m = T.matmul(ps[:, 2 + g, (u % 4) * P:(u % 4 + 1) * P], Zm[:, u, :], Ym[:, u, :], start=True, stop=True)
                    m.then_inc(sig("r_XY"), 1)
            pe.wait_ge(sig("r_x"), i * 12 + 12)
            pe.wait_ge(sig("r_t"), i * 3 + 3)
            for c in range(NC):
                for j in range(2):
                    u, js = j * NC + c, slice(j * C, (j + 1) * C)
                    m = T.matmul(ps[:, 6, js], Bm[:, u, :], Vt[:, u, :], start=j == 0, stop=c == 0, skip_group_check=True)
                if c:
                    pe.wait_ge(sig("r_S"), i * 3 + c)
                    for j in range(2):
                        m = T.matmul(ps[:, 6, j * C:(j + 1) * C], kkZ[:, j * NC + c, :], Sc[:, j, :], start=False, stop=True,
                                     skip_group_check=True)
                m.then_inc(sig("r_W"), 1)
                if c < NC - 1:
                    for j in range(2):
                        u, js = j * NC + c, slice(j * C, (j + 1) * C)
                        T.matmul(ps[:, 0, js], KtZ[:, u, :], Vt[:, u, :], start=j == 0, stop=False, skip_group_check=True)
                pe.wait_ge(sig("r_Wc"), i * NC + c + 1)
                for j in range(2):
                    m = T.matmul(ps[:, 7, j * C:(j + 1) * C], Xm[:, j * NC + c, :], Wc[:, j, :], start=True, stop=True)
                m.then_inc(sig("r_U"), 1)
                if c:
                    pe.wait_ge(sig("r_SZ"), i * 3 + c)
                if c >= 2:
                    pe.wait_ge(sig("r_y_out"), i * NC + c - 1 + CREDIT)
                for j in range(2):
                    u = j * NC + c
                    T.matmul(ps[:, 2 + c % 2, j * C:(j + 1) * C], VtZ[:, u, :], Qk[:, u, :], start=j == 0, stop=False,
                             skip_group_check=True)
                    if c:
                        T.matmul(ps[:, 2 + c % 2, j * C:(j + 1) * C], SZ[:, j, :], rt_[:, j, c * C:(c + 1) * C],
                                 start=False, stop=False, skip_group_check=True)
                pe.wait_ge(sig("r_Uc"), i * NC + c + 1)
                if c < NC - 1:
                    for j in range(2):
                        m = T.matmul(ps[:, 0, j * C:(j + 1) * C], BtZ[:, j * NC + c, :], Uc[:, j, :], start=False, stop=True,
                                     skip_group_check=True)
                    m.then_inc(sig("r_dS"), 1)
                pe.wait_ge(sig("r_UZ"), i * NC + c + 1)
                for j in range(2):
                    m = T.matmul(ps[:, 2 + c % 2, j * C:(j + 1) * C], UZ[:, j, :], Qb[:, j * NC + c, :], start=False,
                                 stop=True, skip_group_check=True)
                m.then_inc(sig("r_y"), 1)
        pe.wait_ge(sig("r_y_out"), RW_T // 2 * NC + CREDIT)
        hsum(yR, ps[0:16, 0, 0:S]).then_inc(sig("y_summed"), 1)
        pe.wait_ge(sig("y_mean"), 1)
        hspread(nrm[0:16, 0, :], 4).then_inc(sig("mean_spread"), 1)
        pe.wait_ge(sig("y_sq"), 1)
        hsum(sq8, ps[0:16, 1, 0:S]).then_inc(sig("sq_summed"), 1)
        pe.wait_ge(sig("y_rstd"), 1)
        hspread(nrm[0:16, 3, :], 4).then_inc(sig("rstd_spread"), 1)

    def rec_act(act):
        with act.Fori(0, RW_T // 2) as i:
            act.wait_ge(sig("r_v"), i + 1)
            for p, r in enumerate(HALVES):
                a = A.activation(vZ[r, :, p * C:(p + 1) * C], blk4(vq[r]), ACT.Copy)
            a.then_inc(sig("r_vZ"), 1)
            act.wait_ge(sig("r_Ap"), i + 1)
            A.activation(Am[:, :, :], banks(2, 2, P), ACT.Copy).then_inc(sig("r_A"), 1)
            for n in range(len(LEVELS)):
                for g in range(2):
                    act.wait_ge(sig("r_XT"), i * 10 + 2 * n + g + 1)
                    A.activation(Zm[:, 4 * g:4 * g + 4, :], bank(6 + g, P), ACT.Copy).then_inc(sig("r_Z"), 1)
                if 1 <= n <= 3:
                    act.wait_ge(sig("r_turned"), i * 3 + n)
                    if n == 1:
                        for p, r in enumerate(HALVES):
                            A.activation(Vt[r, :, :], banks(4, 2, P)[r, :, p * C:(p + 1) * C], ACT.Copy)
                    A.activation((VtZ, KtZ, BtZ)[n - 1][:, :, :], banks(4, 2, P), ACT.Copy).then_inc(sig("r_t"), 1)
            for c in range(NC):
                act.wait_ge(sig("r_Uc"), i * NC + c + 1)
                act.wait_ge(sig("r_y"), i * NC + c + CREDIT)
                for p, r in enumerate(HALVES):
                    a = A.activation(UZ[r, :, p * C:(p + 1) * C], bank(7, C)[r, 0:2, :], ACT.Copy, scale=-1.0)
                a.then_inc(sig("r_UZ"), 1)
                act.wait_ge(sig("r_y"), i * NC + c + 1 + CREDIT)
                A.activation(yR[:, bass.ds(i * 2, 2), c * C:(c + 1) * C], bank(2 + c % 2, C)[:, 0:2, :],
                             ACT.Copy).then_inc(sig("r_y_out"), 1)
        act.wait_ge(sig("y_summed"), 1)
        A.activation(nrm[0:16, 0, :], ps[0:16, 0, 0:S], ACT.Copy, scale=1.0 / HD).then_inc(sig("y_mean"), 1)
        act.wait_ge(sig("y_var"), 1)
        A.activation(nrm[0:16, 2, :], nrm[0:16, 1, :], ACT.Sqrt).then_inc(sig("gn_root"), 1)
        act.wait_ge(sig("yR_ready"), 1)
        A.activation(x_hi[:, 0:RW_T, :], yR[:, :, :], ACT.Copy).then_inc(y_hi_ready, 1)
        A.activation(x_hi[:, RW_T:DK, :], yN[:, :, :], ACT.Copy).then_inc(y_hi_ready, 1)

    def rec_dve(dve):
        masks2 = [bc(msk(f"up{b}").unsqueeze(1), [P, 4, P]) for b in LEVELS]
        eye = bc(ident[:, :].unsqueeze(1), [P, 4, P])
        with dve.Fori(0, RW_T // 2) as i:
            dve.wait_ge(sig("r_y_out"), i * NC + CREDIT)
            two = bass.ds(i * 2, 2)
            r, k, v = rkv[:, two, :], rkv[:, bass.ds(i * 2 + RW_T, 2), :], rkv[:, bass.ds(i * 2 + 2 * RW_T, 2), :]
            w, a, kk = wT[:, two, :], aT[:, two, :], kkT[:, two, :]
            V.tensor_copy(vq[:, :, :], v).then_inc(sig("r_v"), 1)
            V.tensor_tensor(tmp[:, :, :], w, bc(msk("notstart").unsqueeze(1), [P, 2, S]), ALU.mult)
            V.tensor_tensor(iP[:, :, :], w, bc(msk("start").unsqueeze(1), [P, 2, S]), ALU.mult)
            settle()
            V.tensor_tensor_scan(Pd[:, :, :].rearrange("p j t -> p (j t)"), tmp[:, :, :].rearrange("p j t -> p (j t)"),
                                 iP[:, :, :].rearrange("p j t -> p (j t)"), 0.0, ALU.mult, ALU.add)
            settle()
            V.reciprocal(iP[:, :, :], Pd[:, :, :])
            V.tensor_tensor(rt_[:, :, :], r, Pd[:, :, :], ALU.mult)
            V.tensor_copy(Pe[:, :, :], Pd[:, :, C - 1:S:C])
            ka = cols[:, bass.ds(i * 2 + COLS["k_a"], 2)].unsqueeze(2)
            V.scalar_tensor_tensor(out=tmp[:, :, :], in0=a, scalar=-1.0, in1=bc(ka, [P, 2, S]), op0=ALU.add, op1=ALU.mult)
            settle()
            V.scalar_tensor_tensor(out=kp[:, :, :], in0=tmp[:, :, :], scalar=1.0, in1=k, op0=ALU.add, op1=ALU.mult)
            settle()
            V.tensor_tensor(tmp[:, :, :], kk, a, ALU.mult)
            settle()
            for p, rr in enumerate(HALVES):
                cs = slice(p * C, (p + 1) * C)
                kkh = kkT[rr, two, :].rearrange("p j (c t) -> p j c t", t=C)
                ph = Pd[rr, :, :].rearrange("p j (c t) -> p j c t", t=C)
                zh = kkZ[rr, :, cs].rearrange("p (j c) t -> p j c t", j=2)
                V.tensor_tensor(zh[:, :, :, 1:C], kkh[:, :, :, 1:C], ph[:, :, :, 0:C - 1], ALU.mult)
                V.tensor_copy(zh[:, :, :, 0:1], kkh[:, :, :, 0:1])
                V.tensor_tensor(bZ[rr, :, cs], blk4(tmp[rr]), blk4(iP[rr]), ALU.mult)
                V.tensor_tensor(kZ[rr, :, cs], blk4(kp[rr]), blk4(iP[rr]), ALU.mult)
            settle()
            V.tensor_tensor(tmp[:, :, :], r, kp[:, :, :], ALU.mult)
            settle()
            rk = cols[:, bass.ds(i * 2 + COLS["r_k"], 2)].unsqueeze(2)
            V.tensor_tensor(tmp[:, :, :], tmp[:, :, :], bc(rk, [P, 2, S]), ALU.mult).then_inc(sig("r_prep"), 1)
            dve.wait_ge(sig("r_bonus"), i + 1)
            V.tensor_tensor(kkT[:, two, :], bank(7, S), v, ALU.mult).then_inc(sig("r_bonus_out"), 1)
            dve.wait_ge(sig("r_AT"), i + 1)
            V.tensor_tensor(Xm[:, :, :], banks(0, 2, P), bc(msk("neg_up1").unsqueeze(1), [P, 8, P]), ALU.mult)
            settle()
            for g in range(2):
                V.tensor_tensor(Xm[:, 4 * g:4 * g + 4, :], Xm[:, 4 * g:4 * g + 4, :], eye, ALU.add).then_inc(sig("r_x"), 1)
            incl = bc(msk("incl").unsqueeze(1), [P, 8, C])
            dve.wait_ge(sig("r_Qbp"), i + 1)
            V.tensor_tensor(Qb[:, :, :], bank(6, C), incl, ALU.mult)
            dve.wait_ge(sig("r_Qkp"), i + 1)
            V.tensor_tensor(Qk[:, :, :], bank(7, C), incl, ALU.mult).then_inc(sig("r_Q"), 1)
            for n in range(len(LEVELS)):
                for g in range(2):
                    dve.wait_ge(sig("r_AX"), i * 10 + 2 * n + g + 1)
                    if n == 0 and g == 0:
                        dve.wait_ge(sig("r_Ap"), i + 1)
                    V.tensor_tensor(Ym[:, 4 * g:4 * g + 4, :], bank(g, P), masks2[n], ALU.mult).then_inc(sig("r_Y"), 1)
                if n == 0:
                    dve.wait_ge(sig("r_Bmp"), i + 1)
                    V.tensor_tensor(Bm[:, :, :], banks(4, 2, P), bc(msk("strict").unsqueeze(1), [P, 8, P]),
                                    ALU.mult).then_inc(sig("r_gram_out"), 1)
                for g in range(2):
                    dve.wait_ge(sig("r_XY"), i * 10 + 2 * n + g + 1)
                    V.tensor_tensor(Xm[:, 4 * g:4 * g + 4, :], Xm[:, 4 * g:4 * g + 4, :], bank(2 + g, P),
                                    ALU.subtract).then_inc(sig("r_x"), 1)
            for c in range(NC):
                dve.wait_ge(sig("r_W"), i * NC + c + 1)
                V.tensor_copy(Wc[:, :, :], bank(6, C)[:, 0:2, :]).then_inc(sig("r_Wc"), 1)
                if 0 < c < NC - 1:
                    V.tensor_tensor(Sp[:, :, :], Sc[:, :, :], bc(Pe[:, :, c:c + 1], [P, 2, C]), ALU.mult)
                dve.wait_ge(sig("r_U"), i * NC + c + 1)
                V.tensor_scalar(Uc[:, :, :], bank(7, C)[:, 0:2, :], -1.0, None, ALU.mult).then_inc(sig("r_Uc"), 1)
                if c < NC - 1:
                    dve.wait_ge(sig("r_dS"), i * 3 + c + 1)
                    pe_ = bc(Pe[:, :, c:c + 1], [P, 2, C])
                    if c == 0:
                        V.tensor_tensor(Sc[:, :, :], bank(0, C)[:, 0:2, :], pe_, ALU.mult).then_inc(sig("r_S"), 1)
                    else:
                        for j in range(2):
                            x = V.scalar_tensor_tensor(out=Sc[:, j, :], in0=ps[:, 0, j * C:(j + 1) * C],
                                                       scalar=Pe[:, j, c:c + 1], in1=Sp[:, j, :], op0=ALU.mult, op1=ALU.add)
                        x.then_inc(sig("r_S"), 1)
                    settle()
                    dve.wait_ge(sig("r_y"), i * NC + c + 1 + CREDIT)
                    for p, rr in enumerate(HALVES):
                        x = V.tensor_copy(SZ[rr, :, p * C:(p + 1) * C], Sc[rr, :, :])
                    x.then_inc(sig("r_SZ"), 1)
        dve.wait_ge(sig("mean_spread"), 1)
        V.tensor_tensor(yR[:, :, :], yR[:, :, :], banks(4, 4, S), ALU.subtract)
        settle()
        V.tensor_tensor(sq8[:, :, :], yR[:, :, :], yR[:, :, :], ALU.mult).then_inc(sig("y_sq"), 1)
        dve.wait_ge(sig("sq_summed"), 1)
        V.tensor_scalar(nrm[0:16, 1, :], ps[0:16, 1, 0:S], 1.0 / HD, GN_EPS, ALU.mult, ALU.add).then_inc(sig("y_var"), 1)
        dve.wait_ge(sig("gn_root"), 1)
        V.reciprocal(nrm[0:16, 3, :], nrm[0:16, 2, :]).then_inc(sig("y_rstd"), 1)
        dve.wait_ge(sig("rstd_spread"), 1)
        V.tensor_tensor(yR[:, :, :], yR[:, :, :], banks(4, 4, S), ALU.mult)
        settle()
        for j in range(RW_T):
            V.tensor_scalar(yR[:, j, :], yR[:, j, :], col("ln_w", j), col("ln_b", j), ALU.mult, ALU.add)
        settle()
        V.tensor_tensor(yR[:, :, :], yR[:, :, :], kkT[:, :, :], ALU.add)
        settle()
        V.tensor_tensor(yR[:, :, :], yR[:, :, :], gT[:, :, :], ALU.mult).then_inc(sig("yR_ready"), 1)
        for n, src in enumerate((yR, yN)):
            dve.wait_ge(y_hi_ready, n + 1)
            ks = slice(n * RW_T, (n + 1) * RW_T)
            V.tensor_tensor(x_lo[:, ks, :], src[:, :, :], x_hi[:, ks, :].bitcast(F32), ALU.subtract).then_inc(y_lo_ready, 1)

    def out_pe(pe):
        b = Y_BASE["mix"]
        pe.wait_ge(y_lo_ready, 2)
        with pe.Fori(0, 2) as i:
            chunk_products(pe, S_OUT, i, PAIR, 0, NCH, 0)
            pe.wait_ge(y_copied, i * 2 + b + CREDIT)
            chunk_products(pe, S_OUT, i, PAIR, 8, NCH, 2)
            pe.wait_ge(y_copied, i * 2 + (b + 1) + CREDIT)

    def out_act(act):
        with act.Fori(0, 2) as i:
            for k in range(PAIR):
                split_hi(act, S_OUT, i, PAIR, k, SLAB)
                if k == 13:
                    square_y(act, y_b, Y_BASE["mix"], i, 0)
            square_y(act, y_b, Y_BASE["mix"], i, 1)

    def out_dve(dve):
        with dve.Fori(0, 2) as i:
            for k in range(PAIR):
                split_lo(dve, S_OUT, i, PAIR, k, SLAB)
                if k == 11:
                    used(dve, S_OUT, i, PAIR, 7)
                    copy_y(dve, y_b, i, 0)
            used(dve, S_OUT, i, PAIR, PAIR - 1)
            copy_y(dve, y_b, i, 1)
        settle()

    def pe_fn(pe):
        pe.wait_ge(mc_in, 16)
        in_pe(pe)
        nsa_pre_pe(pe)
        nsa_pe(pe)
        pre_pe(pe)
        rec_pe(pe)
        out_pe(pe)

    def act_fn(act):
        in_act(act)
        nsa_pre_act(act)
        nsa_act(act)
        pre_act(act)
        rec_act(act)
        out_act(act)

    def dve_fn(dve):
        in_dve(dve)
        nsa_pre_dve(dve)
        nsa_dve(dve)
        pre_dve(dve)
        rec_dve(dve)
        out_dve(dve)

    return {"pe": pe_fn, "act": act_fn, "dve": dve_fn, "pool": pool_fn}


def memory_attention(nc, e):
    (ps, ident, qs, mqT, mp, mpT, memKT, memV, stat, x_hi, x_lo, y_b) = (e[n] for n in (
        "ps", "ident", "qs", "mqT", "mp", "mpT", "memKT", "memV", "stat", "x_hi", "x_lo", "y_b"))
    (sig, split_hi, split_lo, slab_products, chunk_products, used, square_y, copy_y, y_copied, y_squared, Y_BASE) = (
        e[n] for n in ("sig", "split_hi", "split_lo", "slab_products", "chunk_products", "used", "square_y", "copy_y",
                       "y_copied", "y_squared", "Y_BASE"))
    V, A, T = nc.vector, nc.scalar, nc.tensor
    SCALE = float(MEM_W // MH) ** -0.5

    def banks(n, m, w):
        return ps[:, n:n + m, :].rearrange("p a (b w) -> p (a b) w", w=w)

    def pe_fn(pe):
        chunk_products(pe, S_MQ, None, 0, 0, NCH, 0)
        pe.wait_ge(sig("mq_rows"), 1)
        for a in range(MH):
            for tt in range(TT):
                t = T.transpose(ps[:, 2 + a // 2, (a % 2) * S + tt * P:(a % 2) * S + (tt + 1) * P],
                                qs[:, tt, a * P:(a + 1) * P], ident[:, :])
        t.then_inc(sig("mq_turned"), 1)
        pe.wait_ge(sig("mq_T"), 1)
        for tt in range(TT):
            for a in range(MH):
                m = T.matmul(ps[:, 4 + 2 * tt + a // 2, (a % 2) * S:(a % 2 + 1) * S], mqT[:, a, tt * P:(tt + 1) * P],
                             memKT[:, a, :], start=True, stop=True)
        m.then_inc(sig("m_scores"), 1)
        pe.wait_ge(sig("m_probs"), 1)
        for a in range(MH):
            for kb in range(2):
                for tt in range(TT):
                    t = T.transpose(ps[:, a, kb * S + tt * P:kb * S + (tt + 1) * P], mp[:, tt, a, kb * P:(kb + 1) * P],
                                    ident[:, :])
        t.then_inc(sig("m_turned"), 1)
        pe.wait_ge(sig("m_pT"), 1)
        for a in range(MH):
            for kb in range(2):
                m = T.matmul(ps[:, 4 + a // 2, (a % 2) * S:(a % 2 + 1) * S], memV[:, kb, a * P:(a + 1) * P],
                             mpT[:, a, kb, :], start=kb == 0, stop=kb == 1)
        m.then_inc(sig("m_o"), 1)
        pe.wait_ge(sig("m_o_lo"), 1)
        b = Y_BASE["mem"]
        for c in range(4):
            if c >= 2:
                pe.wait_ge(y_copied, b + c - 1 + CREDIT)
            for m in range(2):
                slab_products(pe, S_MO, None, 0, 2 * c + m, x_hi, x_lo, (2 * m, 2 * m + 1), NCH, 2 * (c % 2), m == 0, m == 1)

    def act_fn(act):
        for k in range(8):
            split_hi(act, S_MQ, None, 0, k, SLAB)
        used(act, S_MQ, None, 0, 7)
        for tt in range(TT):
            a = A.activation(qs[:, tt, :], ps[:, tt, :], ACT.Copy)
        a.then_inc(sig("mq_rows"), 1)
        act.wait_ge(sig("mq_turned"), 1)
        A.activation(mqT[:, :, :], banks(2, 2, S), ACT.Copy).then_inc(sig("mq_T"), 1)
        act.wait_ge(sig("m_max"), 1)
        for tt in range(TT):
            for n in range(MH):
                c = 34 + 4 * tt + n
                a = A.activation(mp[:, tt, n, :], ps[:, 4 + 2 * tt + n // 2, (n % 2) * S:(n % 2 + 1) * S], ACT.Exp,
                                 scale=SCALE, bias=stat[:, c:c + 1], accum_out=stat[:, c + 8:c + 9])
        a.then_inc(sig("m_exp"), 1)
        act.wait_ge(sig("m_turned"), 1)
        A.activation(mpT[:, :, :, :].rearrange("p a k t -> p (a k) t"), banks(0, 4, S), ACT.Copy).then_inc(sig("m_pT"), 1)
        act.wait_ge(sig("m_o"), 1)
        A.activation(x_hi[:, 0:MH, :], banks(4, 2, S), ACT.Copy).then_inc(sig("m_o_hi"), 1)
        for k in range(8):
            split_hi(act, S_MO, None, 0, k, SLAB)
        for c in range(4):
            square_y(act, y_b, Y_BASE["mem"], None, c)

    def dve_fn(dve):
        for k in range(8):
            split_lo(dve, S_MQ, None, 0, k, SLAB)
        dve.wait_ge(sig("m_scores"), 1)
        V.tensor_reduce(stat[:, 50:58], banks(4, 4, S), AX.X, ALU.max)
        V.drain()
        V.tensor_scalar(stat[:, 34:42], stat[:, 50:58], -SCALE, None, ALU.mult).then_inc(sig("m_max"), 1)
        dve.wait_ge(sig("m_exp"), 1)
        V.reciprocal(stat[:, 50:58], stat[:, 42:50])
        V.drain()
        v = mp[:, :, :, :].rearrange("p t a n -> p (t a) n")
        V.tensor_tensor(v, v, bc(stat[:, 50:58].unsqueeze(2), [P, 8, S]), ALU.mult).then_inc(sig("m_probs"), 1)
        dve.wait_ge(sig("m_o_hi"), 1)
        V.tensor_tensor(x_lo[:, 0:MH, :], banks(4, 2, S), x_hi[:, 0:MH, :].bitcast(F32),
                        ALU.subtract).then_inc(sig("m_o_lo"), 1)
        for k in range(8):
            split_lo(dve, S_MO, None, 0, k, SLAB)
            if k in (5, 7):
                c = (k - 5) // 2
                used(dve, S_MO, None, 0, 2 * c + 1)
                copy_y(dve, y_b, None, c)
        for c in (2, 3):
            used(dve, S_MO, None, 0, 2 * c + 1)
            for tt in range(TT):
                x = V.tensor_copy(y_b[:, tt, c * NCH:(c + 1) * NCH], ps[:, 2 * (c % 2) + tt, :])
            x.then_inc(y_copied, 1)
        V.drain()

    return {"pe": pe_fn, "act": act_fn, "dve": dve_fn}



def build(nc, A, out):
    with ExitStack() as ctx:
        base = (nc.sbuf_base + 63) // 64 * 64
        end = nc.sbuf_usable_end
        ctx.enter_context(nc.sbuf_tensor("arena", [P, (end - base - 64) // 4], F32))

        def at(name, shape, offset, dt=F32):
            size = 4 * int(np.prod(shape[1:]))
            assert base + offset + size <= end, (name, base + offset + size, end)
            return nc.alloc_sbuf_tensor_at(name, shape, dt, offset=base + offset)

        o = 0

        def keep(name, shape, dt=F32):
            nonlocal o
            t = at(name, shape, o, dt)
            o += (4 * int(np.prod(shape[1:])) + 31) // 32 * 32
            return t

        raw = keep("raw", [P, RING, SLAB])
        w_hi = keep("w_hi", [P, RING, SLAB], F32R)
        w_lo = keep("w_lo", [P, RING, SLAB], F32R)
        h = keep("h", [P, TT, D])
        memKT = keep("memKT", [P, MH, S])
        memV = keep("memV", [P, TT, MEM_W])
        ident = keep("ident", [P, P])
        cols = keep("cols", [P, NCOLS])
        stat = keep("stat", [P, 64])
        x_hi = keep("x_hi", [P, DK, S], F32R)
        x_lo = keep("x_lo", [P, DK, S], F32R)
        XT = o - 2 * 4 * DK * S
        BIG = o

        hT_hi = at("hT_hi", [P, FK, S], BIG, F32R)
        hT_lo = at("hT_lo", [P, FK, S], BIG + 44032, F32R)
        sg = at("sg", [P, TT, NCH], BIG + 88064)
        prod = at("prod", [P, TT, NCH], BIG + 92160)
        gain = at("gain", [P, D], BIG + 88064)
        y_x = at("y_x", [P, TT, D], XT)
        y_b = at("y_b", [P, TT, D], BIG)
        xn = at("xn", [P, TT, D], BIG + 46592)
        mem_sb = at("mem_sb", [P, TT, D], BIG + 62976)
        k_rows = at("k_rows", [P, TT, MEM_W], BIG)

        mc = at("mc", [P, NMC], BIG)
        R0 = BIG + 13824
        assert 4 * NMC <= 13824
        rkv = at("rkv", [P, 3 * RW_T, S], R0)
        yN = at("yN", [P, RW_T, S], R0 + 24576)
        lora = at("lora", [P, 3, S], R0 + 32768)
        F0 = R0 + 35840
        nf = at("nf", [P, TT, NSA_W], F0)
        T0 = F0 + 20864
        shb = at("shb", [P, 4, S + 1], T0)
        dif = at("dif", [P, 4, S], T0 + 4128)
        fst = at("fst", [P, TT, NCH], T0 + 8224)
        w1 = at("w1", [P, 2, 16, P], T0 + 12320)
        w2 = at("w2", [P, 3, HD], T0 + 28704)
        vblk = at("vblk", [P, G, 4, HD], XT + 28672)
        kdup = at("kdup", [P, TT, G, 2, HD], XT)
        kc2 = at("kc2", [P, 2, G, S], XT + 4096)
        hid = at("hid", [P, 5, 64], XT + 12288)
        hidrep = at("hidrep", [P, G, 4, 32], XT + 13568)
        qn = at("qn", [P, TT, 4, HD], XT)
        qr = at("qr", [P, TT, 4, HD], XT + 2048)
        kk2 = at("kk2", [P, 2, TT, 2, HD], XT + 4096)
        vv = at("vv", [P, 2, TT, HD], XT + 6144)
        qnT = at("qnT", [P, 2, S], XT + 7168)
        qrT = at("qrT", [P, 2, S], XT + 9216)
        kT = at("kT", [P, 2, S], XT + 11264)
        p0 = at("p0", [P, 8, P], XT + 13312)
        p1 = at("p1", [P, 8, S], XT + 17408)
        pc = at("pc", [P, TT, 4, 32], XT + 25600)
        pcT = at("pcT", [P, S], XT + 26624)
        vbg = at("vbg", [P, 4, HD], XT + 27648)
        pT0 = at("pT0", [P, 2, 4, S], T0)
        pT1 = at("pT1", [P, 2, 4, P], T0 + 8192)
        M0 = T0 + 12288
        kcT = at("kcT", [P, G, 16], M0 + 17664)
        kcg = at("kcg", [P, 16], M0 + 17920)
        qrot = at("qrot", [P, TT, 16, 16], M0)
        rt = at("rt", [P, 4, 16, ROPE_H], M0 + 2048)
        gates = at("gates", [P, TT, 48], M0 + 4096)
        gg = at("gg", [P, TT, 3, 4], M0 + 4480)
        sm = at("sm", [P, 8, 16], M0 + 4608)

        kkT = at("kkT", [P, RW_T, S], F0)
        aT = at("aT", [P, RW_T, S], F0 + 8192)
        wT = at("wT", [P, RW_T, S], F0 + 16384)
        gT = at("gT", [P, RW_T, S], F0 + 24576)
        yR = at("yR", [P, RW_T, S], F0 + 32768)
        L0 = F0 + 40960
        loraw = at("loraw", [P, 3, RW_W], L0)
        W0 = 4 * RING * SLAB
        Am = at("Am", [P, 8, P], W0)
        Zm = at("Zm", [P, 8, P], W0 + 4096)
        Ym = at("Ym", [P, 8, P], W0 + 8192)
        vq = at("vq", [P, 2, S], W0 + 12288)
        Sp = at("Sp", [P, 2, C], W0 + 14336)
        sq8 = at("sq8", [P, RW_T, S], XT)
        nrm = at("nrm", [16, 4, S], XT + 8192)
        bZ = at("bZ", [P, 8, P], XT)
        kZ = at("kZ", [P, 8, P], XT + 4096)
        vZ = at("vZ", [P, 8, P], XT + 8192)
        kkZ = at("kkZ", [P, 8, P], XT + 12288)
        VtZ = at("VtZ", [P, 8, P], XT + 16384)
        KtZ = at("KtZ", [P, 8, P], XT + 20480)
        BtZ = at("BtZ", [P, 8, P], XT + 24576)
        Xm = at("Xm", [P, 8, P], XT + 28672)
        Pd = at("Pd", [P, 2, S], XT + 28672)
        iP = at("iP", [P, 2, S], XT + 30720)
        Bm = at("Bm", [P, 8, P], L0)
        kp = at("kp", [P, 2, S], L0)
        tmp = at("tmp", [P, 2, S], L0 + 2048)
        rt_ = at("rt_", [P, 2, S], L0 + 4096)
        Vt = at("Vt", [P, 8, C], L0 + 6144)
        Qb = at("Qb", [P, 8, C], L0 + 8192)
        Qk = at("Qk", [P, 8, C], L0 + 10240)
        UZ = at("UZ", [P, 2, P], L0 + 12288)
        Pe = at("Pe", [P, 2, NC], L0 + 13312)
        Sc = at("Sc", [P, 2, C], R0 + 32768)
        SZ = at("SZ", [P, 2, P], R0 + 33280)
        Wc = at("Wc", [P, 2, C], R0 + 34304)
        Uc = at("Uc", [P, 2, C], R0 + 34816)

        qs = at("qs", [P, TT, MEM_W], BIG)
        mqT = at("mqT", [P, MH, S], BIG + 4096)
        mp = at("mp", [P, TT, MH, S], BIG + 8192)
        mpT = at("mpT", [P, MH, 2, S], BIG + 16384)

        ps = ctx.enter_context(nc.psum_tensor("ps", [P, 8, NCH], F32))

        def sem(name):
            return ctx.enter_context(nc.semaphore(name))

        slab_in = [sem(f"slab_in{n}") for n in range(RING)]
        hi_ready = sem("hi_ready")
        lo_ready = sem("lo_ready")
        slab_used = sem("slab_used")
        x_in, mem_in = sem("x_in"), sem("mem_in")
        ident_in, cols_in = sem("ident_in"), sem("cols_in")
        mc_in, w1_in, loraw_in, gain_in = sem("mc_in"), sem("w1_in"), sem("loraw_in"), sem("gain_in")
        out_done = sem("out_done")
        sq_ready = sem("sq_ready")
        ms_ready = sem("ms_ready")
        root_ready = sem("root_ready")
        xn_ready = sem("xn_ready")
        x_turned = sem("x_turned")
        x_hi_ready, x_lo_ready = sem("x_hi_ready"), sem("x_lo_ready")
        kv_rows = sem("kv_rows")
        k_turned = sem("k_turned")
        mem_kv_ready = sem("mem_kv_ready")
        gate_ready = sem("gate_ready")
        prod_ready = sem("prod_ready")
        prod_turned = sem("prod_turned")
        hT_hi_ready, hT_lo_ready = sem("hT_hi_ready"), sem("hT_lo_ready")
        y_squared, y_copied = sem("y_squared"), sem("y_copied")
        h_ready = sem("h_ready")
        feat_rows = sem("feat_rows")
        feat_turned = sem("feat_turned")
        feat_T = sem("feat_T")
        shifted = sem("shifted")
        y_hi_ready, y_lo_ready = sem("y_hi_ready"), sem("y_lo_ready")

        made = {}

        def sig(name):
            if name not in made:
                made[name] = sem(name)
            return made[name]

        def col(name, n=0, w=1):
            return cols[:, COLS[name] + n:COLS[name] + n + w]

        def msk(name):
            a, n = MC[name]
            return mc[:, a:a + n]

        def load_slab(sp, s0, reg, step, k, src, width):
            s = s0 + k
            shift = 0 if reg is None else reg * step
            if reg is not None or s >= RING:
                sp.wait_ge(lo_ready, shift + (s - RING + 1))
            sp.dma_start(raw[:, s % RING, 0:width], src).then_inc(slab_in[s % RING], 16)

        def split_hi(act, s0, reg, step, k, width):
            s = s0 + k
            act.wait_ge(slab_in[s % RING],
                        16 * (s // RING + 1) + (0 if reg is None else reg * (16 * step // RING)))
            if reg is not None or s >= RING:
                act.wait_ge(slab_used, (0 if reg is None else reg * step) + (s - RING + 1))
            nc.scalar.activation(w_hi[:, s % RING, 0:width], raw[:, s % RING, 0:width], ACT.Copy).then_inc(hi_ready, 1)

        def split_lo(dve, s0, reg, step, k, width):
            s = s0 + k
            dve.wait_ge(hi_ready, (0 if reg is None else reg * step) + s + 1)
            nc.vector.tensor_tensor(w_lo[:, s % RING, 0:width], raw[:, s % RING, 0:width],
                                    w_hi[:, s % RING, 0:width].bitcast(F32), ALU.subtract).then_inc(lo_ready, 1)

        def slab_products(pe, s0, reg, step, k, hi, lo, kts, width, bank, first, last):
            s = s0 + k
            pe.wait_ge(lo_ready, (0 if reg is None else reg * step) + s + 1)
            for n, kt in enumerate(kts):
                wh = w_hi[:, s % RING, n * width:(n + 1) * width]
                wl = w_lo[:, s % RING, n * width:(n + 1) * width]
                for tt in range(TT):
                    acc = ps[:, bank + tt, 0:width]
                    xh = hi[:, kt, tt * P:(tt + 1) * P]
                    begin, finish = first and n == 0, last and n == len(kts) - 1
                    nc.tensor.matmul(acc, xh, wh, start=begin, stop=False)
                    nc.tensor.matmul(acc, xh, wl, start=False, stop=False)
                    mm = nc.tensor.matmul(acc, lo[:, kt, tt * P:(tt + 1) * P], wh, start=False, stop=finish)
            mm.then_inc(slab_used, 1)

        def used(eng, s0, reg, step, k):
            eng.wait_ge(slab_used, (0 if reg is None else reg * step) + s0 + k + 1)

        def chunk_products(pe, s0, reg, step, k0, width, bank):
            for m in range(DK // 2):
                slab_products(pe, s0, reg, step, k0 + m, x_hi, x_lo, (2 * m, 2 * m + 1), width, bank,
                              m == 0, m == DK // 2 - 1)

        def norm_act(act, n, src, gname):
            for tt in range(TT):
                nc.scalar.activation(xn[:, tt, :], src[:, tt, :], ACT.Square,
                                     accum_out=stat[:, tt:tt + 1]).then_inc(sq_ready, 1)
            act.wait_ge(ms_ready, n + 1)
            nc.scalar.activation(stat[:, 4:6], stat[:, 2:4], ACT.Sqrt).then_inc(root_ready, 1)
            for b in range(DK // 2):
                act.wait_ge(x_turned, 8 * n + b + 1)
                for m in range(2):
                    kt = 2 * b + m
                    nc.scalar.activation(x_hi[:, kt, :], ps[:, 4 + b % 4, m * S:(m + 1) * S], ACT.Copy,
                                         scale=col(gname, kt)).then_inc(x_hi_ready, 1)

        def norm_dve(dve, n, src, gname):
            dve.wait_ge(sq_ready, 2 * n + 2)
            nc.vector.tensor_scalar(stat[:, 2:4], stat[:, 0:2], 1.0 / D, EPS, ALU.mult, ALU.add).then_inc(ms_ready, 1)
            dve.wait_ge(root_ready, n + 1)
            nc.vector.reciprocal(stat[:, 6:8], stat[:, 4:6])
            nc.vector.drain()
            for tt in range(TT):
                nc.vector.tensor_scalar(xn[:, tt, :], src[:, tt, :], stat[:, 6 + tt:7 + tt], None,
                                        ALU.mult).then_inc(xn_ready, 1)
            for kt in range(DK):
                dve.wait_ge(x_hi_ready, DK * n + 2 * (kt // 2) + 2)
                nc.vector.scalar_tensor_tensor(out=x_lo[:, kt, :], in0=ps[:, 4 + (kt // 2) % 4, (kt % 2) * S:(kt % 2 + 1) * S],
                                               scalar=col(gname, kt), in1=x_hi[:, kt, :].bitcast(F32),
                                               op0=ALU.mult, op1=ALU.subtract).then_inc(x_lo_ready, 1)

        def norm_pe(pe, n):
            for b in range(DK // 2):
                if b >= 4:
                    pe.wait_ge(x_lo_ready, DK * n + 2 * (b - 3))
                for m in range(2):
                    for tt in range(TT):
                        pe.wait_ge(xn_ready, TT * n + tt + 1)
                        t = nc.tensor.transpose(ps[:, 4 + b % 4, m * S + tt * P:m * S + (tt + 1) * P],
                                                xn[:, tt, (2 * b + m) * P:(2 * b + m + 1) * P], ident[:, :])
                t.then_inc(x_turned, 1)
            pe.wait_ge(x_lo_ready, DK * (n + 1))

        def square_y(act, y, base, reg, k):
            nc.scalar.drain()
            act.wait_ge(y_copied, (0 if reg is None else 2 * reg) + base + k + 1 + CREDIT)
            for tt in range(TT):
                idx = stat[:, bass.ds(16 + (0 if reg is None else 4 * reg) + 2 * k + tt, 1)]
                c0 = (0 if reg is None else reg * (2 * NCH)) + k * NCH
                a = nc.scalar.activation(ps[:, 6 + tt, :], y[:, tt, bass.ds(c0, NCH)], ACT.Square, accum_out=idx)
            a.then_inc(y_squared, 1)

        def copy_y(dve, y, reg, k):
            for tt in range(TT):
                c0 = (0 if reg is None else reg * (2 * NCH)) + k * NCH
                v = nc.vector.tensor_copy(y[:, tt, bass.ds(c0, NCH)], ps[:, 2 * (k % 2) + tt, :])
            v.then_inc(y_copied, 1)

        def post_norm_dve(dve, m, y, half):
            dve.wait_ge(y_squared, 4 * (m + 1))
            nc.vector.tensor_reduce(stat[:, 24:26], stat[:, 16:24].rearrange("p (n t) -> p t n", t=TT), AX.X, ALU.add)
            nc.vector.drain()
            nc.vector.tensor_scalar(stat[:, 26:28], stat[:, 24:26], 1.0 / D, EPS, ALU.mult, ALU.add).then_inc(y_ms, 1)
            dve.wait_ge(y_root, m + 1)
            nc.vector.reciprocal(stat[:, 30:32], stat[:, 28:30])
            nc.vector.drain()
            nc.vector.tensor_scalar(stat[:, 32:34], stat[:, 30:32], half, None, ALU.mult)
            nc.vector.drain()
            dve.wait_ge(gain_in, 16 * (m + 1))
            for tt in range(TT):
                nc.vector.scalar_tensor_tensor(out=y[:, tt, :], in0=y[:, tt, :], scalar=stat[:, 32 + tt:33 + tt],
                                               in1=gain[:, :], op0=ALU.mult, op1=ALU.mult)
                nc.vector.drain()
                nc.vector.tensor_tensor(h[:, tt, :], h[:, tt, :], y[:, tt, :], ALU.add).then_inc(h_ready, 1)
            nc.vector.drain()

        def post_norm_act(act, m):
            act.wait_ge(y_ms, m + 1)
            nc.scalar.activation(stat[:, 28:30], stat[:, 26:28], ACT.Sqrt).then_inc(y_root, 1)
            act.wait_ge(h_ready, TT * (m + 1))

        y_ms, y_root = sem("y_ms"), sem("y_root")

        def ffn_pair_pe(pe, f, s0, i, reg, width):
            b = FFN_PAIRS * f
            n = reg if reg is not None else i
            for k in range(PAIR // 2):
                if k == 0 and (reg is not None or i > 0):
                    pe.wait_ge(gate_ready, n + b)
                slab_products(pe, s0, reg, PAIR, k, x_hi, x_lo, (2 * k, 2 * k + 1), width, 0, k == 0, k == 7)
                if k == 4 and (reg is not None or i > 0):
                    turn_prod(pe, f, n, NCH // P)
            if reg is not None or i > 0:
                pe.wait_ge(prod_ready, n + b)
            for k in range(PAIR // 2):
                slab_products(pe, s0, reg, PAIR, 8 + k, x_hi, x_lo, (2 * k, 2 * k + 1), width, 2, k == 0, k == 7)

        def turn_prod(pe, f, n, blocks):
            b = FFN_PAIRS * f
            pe.wait_ge(prod_ready, n + b)
            pe.wait_ge(hT_lo_ready, n + (b - 1) + CREDIT)
            for tt in range(TT):
                for m in range(blocks):
                    t = nc.tensor.transpose(ps[:, 4 + tt, m * P:(m + 1) * P], prod[:, tt, m * P:(m + 1) * P], ident[:, :])
            t.then_inc(prod_turned, 1)

        def ffn_pair_act(act, f, s0, i, reg, width):
            n = reg if reg is not None else i
            for k in range(PAIR):
                split_hi(act, s0, reg, PAIR, k, 2 * width)
                if k == 8 and (reg is not None or i > 0):
                    hT_hi_evict(act, f, n, NCH // P)
                if k == 11:
                    gate_act(act, f, s0, i, reg, width)

        def hT_hi_evict(act, f, n, blocks):
            act.wait_ge(prod_turned, n + FFN_PAIRS * f + CREDIT)
            for tt in range(TT):
                a = nc.scalar.activation(hT_hi[:, bass.ds((n - 1) * 4, blocks), tt * P:(tt + 1) * P],
                                         ps[:, 4 + tt, 0:blocks * P].rearrange("p (m t) -> p m t", t=P), ACT.Copy)
            a.then_inc(hT_hi_ready, 1)

        def gate_act(act, f, s0, i, reg, width):
            n = reg if reg is not None else i
            used(act, s0, reg, PAIR, 7)
            if reg is not None or i > 0:
                act.wait_ge(prod_ready, n + FFN_PAIRS * f)
            for tt in range(TT):
                a = nc.scalar.activation(sg[:, tt, 0:width], ps[:, tt, 0:width], ACT.Silu)
            a.then_inc(gate_ready, 1)

        def ffn_pair_dve(dve, f, s0, i, reg, width):
            n = reg if reg is not None else i
            for k in range(PAIR):
                split_lo(dve, s0, reg, PAIR, k, 2 * width)
                if k == 3 and (reg is not None or i > 0):
                    make_prod(dve, f, s0, n, reg, -1, NCH)
                if k == 8 and (reg is not None or i > 0):
                    hT_lo_evict(dve, f, n, NCH // P)

        def make_prod(dve, f, s0, n, reg, last_slab, width):
            b = FFN_PAIRS * f
            dve.wait_ge(gate_ready, n + b)
            used(dve, s0, reg, PAIR, last_slab)
            dve.wait_ge(prod_turned, n + (b - 1) + CREDIT)
            for tt in range(TT):
                v = nc.vector.tensor_tensor(prod[:, tt, 0:width], ps[:, 2 + tt, 0:width], sg[:, tt, 0:width], ALU.mult)
            v.then_inc(prod_ready, 1)

        def hT_lo_evict(dve, f, n, blocks):
            dve.wait_ge(hT_hi_ready, n + FFN_PAIRS * f)
            for tt in range(TT):
                kt = bass.ds((n - 1) * 4, blocks)
                v = nc.vector.tensor_tensor(hT_lo[:, kt, tt * P:(tt + 1) * P],
                                            ps[:, 4 + tt, 0:blocks * P].rearrange("p (m t) -> p m t", t=P),
                                            hT_hi[:, kt, tt * P:(tt + 1) * P].bitcast(F32), ALU.subtract)
            v.then_inc(hT_lo_ready, 1)

        def pair_base(s0, i):
            return s0 + PAIR * i

        LASTP = FFN_PAIRS - 1

        def down_width(k):
            return (NCH if k % DOWN == DOWN - 1 else 2 * NCH)

        def ffn_sp(sp, s0, gu, gu_t, dn):
            for k in range(PAIR):
                load_slab(sp, s0, None, 0, k, gu[0, k], SLAB)
            with sp.Fori(1, LASTP) as i:
                for k in range(PAIR):
                    load_slab(sp, s0, i, PAIR, k, gu[bass.ds(i, 1), k].rearrange("a p w -> (a p) w"), SLAB)
            for k in range(PAIR):
                load_slab(sp, pair_base(s0, LASTP), None, 0, k, gu_t[k], 2 * TAIL_F)
            s1 = pair_base(s0, FFN_PAIRS)
            with sp.Fori(0, 2) as i:
                for k in range(2 * DOWN):
                    w = down_width(k)
                    load_slab(sp, s1, i, 2 * DOWN, k, dn[bass.ds(i, 1), k].rearrange("a p w -> (a p) w")[:, 0:w], w)

        def ffn_pe(pe, f, s0):
            ffn_pair_pe(pe, f, s0, 0, None, NCH)
            with pe.Fori(1, LASTP) as i:
                ffn_pair_pe(pe, f, s0, None, i, NCH)
            ffn_pair_pe(pe, f, pair_base(s0, LASTP), LASTP, None, TAIL_F)
            turn_prod(pe, f, FFN_PAIRS, TAIL_F // P)
            s1 = pair_base(s0, FFN_PAIRS)
            b = Y_BASE[f]
            pe.wait_ge(hT_lo_ready, FFN_PAIRS * (f + 1) + CREDIT)
            with pe.Fori(0, 2) as i:
                for c in range(2):
                    if c == 1:
                        pe.wait_ge(y_copied, i * 2 + b + CREDIT)
                    for m in range(DOWN):
                        kts = tuple(k for k in (2 * m, 2 * m + 1) if k < FK)
                        slab_products(pe, s1, i, 2 * DOWN, c * DOWN + m, hT_hi, hT_lo, kts, NCH, 2 * c,
                                      m == 0, m == DOWN - 1)
                pe.wait_ge(y_copied, i * 2 + (b + 1) + CREDIT)

        def ffn_act(act, f, s0):
            ffn_pair_act(act, f, s0, 0, None, NCH)
            with act.Fori(1, LASTP) as i:
                ffn_pair_act(act, f, s0, None, i, NCH)
            ffn_pair_act(act, f, pair_base(s0, LASTP), LASTP, None, TAIL_F)
            s1 = pair_base(s0, FFN_PAIRS)
            hT_hi_evict(act, f, FFN_PAIRS, TAIL_F // P)
            with act.Fori(0, 2) as i:
                for k in range(2 * DOWN):
                    split_hi(act, s1, i, 2 * DOWN, k, down_width(k))
                    if k == DOWN + 5:
                        square_y(act, y_x, Y_BASE[f], i, 0)
                square_y(act, y_x, Y_BASE[f], i, 1)

        def ffn_dve(dve, f, s0):
            ffn_pair_dve(dve, f, s0, 0, None, NCH)
            with dve.Fori(1, LASTP) as i:
                ffn_pair_dve(dve, f, s0, None, i, NCH)
            ffn_pair_dve(dve, f, pair_base(s0, LASTP), LASTP, None, TAIL_F)
            make_prod(dve, f, pair_base(s0, LASTP), FFN_PAIRS, None, PAIR - 1, TAIL_F)
            hT_lo_evict(dve, f, FFN_PAIRS, TAIL_F // P)
            s1 = pair_base(s0, FFN_PAIRS)
            with dve.Fori(0, 2) as i:
                for k in range(2 * DOWN):
                    split_lo(dve, s1, i, 2 * DOWN, k, down_width(k))
                    if k == DOWN + 3:
                        used(dve, s1, i, 2 * DOWN, DOWN - 1)
                        copy_y(dve, y_x, i, 0)
                used(dve, s1, i, 2 * DOWN, 2 * DOWN - 1)
                copy_y(dve, y_x, i, 1)
            nc.vector.drain()

        Y_BASE = {0: 0, "mix": 4, "mem": 8, 1: 12}

        drams_of = A.get
        env = dict(locals())
        mix = mixing(nc, env)
        mat = memory_attention(nc, env)

        block = ctx.enter_context(nc.Block())
        drams = A

        @block.sync
        def _(sp):
            sp.dma_start(mem_sb[:, :, :], drams["mem"].rearrange("a (t p) d -> p (a t) d", p=P)).then_inc(mem_in, 16)
            sp.dma_start(ident[:, :], drams["ident"]).then_inc(ident_in, 16)
            sp.dma_start(cols[:, :], drams["cols"]).then_inc(cols_in, 16)
            for k in range(PAIR):
                load_slab(sp, S_KV, None, 0, k, drams["w_kv"][k], SLAB)
            ffn_sp(sp, S_GU1, drams["gu1"], drams["gu1_t"], drams["dn1"])
            with sp.Fori(0, 5) as i:
                for k in range(PAIR):
                    load_slab(sp, S_IN, i, PAIR, k, drams["w_in"][bass.ds(i, 1), k].rearrange("a p w -> (a p) w"), SLAB)
            for k in range(PAIR // 2):
                load_slab(sp, S_IN + 5 * PAIR, None, 0, k, drams["w_in5"][k], SLAB)
            for k in range(PAIR // 2):
                load_slab(sp, S_IN + 5 * PAIR, None, 0, 8 + k, drams["w_in_t"][k], 2 * TAIL_IN)
            with sp.Fori(0, 2) as i:
                for k in range(PAIR):
                    load_slab(sp, S_OUT, i, PAIR, k, drams["w_out"][bass.ds(i, 1), k].rearrange("a p w -> (a p) w"), SLAB)
            for k in range(8):
                load_slab(sp, S_MQ, None, 0, k, drams["w_mq"][k], SLAB)
            for k in range(8):
                load_slab(sp, S_MO, None, 0, k, drams["w_mo"][k], SLAB)
            ffn_sp(sp, S_GU2, drams["gu2"], drams["gu2_t"], drams["dn2"])
            for tt in range(TT):
                sp.wait_ge(h_ready, TT * 3 + tt + 1)
                sp.dma_start(out[0, tt * P:(tt + 1) * P, :], h[:, tt, :]).then_inc(out_done, 16)
            sp.wait_ge(out_done, 16 * TT)

        @block.gpsimd
        def _(pool):
            pool.dma_start(h[:, :, :], drams["x"].rearrange("a (t p) d -> p (a t) d", p=P)).then_inc(x_in, 16)
            pool.wait_ge(hT_hi_ready, FFN_PAIRS)
            pool.wait_ge(hT_lo_ready, FFN_PAIRS + CREDIT)
            pool.dma_start(gain[:, :], drams["post1"].partition_broadcast(P)).then_inc(gain_in, 16)
            pool.wait_ge(slab_used, S_IN)
            pool.wait_ge(h_ready, TT)
            pool.dma_start(mc[:, :], drams["mc"]).then_inc(mc_in, 16)
            pool.dma_start(w1[:, 0], drams["w1_k"]).then_inc(w1_in, 16)
            pool.dma_start(w1[:, 1], drams["w1_v"]).then_inc(w1_in, 16)
            pool.dma_start(w2[:, 0, :], drams["w2_k"]).then_inc(w1_in, 16)
            pool.dma_start(w2[:, 1, :], drams["w2_k"]).then_inc(w1_in, 16)
            pool.dma_start(w2[:, 2, :], drams["w2_v"]).then_inc(w1_in, 16)
            mix["pool"](pool)
            pool.dma_start(gain[:, :], drams["post2"].partition_broadcast(P)).then_inc(gain_in, 16)
            pool.wait_ge(h_ready, 2 * TT)
            pool.dma_start(gain[:, :], drams["post3"].partition_broadcast(P)).then_inc(gain_in, 16)
            pool.wait_ge(hT_hi_ready, 2 * FFN_PAIRS)
            pool.wait_ge(hT_lo_ready, 2 * FFN_PAIRS + CREDIT)
            pool.dma_start(gain[:, :], drams["post4"].partition_broadcast(P)).then_inc(gain_in, 16)

        @block.scalar
        def _(act):
            for name in ("feat_rows", "feat_T"):
                act.sem_inc(env[name], CREDIT)
            for name in ("g_o_out", "r_y_out"):
                act.sem_inc(sig(name), CREDIT)
            act.wait_ge(mem_in, 16)
            act.wait_ge(cols_in, 16)
            norm_act(act, 0, mem_sb, "mem")
            for k in range(PAIR):
                split_hi(act, S_KV, None, 0, k, SLAB)
                if k == 11:
                    used(act, S_KV, None, 0, 7)
                    for tt in range(TT):
                        a = nc.scalar.activation(k_rows[:, tt, :], ps[:, tt, :], ACT.Copy)
                    a.then_inc(kv_rows, 1)
            used(act, S_KV, None, 0, PAIR - 1)
            for tt in range(TT):
                a = nc.scalar.activation(memV[:, tt, :], ps[:, 2 + tt, :], ACT.Copy)
            a.then_inc(kv_rows, 1)
            act.wait_ge(k_turned, 1)
            for b in range(2):
                a = nc.scalar.activation(memKT[:, 2 * b:2 * b + 2, :], ps[:, 4 + b, :].rearrange("p (m t) -> p m t", t=S), ACT.Copy)
            a.then_inc(mem_kv_ready, 1)
            act.wait_ge(x_in, 16)
            norm_act(act, 1, h, "ffn1")
            ffn_act(act, 0, S_GU1)
            post_norm_act(act, 0)
            norm_act(act, 2, h, "mix")
            mix["act"](act)
            post_norm_act(act, 1)
            norm_act(act, 3, h, "mattn")
            mat["act"](act)
            post_norm_act(act, 2)
            norm_act(act, 4, h, "ffn2")
            ffn_act(act, 1, S_GU2)
            post_norm_act(act, 3)

        @block.vector
        def _(dve):
            for name in ("hT_lo_ready", "y_copied", "shifted"):
                dve.sem_inc(env[name], CREDIT)
            dve.wait_ge(mem_in, 16)
            dve.wait_ge(cols_in, 16)
            norm_dve(dve, 0, mem_sb, "mem")
            for k in range(PAIR):
                split_lo(dve, S_KV, None, 0, k, SLAB)
            dve.wait_ge(x_in, 16)
            norm_dve(dve, 1, h, "ffn1")
            ffn_dve(dve, 0, S_GU1)
            post_norm_dve(dve, 0, y_x, 0.5)
            norm_dve(dve, 2, h, "mix")
            mix["dve"](dve)
            post_norm_dve(dve, 1, y_b, 1.0)
            norm_dve(dve, 3, h, "mattn")
            mat["dve"](dve)
            post_norm_dve(dve, 2, y_b, 1.0)
            norm_dve(dve, 4, h, "ffn2")
            ffn_dve(dve, 1, S_GU2)
            post_norm_dve(dve, 3, y_x, 0.5)

        @block.tensor
        def _(pe):
            for name in ("prod_turned", "feat_turned"):
                pe.sem_inc(env[name], CREDIT)
            for name in ("g_o", "r_y"):
                pe.sem_inc(sig(name), CREDIT)
            pe.wait_ge(ident_in, 16)
            norm_pe(pe, 0)
            for c in range(2):
                chunk_products(pe, S_KV, None, 0, 8 * c, NCH, 2 * c)
            pe.wait_ge(kv_rows, 1)
            for hh in range(MH):
                for tt in range(TT):
                    t = nc.tensor.transpose(ps[:, 4 + hh // 2, (hh % 2) * S + tt * P:(hh % 2) * S + (tt + 1) * P],
                                            k_rows[:, tt, hh * P:(hh + 1) * P], ident[:, :])
            t.then_inc(k_turned, 1)
            pe.wait_ge(kv_rows, 2)
            pe.wait_ge(mem_kv_ready, 1)
            norm_pe(pe, 1)
            ffn_pe(pe, 0, S_GU1)
            norm_pe(pe, 2)
            mix["pe"](pe)
            norm_pe(pe, 3)
            mat["pe"](pe)
            norm_pe(pe, 4)
            ffn_pe(pe, 1, S_GU2)


def weight_slabs(w, widths):
    K, N = w.shape
    out, c0 = [], 0
    for wd in widths:
        c = w[:, c0:c0 + wd]
        out.append(c.reshape(K // (2 * P), 2, P, wd).transpose(0, 2, 1, 3).reshape(K // (2 * P), P, 2 * wd))
        c0 += wd
    return out


def down_slabs(w):
    out = np.zeros((4, DOWN, P, SLAB), w.dtype)
    for c in range(4):
        x = w[:, c * NCH:(c + 1) * NCH].reshape(FK, P, NCH)
        out[c, :DOWN - 1] = x[:FK - 1].reshape(DOWN - 1, 2, P, NCH).transpose(0, 2, 1, 3).reshape(DOWN - 1, P, SLAB)
        out[c, DOWN - 1, :, :NCH] = x[FK - 1]
    return out.reshape(2, 2 * DOWN, P, SLAB)


def gate_up_slabs(wg, wu):
    widths = [NCH] * (FFN_PAIRS - 1) + [TAIL_F]
    g, u = weight_slabs(wg, widths), weight_slabs(wu, widths)
    main = np.stack([np.concatenate([a, b]) for a, b in zip(g[:-1], u[:-1])])
    return main, np.concatenate([g[-1], u[-1]])


def channel_columns(parts):
    done = []
    for v, n in parts:
        v = v.reshape(-1)
        x = np.zeros(n * P, v.dtype)
        x[:v.size] = v
        done.append(x.reshape(n, P).T)
    return np.concatenate(done, axis=1)


def kernel(**inputs):
    import concourse.bacc as bacc
    from concourse.bass_utils import run_bass_kernel_spmd

    z = {n: np.asarray(a) for n, a in inputs.items()}
    t = {"x": z["x"], "mem": z["mem"]}
    t["w_kv"] = np.concatenate(weight_slabs(z["mem_w_kv"], [NCH, NCH]))
    t["gu1"], t["gu1_t"] = gate_up_slabs(z["ffn1_w_gate"], z["ffn1_w_up"])
    t["gu2"], t["gu2_t"] = gate_up_slabs(z["ffn2_w_gate"], z["ffn2_w_up"])
    t["dn1"], t["dn2"] = down_slabs(z["ffn1_w_down"]), down_slabs(z["ffn2_w_down"])
    w_in = z["w_in"]
    nsa0 = RW_MAIN + LORA
    w_in = np.concatenate([w_in[:, :RW_MAIN], w_in[:, nsa0:nsa0 + NSA_MAIN], w_in[:, RW_MAIN:nsa0],
                           w_in[:, nsa0 + NSA_MAIN:]], axis=1)
    s = weight_slabs(w_in, [NCH] * 11 + [TAIL_IN])
    t["w_in"] = np.stack([np.concatenate(s[2 * i:2 * i + 2]) for i in range(5)])
    t["w_in5"], t["w_in_t"] = s[10], s[11]
    s = weight_slabs(z["w_out"], [NCH] * 4)
    t["w_out"] = np.stack([np.concatenate(s[2 * i:2 * i + 2]) for i in range(2)])
    t["w_mq"] = weight_slabs(z["mem_w_q"], [NCH])[0]
    t["w_mo"] = np.concatenate(weight_slabs(z["mem_w_o"], [NCH] * 4))
    t["cols"] = channel_columns([
        (z["mem_norm_g"], 16), (z["ffn1_pre_g"], 16), (z["mix_pre_g"], 16), (z["mem_pre_g"], 16), (z["ffn2_pre_g"], 16),
        (z["cmp_pe_k"], 16), (z["cmp_pe_v"], 16), (z["rw_mu"], 27), (z["rw_w0"], 8), (z["rw_a0"], 8), (z["rw_k_k"], 8),
        (z["rw_k_a"], 8), (z["rw_r_k"], 8), (z["rw_ln_w"], 8), (z["rw_ln_b"], 8)])
    t["ident"] = np.eye(P, dtype=np.float32)
    t["mc"] = shape_constants()
    for a in "kv":
        t["w1_" + a] = np.ascontiguousarray(z["cmp_w1_" + a].reshape(16, P, P).transpose(1, 0, 2))
        t["w2_" + a] = z["cmp_w2_" + a]
    t["loraw_wa"] = np.concatenate([z["rw_w_up"], z["rw_a_up"]])
    t["loraw_g"] = z["rw_g_up"]
    for n, a in enumerate(("ffn1_post_g", "mix_post_g", "mem_post_g", "ffn2_post_g")):
        t[f"post{n + 1}"] = z[a]

    nc = bacc.Bacc("TRN2", target_bir_lowering=False, num_devices=1)
    arrays, drams = {}, {}
    for name, a in t.items():
        a = np.ascontiguousarray(a)
        arrays[f"in_{name}_dram"] = a
        drams[name] = nc.dram_tensor(f"in_{name}_dram", a.shape, mybir.dt.from_np(a.dtype), kind="ExternalInput").ap()
    out = nc.dram_tensor("out_0_dram", (1, S, D), F32, kind="ExternalOutput").ap()
    build(nc, drams, out)
    r = run_bass_kernel_spmd(nc, [arrays], core_ids=[0])
    return r.results[0]["out_0_dram"]
```

```python
from contextlib import ExitStack

import numpy as np
import concourse.bass as bass
from concourse import mybir

F32 = mybir.dt.float32
F32R = mybir.dt.float32r
ALU = mybir.AluOpType
ACT = mybir.ActivationFunctionType
AX = mybir.AxisListType

P = 128
D = 2048
S = 256
TT = S // P
DK = D // P
FF = 5504
FK = FF // P
NCH = 512
EPS = 1e-6

RW_HEADS = 16
RW_W = 1024
RW_T = RW_W // P
GN_EPS = 64e-5
C = 64
NC = S // C
RW_MAIN = 3 * RW_W
LORA = 64 + 64 + 160
HD = 64

G = 4
HPG = 4
N_CMP = 15
NSA_MAIN = 1024 + 6 * 256
NSA_W = NSA_MAIN + 48
OFF_KC, OFF_VC, OFF_KS, OFF_VS, OFF_KW, OFF_VW, OFF_GL = (1024 + 256 * n for n in range(7))
ROPE_H = 8
NEG = -1e30

MH = 4
MEM_W = 512

CREDIT = 1
RING = 4
SLAB = 2 * NCH
TAIL_F = FF - 10 * NCH
TAIL_IN = LORA + 48

FFN_PAIRS = 11
PAIR = 2 * (DK // 2)
DOWN = (FK + 1) // 2

S_KV = 0
S_GU1 = S_KV + PAIR
S_DN1 = S_GU1 + FFN_PAIRS * PAIR
S_IN = S_DN1 + 4 * DOWN
S_OUT = S_IN + 6 * PAIR
S_MQ = S_OUT + 2 * PAIR
S_MO = S_MQ + PAIR // 2
S_GU2 = S_MO + 8
S_DN2 = S_GU2 + FFN_PAIRS * PAIR
S_END = S_DN2 + 4 * DOWN

COLS = {}
_at = 0
for _name, _n in (("mem", 16), ("ffn1", 16), ("mix", 16), ("mattn", 16), ("ffn2", 16), ("pe_k", 16), ("pe_v", 16),
                  ("mu", 27), ("w0", 8), ("a0", 8), ("k_k", 8), ("k_a", 8), ("r_k", 8), ("ln_w", 8), ("ln_b", 8)):
    COLS[_name] = _at
    _at += _n
NCOLS = _at

MC = {}
_at = 0
for _name, _n in (("hsel", 8 * 16), ("bones", 128), ("hselT", 8 * 128), ("neg_up1", 128), ("up2", 64),
                  ("up4", 64), ("up8", 64), ("up16", 64), ("up32", 64), ("strict", 128), ("incl", 64),
                  ("causal", 256), ("cmp_add", 2 * 15), ("cmp_mul", 2 * 15), ("cos", 16), ("sin", 16),
                  ("blk", 4), ("start", 256), ("notstart", 256)):
    MC[_name] = (_at, _n)
    _at += _n
NMC = _at


def shape_constants():
    m = np.zeros((P, NMC), np.float32)

    def put(name, a):
        at, n = MC[name]
        m[:a.shape[0], at:at + n] = a.reshape(a.shape[0], n)

    p = np.arange(P)
    half, loc = p // C, p % C
    put("hsel", (np.arange(16)[None, None, :] == 2 * np.arange(8)[None, :, None] + half[:, None, None]).astype("f"))
    put("hselT", (np.arange(16)[:, None, None] == 2 * np.arange(8)[None, :, None] + half[None, None, :]).astype("f"))
    same = half[:, None] == half[None, :]
    put("bones", same.astype("f"))
    row, col = loc[:, None], loc[None, :]

    def up(b):
        return same & (row < col) & (row // (2 * b) == col // (2 * b)) & (row // b != col // b)

    put("neg_up1", -up(1).astype("f"))
    for b in (2, 4, 8, 16, 32):
        put(f"up{b}", up(b)[:, p // b % 2 == 1].astype("f"))
    put("strict", (same & (row < col)).astype("f"))
    put("incl", (row <= np.arange(C)[None, :]).astype("f"))
    causal = np.zeros((P, 2 * P), np.float32)
    causal[:, P:] = np.where(np.arange(P)[None, :] <= p[:, None], 0.0, NEG)
    put("causal", causal)
    t = p[:, None, None] + P * np.arange(TT)[None, :, None]
    seen = 16 * np.arange(N_CMP)[None, None, :] + 31 <= t
    put("cmp_add", np.where(seen, 0.0, NEG).astype("f"))
    put("cmp_mul", seen.astype("f"))
    inv = (np.float32(500000.0) ** (-np.arange(ROPE_H, dtype=np.float32) * np.float32(2.0) / np.float32(16))).astype("f")
    ang = (t.astype("f") * inv[None, None, :]).astype("f")
    put("cos", np.cos(ang))
    put("sin", np.sin(ang))
    put("blk", (p[:, None] // 32 == np.arange(4)[None, :]).astype("f"))
    start = np.broadcast_to((np.arange(S) % C == 0).astype("f"), (P, S))
    put("start", start)
    put("notstart", 1 - start)
    return m


def bc(ap, shape):
    return ap.to_broadcast(list(shape))


def mixing(nc, e):
    g_ = e
    (raw, ps, ident, cols, h) = (g_[n] for n in ("raw", "ps", "ident", "cols", "h"))
    (x_hi, x_lo, mc, rkv, yN, lora, nf, shb, dif, fst, w1, w2, vblk) = (g_[n] for n in (
        "x_hi", "x_lo", "mc", "rkv", "yN", "lora", "nf", "shb", "dif", "fst", "w1", "w2", "vblk"))
    (kdup, kc2, hid, hb, hidrep, qn, qr, kk2, vv, qnT, qrT, kT, p0, p1, pc, pcT, vbg, pT0, pT1, kcT, kcg, qrot, rt, gates,
     gg, sm, smc) = (g_[n] for n in (
         "kdup", "kc2", "hid", "hb", "hidrep", "qn", "qr", "kk2", "vv", "qnT", "qrT", "kT", "p0", "p1", "pc", "pcT", "vbg",
         "pT0", "pT1", "kcT", "kcg", "qrot", "rt", "gates", "gg", "sm", "smc"))
    (kkT, aT, wT, yR, wa_up, g_up, sq8, nrm, bZ, kZ, vZ, kkZ, Am, Zm, Ym, VtZ, KtZ, BtZ, Xm, Pd, iP, Bm, kp, tmp, rt_, Vt,
     Qb, Qk, Sc, SZ, Wc, Uc, UZ, Pe, vq, Sp, rtn, kkd, bon, Pn) = (g_[n] for n in (
         "kkT", "aT", "wT", "yR", "wa_up", "g_up", "sq8", "nrm", "bZ", "kZ", "vZ", "kkZ", "Am", "Zm", "Ym", "VtZ", "KtZ",
         "BtZ", "Xm", "Pd", "iP", "Bm", "kp", "tmp", "rt_", "Vt", "Qb", "Qk", "Sc", "SZ", "Wc", "Uc", "UZ", "Pe",
         "vq", "Sp", "rtn", "kkd", "bon", "Pn"))
    root_tables, AHEAD = g_["root_tables"], g_["AHEAD"]
    (sig, col, msk, split_hi, split_lo, slab_products, chunk_products, used, square_y, copy_y) = (g_[n] for n in (
        "sig", "col", "msk", "split_hi", "split_lo", "slab_products", "chunk_products", "used", "square_y", "copy_y"))
    (feat_rows, feat_turned, feat_T, shifted, mc_in, w1_in, loraw_in, y_copied, y_squared, h_ready, slab_used,
     y_hi_ready, y_lo_ready, Y_BASE, y_b) = (g_[n] for n in (
         "feat_rows", "feat_turned", "feat_T", "shifted", "mc_in", "w1_in", "loraw_in", "y_copied", "y_squared",
         "h_ready", "slab_used", "y_hi_ready", "y_lo_ready", "Y_BASE", "y_b"))
    V, A, T = nc.vector, nc.scalar, nc.tensor
    NS0 = S_IN + 3 * PAIR
    TL0 = S_IN + 5 * PAIR
    LEVELS = (2, 4, 8, 16, 32)
    DECAY = -float(np.exp(-0.5))
    cmp_add = msk("cmp_add").rearrange("p (t n) -> p t n", t=TT)
    cmp_mul = msk("cmp_mul").rearrange("p (t n) -> p t n", t=TT)
    cos = msk("cos").rearrange("p (t n) -> p t n", t=TT)
    sin = msk("sin").rearrange("p (t n) -> p t n", t=TT)

    def bank(n, w):
        return ps[:, n, :].rearrange("p (b w) -> p b w", w=w)

    def banks(n, m, w):
        return ps[:, n:n + m, :].rearrange("p a (b w) -> p (a b) w", w=w)

    def settle():
        V.drain()

    def pool_fn(pool):
        G_ = nc.gpsimd
        pool.dma_start(wa_up[:, :], e["drams_of"]("loraw_wa")).then_inc(loraw_in, 16)
        pool.wait_ge(feat_rows, 9 + CREDIT)
        for n, off in enumerate((OFF_KC, OFF_VC)):
            for tt in range(TT):
                src = nf[:, tt, off:off + G * HD].rearrange("p (g d) -> p g d", g=G).unsqueeze(2)
                v = G_.tensor_copy(kdup[:, n, tt], bc(src, [P, G, 2, HD]))
        v.then_inc(sig("c_dup"), 1)
        nsa_pool(pool)
        pool.wait_ge(sig("g_values"), G)
        pool.dma_start(g_up[:, 0, :], e["drams_of"]("loraw_g")[0:P, :]).then_inc(loraw_in, 16)
        pool.dma_start(g_up[0:32, 1, :], e["drams_of"]("loraw_g")[P:160, :]).then_inc(loraw_in, 16)
        G_.tensor_tensor(kkT[:, :, :], rkv[:, RW_T:2 * RW_T, :], bc(col("k_k", 0, 8).unsqueeze(2), [P, RW_T, S]),
                         ALU.mult).then_inc(sig("kk_made"), 1)
        pool.wait_ge(sig("kk_made"), 1)
        G_.tensor_tensor(sq8[:, :, :], kkT[:, :, :], kkT[:, :, :], ALU.mult).then_inc(sig("kk_squared"), 1)
        pool.wait_ge(sig("g_o_out"), G + CREDIT)
        for z in (bZ, kZ, vZ, kkZ):
            G_.memset(z[:, :, :], 0.0)
        G_.memset(SZ[:, :, :], 0.0)
        G_.memset(UZ[:, :, :], 0.0).then_inc(sig("r_cleared"), 1)
        rec_pool(pool)
        pool.wait_ge(y_lo_ready, 2)

    def turn(blocks):
        for m in range(blocks):
            w = P if m < 2 or blocks == 4 else 32
            for tt in range(TT):
                t = T.transpose(ps[0:w, 4 + m // 2, (m % 2) * S + tt * P:(m % 2) * S + (tt + 1) * P],
                                fst[:, tt, m * P:m * P + w], ident[:, :])
        t.then_inc(feat_turned, 1)

    def in_last_turn(pe):
        pe.wait_ge(feat_rows, 12 + CREDIT)
        pe.wait_ge(feat_T, 6 + CREDIT)
        turn(3)

    def in_pe(pe):
        with pe.Fori(0, 3) as i:
            for k in range(PAIR):
                if k == PAIR // 2:
                    pe.wait_ge(feat_rows, i * 2 + CREDIT)
                m = k % (PAIR // 2)
                slab_products(pe, S_IN, i, PAIR, k, x_hi, x_lo, (2 * m, 2 * m + 1), NCH, 2 * (k // 8), m == 0, m == 7,
                              fresh=2 if k < 8 else None)
                if k == 12:
                    pe.wait_ge(feat_rows, i * 2 + 1 + CREDIT)
                    pe.wait_ge(feat_T, i * 2 + CREDIT)
                    turn(4)
            pe.wait_ge(feat_rows, i * 2 + 2 + CREDIT)
            pe.wait_ge(feat_T, i * 2 + 1 + CREDIT)
            turn(4)
        with pe.Fori(0, 2) as i:
            for k in range(PAIR):
                if k == PAIR // 2:
                    pe.wait_ge(feat_rows, i * 2 + 6 + CREDIT)
                m = k % (PAIR // 2)
                slab_products(pe, NS0, i, PAIR, k, x_hi, x_lo, (2 * m, 2 * m + 1), NCH, 2 * (k // 8), m == 0, m == 7)
            pe.wait_ge(feat_rows, i * 2 + 7 + CREDIT)
        chunk_products(pe, TL0, None, 0, 0, NCH, 0)
        pe.wait_ge(feat_rows, 10 + CREDIT)
        chunk_products(pe, TL0, None, 0, 8, TAIL_IN, 2)

    def in_act(act):
        def rows(dst, bank0, w=NCH):
            for tt in range(TT):
                a = A.activation(dst(tt), ps[:, bank0 + tt, 0:w], ACT.Copy)
            a.then_inc(feat_rows, 1)

        def turned():
            for b in range(2):
                a = A.activation(shb[:, 2 * b:2 * b + 2, 1:S + 1], bank(4 + b, S), ACT.Copy)
            a.then_inc(feat_T, 1)

        def streams(i, done=0):
            for k in range(done, PAIR):
                split_hi(act, S_IN, i, PAIR, k, SLAB)
                if k == 11:
                    used(act, S_IN, i, PAIR, 7)
                    act.wait_ge(feat_turned, i * 2 + CREDIT)
                    rows(lambda tt: fst[:, tt, :], 0)
            act.wait_ge(feat_turned, i * 2 + 1 + CREDIT)
            act.wait_ge(shifted, i * 2 + CREDIT)
            turned()
            used(act, S_IN, i, PAIR, PAIR - 1)
            rows(lambda tt: fst[:, tt, :], 2)
            act.wait_ge(feat_turned, i * 2 + 2 + CREDIT)
            act.wait_ge(shifted, i * 2 + 1 + CREDIT)
            turned()
        streams(0, AHEAD)
        with act.Fori(1, 3) as i:
            streams(i)
        with act.Fori(0, 2) as i:
            for k in range(PAIR):
                split_hi(act, NS0, i, PAIR, k, SLAB)
                if k == 11:
                    used(act, NS0, i, PAIR, 7)
                    rows(lambda tt: nf[:, tt, bass.ds(i * (2 * NCH), NCH)], 0)
            used(act, NS0, i, PAIR, PAIR - 1)
            rows(lambda tt: nf[:, tt, bass.ds(i * (2 * NCH) + NCH, NCH)], 2)
        for k in range(PAIR):
            split_hi(act, TL0, None, 0, k, SLAB if k < 8 else 2 * TAIL_IN)
            if k == 11:
                used(act, TL0, None, 0, 7)
                rows(lambda tt: nf[:, tt, 4 * NCH:5 * NCH], 0)
        used(act, TL0, None, 0, PAIR - 1)
        for tt in range(TT):
            A.activation(fst[:, tt, 0:LORA], ps[:, 2 + tt, 0:LORA], ACT.Copy)
            a = A.activation(nf[:, tt, OFF_GL:OFF_GL + 48], ps[:, 2 + tt, LORA:TAIL_IN], ACT.Copy)
        a.then_inc(feat_rows, 1)

    def in_last_turned(act):
        act.wait_ge(feat_turned, 7 + CREDIT)
        act.wait_ge(shifted, 6 + CREDIT)
        A.activation(shb[:, 0:2, 1:S + 1], bank(4, S), ACT.Copy)
        A.activation(shb[0:32, 2, 1:S + 1], ps[0:32, 5, 0:S], ACT.Copy).then_inc(feat_T, 1)

    MU = COLS["mu"]

    def shift(dst, mu0, q, n):
        V.tensor_tensor(dif[0:q, 0:n, :], shb[0:q, 0:n, 0:S], shb[0:q, 0:n, 1:S + 1], ALU.subtract)
        settle()
        mu = cols[0:q, bass.ds(mu0, n)].unsqueeze(2)
        V.tensor_tensor(dif[0:q, 0:n, :], dif[0:q, 0:n, :], bc(mu, [q, n, S]), ALU.mult)
        settle()
        return V.tensor_tensor(dst, dif[0:q, 0:n, :], shb[0:q, 0:n, 1:S + 1], ALU.add)

    def in_dve(dve):
        dve.wait_ge(mc_in, 16)
        V.memset(shb[:, :, 0:1], 0.0)
        settle()
        def streams(i, done=0):
            for k in range(done, PAIR):
                split_lo(dve, S_IN, i, PAIR, k, SLAB)
            for c in range(2):
                dve.wait_ge(feat_T, i * 2 + c + 1 + CREDIT)
                shift(rkv[:, bass.ds(i * 8 + 4 * c, 4), :], i * 8 + (MU + 4 * c), P, 4).then_inc(shifted, 1)
        streams(0, AHEAD)
        with dve.Fori(1, 3) as i:
            streams(i)
        with dve.Fori(0, 2) as i:
            for k in range(PAIR):
                split_lo(dve, NS0, i, PAIR, k, SLAB)
        for k in range(PAIR):
            split_lo(dve, TL0, None, 0, k, SLAB if k < 8 else 2 * TAIL_IN)

    def in_last_shift(dve):
        dve.wait_ge(feat_T, 7 + CREDIT)
        shift(lora[:, 0:2, :], MU + 24, P, 2)
        settle()
        V.tensor_tensor(dif[0:32, 0, :], shb[0:32, 2, 0:S], shb[0:32, 2, 1:S + 1], ALU.subtract)
        settle()
        V.scalar_tensor_tensor(out=lora[0:32, 2, :], in0=dif[0:32, 0, :], scalar=cols[0:32, MU + 26:MU + 27],
                               in1=shb[0:32, 2, 1:S + 1], op0=ALU.mult, op1=ALU.add).then_inc(shifted, 1)

    W = G * N_CMP

    def lora_up(k):
        for j in range(RW_T):
            m = T.matmul(ps[:, 4 + j // 2, (j % 2) * S:(j % 2 + 1) * S], wa_up[64 * k:64 * k + 64, P * j:P * (j + 1)],
                         lora[64 * k:64 * k + 64, 0, :], start=True, stop=True)
        m.then_inc(sig("wa_done"), 1)

    def sigmoids(act, k, dst, bias):
        act.wait_ge(sig("wa_done"), k + 1)
        for j in range(RW_T):
            a = A.activation(dst[:, j, :], ps[:, 4 + j // 2, (j % 2) * S:(j % 2 + 1) * S], ACT.Sigmoid, bias=col(bias, j))
        a.then_inc(sig("wa_out"), 1)

    def pre_pe(pe):
        pe.wait_ge(sig("c_dup"), 1)
        for n in range(2):
            for g in range(G):
                for tt in range(TT):
                    t = T.transpose(ps[:, 6 * n + g // 2, (g % 2) * S + tt * P:(g % 2) * S + (tt + 1) * P],
                                    kdup[:, n, tt, g].rearrange("p a d -> p (a d)"), ident[:, :])
            t.then_inc(sig("c_turned"), 1)
        in_last_turn(pe)
        pe.wait_ge(w1_in, 80)
        pe.wait_ge(sig("c_pe"), 1)
        for n in range(2):
            pe.wait_ge(sig("c_T"), n + 1)
            for j in range(16):
                m = T.matmul(ps[:, 3, n * S:n * S + W + N_CMP], w1[:, n, j, :], kc2[:, n, :, 2 * j:2 * j + 16 * 14 + 1:16],
                             start=j == 0, stop=j == 15)
        m.then_inc(sig("c_hidden"), 1)
        pe.wait_ge(loraw_in, 16)
        pe.wait_ge(sig("lora_act"), 1)
        lora_up(0)
        pe.wait_ge(sig("c_gelu"), 1)
        T.matmul(ps[:, 3, 0:W], w2[:, 0:2, :].rearrange("p a d -> p (a d)"), hid[:, 6, 0:W],
                 start=True, stop=True).then_inc(sig("kc_done"), 1)
        for g in range(G):
            m = T.matmul(ps[:, 2, g * HD:(g + 1) * HD], hidrep[:, g].rearrange("p a n -> p (a n)"), w2[:, 2, :],
                         start=True, stop=True)
        m.then_inc(sig("vc_done"), 1)
        pe.wait_ge(sig("vblk_ready"), 1)

    def pre_act(act):
        for n in range(2):
            act.wait_ge(sig("c_turned"), n + 1)
            v = banks(6 * n, 2, S)
            A.activation(kc2[0:HD, n, 0:G, :], v[0:HD], ACT.Copy)
            A.activation(kc2[HD:P, n, 0:G, 0:S - 1], v[HD:P, :, 1:S], ACT.Copy).then_inc(sig("c_T"), 1)
            if n == 0:
                in_last_turned(act)
        act.wait_ge(shifted, 7 + CREDIT)
        A.activation(lora[0:64, 0, :], lora[0:64, 0, :], ACT.Tanh)
        A.activation(lora[:, 1, :], lora[:, 1, :], ACT.Sigmoid)
        A.activation(lora[0:32, 2, :], lora[0:32, 2, :], ACT.Sigmoid).then_inc(sig("lora_act"), 1)
        A.activation(gates[:, :, :], nf[:, :, OFF_GL:OFF_GL + 48], ACT.Sigmoid).then_inc(sig("gates_ready"), 1)
        act.wait_ge(sig("c_inner"), 1)
        A.activation(hid[:, 4:6, 0:W], hid[:, 2:4, 0:W], ACT.Tanh, scale=0.7978845608028654).then_inc(sig("c_tanh"), 1)
        sigmoids(act, 0, wT, "w0")
        act.wait_ge(sig("kc_done"), 1)
        A.activation(kcT[:, :, 0:N_CMP], ps[:, 3, 0:W].rearrange("p (g n) -> p g n", g=G),
                     ACT.Copy).then_inc(sig("kcT_ready"), 1)

    def pre_dve(dve):
        dve.wait_ge(feat_rows, 12 + CREDIT)
        V.memset(kc2[:, :, G, :], 0.0)
        settle()
        V.tensor_copy(kc2[:, :, G, 0:32:2], cols[:, COLS["pe_k"]:COLS["pe_k"] + 32].rearrange("p (n j) -> p n j", n=2)
                      ).then_inc(sig("c_pe"), 1)
        in_last_shift(dve)
        for tt in range(TT):
            for kind in ("q", "k"):
                if kind == "q":
                    heads = nf[:, tt, 0:1024].rearrange("p (h d) -> p h d", d=HD)
                    x1, x2 = heads[:, :, 0:ROPE_H], heads[:, :, ROPE_H:2 * ROPE_H]
                    o1, o2 = qrot[:, tt, :, 0:ROPE_H], qrot[:, tt, :, ROPE_H:2 * ROPE_H]
                    cs, sn = (bc(a[:, tt].unsqueeze(1), [P, 16, ROPE_H]) for a in (cos, sin))
                    views = [(x1, x2, o1, o2, [rt[:, m, 0:16, :] for m in range(4)])]
                else:
                    views = []
                    for off in (OFF_KS, OFF_KW):
                        heads = nf[:, tt, off:off + 256].rearrange("p (h d) -> p h d", d=HD)
                        x1, x2 = heads[:, :, 0:ROPE_H], heads[:, :, ROPE_H:2 * ROPE_H]
                        views.append((x1, x2, x1, x2, [rt[:, m, 0:4, :] for m in range(4)]))
                    cs, sn = (bc(a[:, tt].unsqueeze(1), [P, 4, ROPE_H]) for a in (cos, sin))
                for x1, x2, o1, o2, tb in views:
                    settle()
                    V.tensor_tensor(tb[0], x1, cs, ALU.mult)
                    V.tensor_tensor(tb[1], x2, sn, ALU.mult)
                    V.tensor_tensor(tb[2], x2, cs, ALU.mult)
                    V.tensor_tensor(tb[3], x1, sn, ALU.mult)
                    settle()
                    V.tensor_tensor(o1, tb[0], tb[1], ALU.subtract)
                    v = V.tensor_tensor(o2, tb[2], tb[3], ALU.add)
        v.then_inc(sig("nsa_prepared"), 1)
        V.memset(pc[:, :, :, :], 0.0)
        V.memset(hidrep[:, :, :, :], 0.0)
        dve.wait_ge(sig("c_hidden"), 1)
        x, t, y = hid[:, 0:2, 0:W], hid[:, 2:4, 0:W], hid[:, 6:8, 0:W]
        V.tensor_copy(hb[:, :], bank(3, S)[:, :, W])
        settle()
        V.tensor_tensor(x, bank(3, S)[:, :, 0:W], bc(hb[:, :].unsqueeze(2), [P, 2, W]), ALU.add)
        settle()
        V.tensor_tensor(t, x, x, ALU.mult)
        settle()
        V.tensor_tensor(t, t, x, ALU.mult)
        settle()
        V.scalar_tensor_tensor(out=t, in0=t, scalar=0.044715, in1=x, op0=ALU.mult, op1=ALU.add).then_inc(sig("c_inner"), 1)
        dve.wait_ge(sig("c_tanh"), 1)
        V.scalar_tensor_tensor(out=y, in0=hid[:, 4:6, 0:W], scalar=1.0, in1=x, op0=ALU.add, op1=ALU.mult)
        settle()
        V.tensor_scalar(y, y, 0.5, None, ALU.mult)
        settle()
        V.tensor_copy(hidrep[:, :, :, 0:N_CMP],
                      bc(hid[:, 7, 0:W].rearrange("p (g n) -> p g n", g=G).unsqueeze(2), [P, G, 4, N_CMP])
                      ).then_inc(sig("c_gelu"), 1)
        dve.wait_ge(sig("vc_done"), 1)
        V.tensor_tensor(vblk[:, :, :, :],
                        bc(ps[:, 2, 0:G * HD].rearrange("p (g d) -> p g d", g=G).unsqueeze(2), [P, G, 4, HD]),
                        bc(msk("blk").unsqueeze(1).unsqueeze(3), [P, G, 4, HD]), ALU.mult).then_inc(sig("vblk_ready"), 1)

    def nsa_pool(pool):
        def rows(n):
            q = nf[:, :, bass.ds(n * 256, 256)].rearrange("p t (a d) -> p t a d", a=4)
            nc.gpsimd.tensor_copy(qr[:, :, :, 2 * ROPE_H:], q[:, :, :, 2 * ROPE_H:])
            nc.gpsimd.tensor_copy(qr[:, :, :, 0:2 * ROPE_H], qrot[:, :, bass.ds(n * 4, 4), :])
            for b, off in enumerate((OFF_KS, OFF_KW)):
                for tt in range(TT):
                    nc.gpsimd.tensor_copy(kk2[:, b, tt], bc(nf[:, tt, bass.ds(n * HD + off, HD)].unsqueeze(1), [P, 2, HD]))
            nc.gpsimd.tensor_copy(qn[:, :, :, :], q).then_inc(sig("g_rows"), 1)

        def values(n):
            for b, off in enumerate((OFF_VS, OFF_VW)):
                nc.gpsimd.tensor_copy(vv[:, b], nf[:, :, bass.ds(n * HD + off, HD)])
            for tt in range(TT):
                nc.gpsimd.tensor_copy(gg[:, tt], gates[:, tt, :].rearrange("p (b h) -> p b h", b=3)[:, :, bass.ds(n * 4, 4)])
            nc.gpsimd.tensor_copy(vbg[:, :, :], vblk[:, bass.ds(n, 1)].rearrange("p a b d -> p (a b) d")
                                  ).then_inc(sig("g_values"), 1)

        def keys(n):
            nc.gpsimd.tensor_copy(kcg[:, 0:N_CMP], kcT[:, bass.ds(n, 1), 0:N_CMP].rearrange("p a n -> p (a n)")
                                  ).then_inc(sig("g_keys"), 1)

        pool.wait_ge(sig("nsa_prepared"), 1)
        rows(0)
        pool.wait_ge(sig("kcT_ready"), 1)
        keys(0)
        pool.wait_ge(sig("gates_ready"), 1)
        pool.wait_ge(sig("vblk_ready"), 1)
        values(0)
        with pool.Fori(1, G) as n:
            pool.wait_ge(sig("g_turned"), n)
            rows(n)
            pool.wait_ge(sig("g_scores"), n * 2 - 1)
            keys(n)
            pool.wait_ge(sig("g_o"), n + CREDIT)
            values(n)

    def nsa_pe(pe):
        def turn_rows(n):
            pe.wait_ge(sig("g_rows"), n + 1)
            for src, b in ((qn, 0), (qr, 1)):
                for j in range(2):
                    for tt in range(TT):
                        T.transpose(ps[:, b, j * S + tt * P:j * S + (tt + 1) * P],
                                    src[:, tt, 2 * j:2 * j + 2, :].rearrange("p a d -> p (a d)"), ident[:, :])
            for b in range(2):
                for tt in range(TT):
                    t = T.transpose(ps[:, 2, b * S + tt * P:b * S + (tt + 1) * P],
                                    kk2[:, b, tt].rearrange("p a d -> p (a d)"), ident[:, :])
            t.then_inc(sig("g_turned"), 1)

        def scores(b):
            for p in range(2):
                r = slice(64 * p, 64 * p + 64)
                for j in range(2):
                    T.matmul(ps[:, p, j * P:(j + 1) * P], qrT[r, j, 0:P], kT[r, b, 0:P], start=True, stop=True)
                    m = T.matmul(ps[:, 2 + p, j * S:(j + 1) * S], qrT[r, j, P:S], kT[r, b, :], start=True, stop=True)
                    if b == 0:
                        for tt in range(TT):
                            c0 = S + (2 * tt + j) * 16
                            m = T.matmul(ps[:, p, c0:c0 + N_CMP], qnT[r, j, tt * P:(tt + 1) * P], kcg[r, 0:N_CMP],
                                         start=True, stop=True)
            m.then_inc(sig("g_scores"), 1)

        def turn_probs(n, b):
            pe.wait_ge(sig("g_probs"), n * 2 + b + 1)
            if b == 0:
                pe.wait_ge(sig("g_o_out"), n + CREDIT)
                for tt in range(TT):
                    T.transpose(ps[:, 7, tt * P:(tt + 1) * P], pc[:, tt].rearrange("p a n -> p (a n)"), ident[:, :])
            for j in range(2):
                for p in range(2):
                    T.transpose(ps[:, 4 + j, p * S:p * S + P], p0[:, b, 2 * p + j, :], ident[:, :])
                    T.transpose(ps[:, 4 + j, p * S + P:(p + 1) * S], p1[:, b, 2 * p + j, 0:P], ident[:, :])
                    t = T.transpose(ps[:, 6, (2 * j + p) * P:(2 * j + p + 1) * P], p1[:, b, 2 * p + j, P:S], ident[:, :])
            t.then_inc(sig("g_p_turned"), 1)

        def outputs(n, b):
            pe.wait_ge(sig("g_pT_act"), n * 2 + b + 1)
            pe.wait_ge(sig("g_pT_dve"), n * 2 + b + 1)
            if b == 0:
                pe.wait_ge(sig("g_values"), n + 1)
                for j in range(2):
                    T.matmul(ps[:, 7, j * S:(j + 1) * S], vbg[:, 2 * j:2 * j + 2, :].rearrange("p a d -> p (a d)"),
                             pcT[:, :], start=j == 0, stop=False, skip_group_check=True)
            for j in range(2):
                for p in range(2):
                    r = slice(64 * p, 64 * p + 64)
                    T.matmul(ps[r, 7, j * S:(j + 1) * S], vv[:, b, 0, :], pT0[:, b, 2 * j + p, :],
                             start=False, stop=False, skip_group_check=True)
                    m = T.matmul(ps[r, 7, j * S + P:(j + 1) * S], vv[:, b, 1, :], pT1[:, b, 2 * j + p, :],
                                 start=False, stop=b == 1, skip_group_check=True)
            if b == 1:
                m.then_inc(sig("g_o"), 1)

        def group(n, last=False):
            pe.wait_ge(sig("g_masked"), n * 2 + 1)
            scores(1)
            if not last:
                pe.wait_ge(sig("g_masked"), n * 2 + 2)
                turn_rows(n + 1)
            turn_probs(n, 0)
            if not last:
                pe.wait_ge(sig("g_keys"), n + 2)
                pe.wait_ge(sig("g_T"), n + 2)
                scores(0)
            outputs(n, 0)
            turn_probs(n, 1)
            outputs(n, 1)

        turn_rows(0)
        pe.wait_ge(sig("wa_out"), 1)
        lora_up(1)
        pe.wait_ge(sig("g_keys"), 1)
        pe.wait_ge(sig("g_T"), 1)
        scores(0)
        with pe.Fori(0, G - 1) as n:
            group(n)
        group(G - 1, last=True)

    def nsa_act(act):
        def rows_T(n):
            act.wait_ge(sig("g_turned"), n + 1)
            A.activation(qrT[:, :, :], bank(1, S), ACT.Copy, scale=HD ** -0.5)
            A.activation(kT[:, :, :], bank(2, S), ACT.Copy)
            A.activation(qnT[:, :, :], bank(0, S), ACT.Copy, scale=HD ** -0.5).then_inc(sig("g_T"), 1)

        def exps(n, b):
            act.wait_ge(sig("g_max"), n * 2 + b + 1)
            if b == 0:
                cmp = pc[:, :, :, 0:N_CMP].rearrange("p t a n -> p (t a) n")
                A.activation(cmp, cmp, ACT.Exp)
            for k in range(4):
                A.activation(p0[:, b, k, :], p0[:, b, k, :], ACT.Exp, bias=sm[:, b, 0, k:k + 1],
                             accum_out=sm[:, b, 1, k:k + 1])
                a = A.activation(p1[:, b, k, :], p1[:, b, k, :], ACT.Exp, bias=sm[:, b, 0, 4 + k:5 + k],
                                 accum_out=sm[:, b, 1, 4 + k:5 + k])
            a.then_inc(sig("g_exp"), 1)

        def probs_T(n, b):
            act.wait_ge(sig("g_p_turned"), n * 2 + b + 1)
            if b == 0:
                A.activation(pcT[:, :], ps[:, 7, 0:S], ACT.Copy)
            A.activation(pT0[:, b], banks(4, 2, S), ACT.Copy).then_inc(sig("g_pT_act"), 1)

        def group(n, last=False):
            exps(n, 0)
            if not last:
                rows_T(n + 1)
            exps(n, 1)
            probs_T(n, 0)
            probs_T(n, 1)
            act.wait_ge(sig("g_o"), n + 1 + CREDIT)
            A.activation(yN[:, bass.ds(n * 2, 2), :], bank(7, S), ACT.Copy).then_inc(sig("g_o_out"), 1)

        rows_T(0)
        sigmoids(act, 1, aT, "a0")
        A.activation(wT[:, :, :], wT[:, :, :], ACT.Exp, scale=DECAY)
        with act.Fori(0, G - 1) as n:
            group(n)
        group(G - 1, last=True)

    def nsa_dve(dve):
        causal = msk("causal")
        cmp = pc[:, :, :, 0:N_CMP].rearrange("p t a n -> p (t a) n")

        def masked(n, b):
            dve.wait_ge(sig("g_scores"), n * 2 + b + 1)
            for p in range(2):
                V.tensor_tensor(p0[:, b, 2 * p:2 * p + 2, :], ps[:, p, 0:S].rearrange("p (j k) -> p j k", j=2),
                                bc(causal[:, P:2 * P].unsqueeze(1), [P, 2, P]), ALU.add)
                x = V.tensor_tensor(p1[:, b, 2 * p:2 * p + 2, :], bank(2 + p, S), bc(causal.unsqueeze(1), [P, 2, S]), ALU.add)
                if b == 0:
                    s = ps[:, p, S:S + 64].rearrange("p (t j n) -> p t j n", t=TT, j=2)[:, :, :, 0:N_CMP]
                    x = V.tensor_tensor(pc[:, :, :, :].rearrange("q t (j p) n -> q t j p n", p=2)[:, :, :, p, 0:N_CMP], s,
                                        bc(cmp_add.unsqueeze(2), [P, TT, 2, N_CMP]), ALU.add)
            x.then_inc(sig("g_masked"), 1)
            settle()
            V.tensor_reduce(sm[:, b, 0, 0:4], p0[:, b], AX.X, ALU.max, negate=True)
            x = V.tensor_reduce(sm[:, b, 0, 4:8], p1[:, b], AX.X, ALU.max, negate=True)
            if b == 0:
                V.tensor_reduce(smc[:, 0, :], cmp, AX.X, ALU.max, negate=True)
                settle()
                x = V.tensor_tensor(cmp, cmp, bc(smc[:, 0, :].unsqueeze(2), [P, 8, N_CMP]), ALU.add)
            x.then_inc(sig("g_max"), 1)

        def probs(n, b):
            dve.wait_ge(sig("g_exp"), n * 2 + b + 1)
            if b == 0:
                dve.wait_ge(sig("g_values"), n + 1)
                V.tensor_reduce(smc[:, 1, :], cmp, AX.X, ALU.add)
            V.reciprocal(sm[:, b, 2, :], sm[:, b, 1, :])
            settle()
            V.tensor_tensor(sm[:, b, 3, :].rearrange("q (t p j) -> q t p j", t=TT, p=2),
                            sm[:, b, 2, :].rearrange("q (t p j) -> q t p j", t=TT, p=2),
                            gg[:, :, 1 + b, :].rearrange("q t (j p) -> q t p j", p=2), ALU.mult)
            if b == 0:
                V.reciprocal(smc[:, 2, :], smc[:, 1, :])
                V.tensor_tensor(pc[:, :, :, 0:N_CMP], pc[:, :, :, 0:N_CMP], bc(cmp_mul.unsqueeze(2), [P, TT, 4, N_CMP]),
                                ALU.mult)
            settle()
            if b == 0:
                V.tensor_tensor(smc[:, 3, :].rearrange("p (t a) -> p t a", t=TT),
                                smc[:, 2, :].rearrange("p (t a) -> p t a", t=TT), gg[:, :, 0, :], ALU.mult)
            V.tensor_tensor(p0[:, b], p0[:, b], bc(sm[:, b, 3, 0:4].unsqueeze(2), [P, 4, P]), ALU.mult)
            x = V.tensor_tensor(p1[:, b], p1[:, b], bc(sm[:, b, 3, 4:8].unsqueeze(2), [P, 4, S]), ALU.mult)
            if b == 0:
                settle()
                x = V.tensor_tensor(cmp, cmp, bc(smc[:, 3, :].unsqueeze(2), [P, 8, N_CMP]), ALU.mult)
            x.then_inc(sig("g_probs"), 1)

        def probs_T(n, b):
            dve.wait_ge(sig("g_p_turned"), n * 2 + b + 1)
            V.tensor_copy(pT1[:, b], bank(6, P)).then_inc(sig("g_pT_dve"), 1)

        def group(n, last=False):
            masked(n, 1)
            probs(n, 0)
            probs_T(n, 0)
            if not last:
                masked(n + 1, 0)
            probs(n, 1)
            probs_T(n, 1)

        masked(0, 0)
        with dve.Fori(0, G - 1) as n:
            group(n)
        group(G - 1, last=True)

    def hsum(src, dst):
        for j in range(RW_T):
            m = T.matmul(dst, msk("hsel")[:, 16 * j:16 * j + 16], src[:, j, :], start=j == 0, stop=j == RW_T - 1)
        return m

    def hspread(src, bank0):
        for j in range(RW_T):
            m = T.matmul(ps[:, bank0 + j // 2, (j % 2) * S:(j % 2 + 1) * S], msk("hselT")[0:16, P * j:P * (j + 1)], src,
                         start=True, stop=True)
        return m

    def kk_pe(pe):
        pe.wait_ge(sig("kk_squared"), 1)
        pe.wait_ge(sig("g_o_out"), G + CREDIT)
        hsum(sq8, ps[0:16, 4, 0:S]).then_inc(sig("kk_summed"), 1)
        pe.wait_ge(sig("kk_rnorm"), 1)
        hspread(nrm[0:16, 1, :], 4).then_inc(sig("kk_spread"), 1)

    def kk_act(act):
        act.wait_ge(sig("kk_clamped"), 1)
        A.activation(nrm[0:16, 2, :], nrm[0:16, 0, :], ACT.Sqrt).then_inc(sig("kk_root"), 1)

    def kk_dve(dve):
        def keys_ready():
            dve.wait_ge(sig("kk_summed"), 1)
            V.tensor_scalar(nrm[0:16, 0, :], ps[0:16, 4, 0:S], 1e-24, None, ALU.max).then_inc(sig("kk_clamped"), 1)
            dve.wait_ge(sig("kk_root"), 1)
            V.reciprocal(nrm[0:16, 1, :], nrm[0:16, 2, :]).then_inc(sig("kk_rnorm"), 1)
            dve.wait_ge(sig("kk_spread"), 1)
            V.tensor_tensor(kkT[:, :, :], kkT[:, :, :], banks(4, 4, S), ALU.mult)
            settle()
            dve.wait_ge(sig("r_cleared"), 1)

        dve.wait_ge(sig("g_o_out"), G + CREDIT)
        prepare(V, 0, keys_ready)

    HALVES = (slice(0, C), slice(C, P))
    UNITS = [(j, c) for j in range(2) for c in range(NC)]

    def blk4(ap):
        return ap.rearrange("p j (c t) -> p (j c) t", t=C)

    def odd(ap, b):
        if len(ap.shape) == 2:
            return ap.rearrange("p (q s b) -> p q s b", s=2, b=b)[:, :, 1, :]
        return ap.rearrange("p u (q s b) -> p u q s b", s=2, b=b)[:, :, :, 1, :]

    def prepare(eng, n, keys_ready=None):
        pool = eng is nc.gpsimd
        two = bass.ds(n * 2, 2)
        r, k, v = rkv[:, two, :], rkv[:, bass.ds(n * 2 + RW_T, 2), :], rkv[:, bass.ds(n * 2 + 2 * RW_T, 2), :]
        w, a, kk = wT[:, two, :], aT[:, two, :], kkT[:, two, :]
        ka = bc(cols[:, bass.ds(n * 2 + COLS["k_a"], 2)].unsqueeze(2), [P, 2, S])
        rk = bc(cols[:, bass.ds(n * 2 + COLS["r_k"], 2)].unsqueeze(2), [P, 2, S])
        if pool:
            eng.wait_ge(sig("r_bonus"), n)
            eng.wait_ge(sig("r_vZ"), n)
        eng.tensor_copy(kp[:, :, :], k)
        eng.tensor_tensor(tmp[:, :, :], w, bc(msk("notstart").unsqueeze(1), [P, 2, S]), ALU.mult)
        x = eng.tensor_tensor(iP[:, :, :], w, bc(msk("start").unsqueeze(1), [P, 2, S]), ALU.mult)
        if pool:
            x.then_inc(sig("r_scan_in"), 1)
            eng.wait_ge(sig("r_scan"), n)
            eng.tensor_copy(vq[:, :, :], v)
        else:
            eng.drain()
            scan()
        eng.tensor_copy(Pn[:, :, :], Pd[:, :, C - 1:S:C])
        eng.tensor_tensor(tmp[:, :, :], a, ka, ALU.mult)
        eng.tensor_tensor(kp[:, :, :], kp[:, :, :], ka, ALU.mult)
        eng.tensor_tensor(rtn[:, :, :], r, Pd[:, :, :], ALU.mult)
        eng.drain()
        eng.tensor_tensor(tmp[:, :, :], tmp[:, :, :], k, ALU.mult)
        eng.tensor_tensor(kp[:, :, :], k, kp[:, :, :], ALU.subtract)
        eng.drain()
        eng.tensor_tensor(kp[:, :, :], kp[:, :, :], tmp[:, :, :], ALU.add)
        eng.drain()
        if keys_ready:
            keys_ready()
            eng.tensor_copy(vq[:, :, :], v)
        eng.tensor_tensor(bon[:, :, :], r, kp[:, :, :], ALU.mult)
        eng.tensor_tensor(tmp[:, :, :], kk, a, ALU.mult)
        kd = kkd[:, :, :].rearrange("p j (c t) -> p j c t", t=C)
        kk4 = kk.rearrange("p j (c t) -> p j c t", t=C)
        pd4 = Pd[:, :, :].rearrange("p j (c t) -> p j c t", t=C)
        for j in range(2):
            eng.tensor_tensor(kd[:, j, :, 1:C], kk4[:, j, :, 1:C], pd4[:, j, :, 0:C - 1], ALU.mult)
        eng.tensor_copy(kd[:, :, :, 0:1], kk4[:, :, :, 0:1])
        eng.drain()
        eng.tensor_tensor(bon[:, :, :], bon[:, :, :], rk, ALU.mult)
        for p, rr in enumerate(HALVES):
            cs = slice(p * C, (p + 1) * C)
            eng.drain()
            if pool and p == 0:
                eng.wait_ge(sig("r_turned"), n * 3)
            eng.tensor_tensor(bZ[rr, :, cs], blk4(tmp[rr]), blk4(iP[rr]), ALU.mult)
            x = eng.tensor_tensor(kZ[rr, :, cs], blk4(kp[rr]), blk4(iP[rr]), ALU.mult)
        x.then_inc(sig("r_prep"), 1)

    def scan():
        V.tensor_tensor_scan(Pd[:, :, :].rearrange("p j t -> p (j t)"), tmp[:, :, :].rearrange("p j t -> p (j t)"),
                             iP[:, :, :].rearrange("p j t -> p (j t)"), 0.0, ALU.mult, ALU.add)
        settle()
        return V.reciprocal(iP[:, :, :], Pd[:, :, :])

    def rec_pool(pool):
        with pool.Fori(1, RW_T // 2) as n:
            pool.wait_ge(sig("r_prep"), n)
            pool.wait_ge(sig("r_kkZ_dve"), n)
            pool.wait_ge(sig("r_kkZ_act"), n)
            prepare(nc.gpsimd, n)

    def rec_pe(pe):
        with pe.Fori(0, RW_T // 2) as i:
            pe.wait_ge(sig("r_prep"), i + 1)
            pe.wait_ge(sig("r_y_out"), i * NC + CREDIT)
            T.matmul(ps[:, 7, :], msk("bones"), bon[:, :, :].rearrange("p j t -> p (j t)"), start=True,
                     stop=True).then_inc(sig("r_bonus"), 1)

            def gram(bank0, lhs, rhs, w, name):
                for u in range(8):
                    n = u * w // NCH
                    m = T.matmul(ps[:, bank0 + n, u * w - n * NCH:(u + 1) * w - n * NCH], lhs[:, u, :], rhs(u),
                                 start=True, stop=True)
                m.then_inc(sig(name), 1)

            pe.wait_ge(sig("r_kkZ_act"), i + 1)
            pe.wait_ge(sig("r_kkZ_dve"), i + 1)
            gram(0, bZ, lambda u: kkZ[:, u, :], P, "r_AT")
            gram(2, kkZ, lambda u: bZ[:, u, :], P, "r_Ap")
            gram(6, bZ, lambda u: rt_[:, u // NC, (u % NC) * C:(u % NC + 1) * C], C, "r_Qbp")
            pe.wait_ge(sig("r_bonus_out"), i + 1)
            gram(7, kZ, lambda u: rt_[:, u // NC, (u % NC) * C:(u % NC + 1) * C], C, "r_Qkp")
            gram(4, kZ, lambda u: kkZ[:, u, :], P, "r_Bmp")

            def turn(src, n):
                if n == 0:
                    pe.wait_ge(sig("r_vZ"), i + 1)
                    pe.wait_ge(sig("r_gram_out"), i + 1)
                else:
                    pe.wait_ge(sig("r_t"), i * 3 + n)
                for u in range(8):
                    t = T.transpose(ps[:, 4 + u // 4, (u % 4) * P:(u % 4 + 1) * P], src[:, u, :], ident[:, :])
                t.then_inc(sig("r_turned"), 1)

            pe.wait_ge(sig("r_A"), i + 1)
            pe.wait_ge(sig("r_Q"), i + 1)
            for n in range(len(LEVELS)):
                for g in range(2):
                    pe.wait_ge(sig("r_x"), i * 12 + 2 * n + g + 1)
                    for u in range(4 * g, 4 * g + 4):
                        m = T.matmul(ps[:, g, (u % 4) * C:(u % 4 + 1) * C], Am[:, u, :], odd(Xm[:, u, :], LEVELS[n]),
                                     start=True, stop=True)
                    m.then_inc(sig("r_AX"), 1)
                    for u in range(4 * g, 4 * g + 4):
                        m = T.transpose(ps[:, 6 + g, (u % 4) * P:(u % 4 + 1) * P], Xm[:, u, :], ident[:, :])
                    m.then_inc(sig("r_XT"), 1)
                if 1 <= n <= 3:
                    turn((vZ, kZ, bZ)[n - 1], n - 1)
                for g in range(2):
                    pe.wait_ge(sig("r_Y"), i * 10 + 2 * n + g + 1)
                    pe.wait_ge(sig("r_Z"), i * 10 + 2 * n + g + 1)
                    for u in range(4 * g, 4 * g + 4):
                        m = T.matmul(ps[:, 2 + g, (u % 4) * C:(u % 4 + 1) * C], Zm[:, u, :], Ym[:, u, :], start=True, stop=True)
                    m.then_inc(sig("r_XY"), 1)
            pe.wait_ge(sig("r_x"), i * 12 + 12)
            pe.wait_ge(sig("r_t"), i * 3 + 3)
            for c in range(NC):
                for j in range(2):
                    u, js = j * NC + c, slice(j * C, (j + 1) * C)
                    m = T.matmul(ps[:, 6, js], Bm[:, u, :], Vt[:, u, :], start=j == 0, stop=c == 0, skip_group_check=True)
                if c:
                    pe.wait_ge(sig("r_S"), i * 3 + c)
                    for j in range(2):
                        m = T.matmul(ps[:, 6, j * C:(j + 1) * C], kkZ[:, j * NC + c, :], Sc[:, j, :], start=False, stop=True,
                                     skip_group_check=True)
                m.then_inc(sig("r_W"), 1)
                if c < NC - 1:
                    for j in range(2):
                        u, js = j * NC + c, slice(j * C, (j + 1) * C)
                        T.matmul(ps[:, 0, js], KtZ[:, u, :], Vt[:, u, :], start=j == 0, stop=False, skip_group_check=True)
                pe.wait_ge(sig("r_Wc"), i * NC + c + 1)
                for j in range(2):
                    m = T.matmul(ps[:, 7, j * C:(j + 1) * C], Xm[:, j * NC + c, :], Wc[:, j, :], start=True, stop=True)
                m.then_inc(sig("r_U"), 1)
                if c:
                    pe.wait_ge(sig("r_SZ"), i * 3 + c)
                if c >= 2:
                    pe.wait_ge(sig("r_y_out"), i * NC + c - 1 + CREDIT)
                for j in range(2):
                    u = j * NC + c
                    T.matmul(ps[:, 2 + c % 2, j * C:(j + 1) * C], VtZ[:, u, :], Qk[:, u, :], start=j == 0, stop=False,
                             skip_group_check=True)
                    if c:
                        T.matmul(ps[:, 2 + c % 2, j * C:(j + 1) * C], SZ[:, j, :], rt_[:, j, c * C:(c + 1) * C],
                                 start=False, stop=False, skip_group_check=True)
                pe.wait_ge(sig("r_Uc"), i * NC + c + 1)
                if c < NC - 1:
                    for j in range(2):
                        m = T.matmul(ps[:, 0, j * C:(j + 1) * C], BtZ[:, j * NC + c, :], Uc[:, j, :], start=False, stop=True,
                                     skip_group_check=True)
                    m.then_inc(sig("r_dS"), 1)
                pe.wait_ge(sig("r_UZ"), i * NC + c + 1)
                for j in range(2):
                    m = T.matmul(ps[:, 2 + c % 2, j * C:(j + 1) * C], UZ[:, j, :], Qb[:, j * NC + c, :], start=False,
                                 stop=True, skip_group_check=True)
                m.then_inc(sig("r_y"), 1)
        pe.wait_ge(sig("r_y_out"), RW_T // 2 * NC + CREDIT)
        hsum(yR, ps[0:16, 4, 0:S]).then_inc(sig("y_summed"), 1)
        pe.wait_ge(sig("y_mean"), 1)
        hspread(nrm[0:16, 0, :], 4).then_inc(sig("mean_spread"), 1)
        pe.wait_ge(loraw_in, 48)
        for j in range(RW_T):
            acc = ps[:, j // 2, (j % 2) * S:(j % 2 + 1) * S]
            T.matmul(acc, g_up[:, 0, P * j:P * (j + 1)], lora[:, 1, :], start=True, stop=False)
            m = T.matmul(acc, g_up[0:32, 1, P * j:P * (j + 1)], lora[0:32, 2, :], start=False, stop=True)
        m.then_inc(sig("gate_done"), 1)
        pe.wait_ge(sig("y_sq"), 1)
        hsum(sq8, ps[0:16, 4, 0:S]).then_inc(sig("sq_summed"), 1)
        pe.wait_ge(sig("y_rstd"), 1)
        hspread(nrm[0:16, 3, :], 4).then_inc(sig("rstd_spread"), 1)

    def rec_act(act):
        with act.Fori(0, RW_T // 2) as i:
            act.wait_ge(sig("r_prep"), i + 1)
            act.wait_ge(sig("r_y"), i * NC + CREDIT)
            A.activation(rt_[:, :, :], rtn[:, :, :], ACT.Copy)
            A.activation(kkZ[HALVES[1], :, C:P], blk4(kkd[HALVES[1]]), ACT.Copy).then_inc(sig("r_kkZ_act"), 1)
            for p, r in enumerate(HALVES):
                a = A.activation(vZ[r, :, p * C:(p + 1) * C], blk4(vq[r]), ACT.Copy)
            a.then_inc(sig("r_vZ"), 1)
            act.wait_ge(sig("r_Ap"), i + 1)
            A.activation(Am[:, :, :], banks(2, 2, P), ACT.Copy).then_inc(sig("r_A"), 1)
            for n in range(len(LEVELS)):
                for g in range(2):
                    act.wait_ge(sig("r_XT"), i * 10 + 2 * n + g + 1)
                    A.activation(Zm[:, 4 * g:4 * g + 4, :], bank(6 + g, P), ACT.Copy).then_inc(sig("r_Z"), 1)
                if 1 <= n <= 3:
                    act.wait_ge(sig("r_turned"), i * 3 + n)
                    if n == 1:
                        for p, r in enumerate(HALVES):
                            A.activation(Vt[r, :, :], banks(4, 2, P)[r, :, p * C:(p + 1) * C], ACT.Copy)
                    A.activation((VtZ, KtZ, BtZ)[n - 1][:, :, :], banks(4, 2, P), ACT.Copy).then_inc(sig("r_t"), 1)
            for c in range(NC):
                act.wait_ge(sig("r_Uc"), i * NC + c + 1)
                act.wait_ge(sig("r_y"), i * NC + c + CREDIT)
                for p, r in enumerate(HALVES):
                    a = A.activation(UZ[r, :, p * C:(p + 1) * C], bank(7, C)[r, 0:2, :], ACT.Copy, scale=-1.0)
                a.then_inc(sig("r_UZ"), 1)
                act.wait_ge(sig("r_y"), i * NC + c + 1 + CREDIT)
                A.activation(yR[:, bass.ds(i * 2, 2), c * C:(c + 1) * C], bank(2 + c % 2, C)[:, 0:2, :],
                             ACT.Copy).then_inc(sig("r_y_out"), 1)
        act.wait_ge(sig("y_summed"), 1)
        A.activation(nrm[0:16, 0, :], ps[0:16, 4, 0:S], ACT.Copy, scale=1.0 / HD).then_inc(sig("y_mean"), 1)
        act.wait_ge(sig("y_var"), 1)
        A.activation(nrm[0:16, 2, :], nrm[0:16, 1, :], ACT.Sqrt).then_inc(sig("gn_root"), 1)
        act.wait_ge(sig("yR_ready"), 1)
        A.activation(x_hi[:, 0:RW_T, :], yR[:, :, :], ACT.Copy).then_inc(y_hi_ready, 1)
        A.activation(x_hi[:, RW_T:DK, :], yN[:, :, :], ACT.Copy).then_inc(y_hi_ready, 1)

    def rec_dve(dve):
        masks2 = [bc(msk(f"up{b}").unsqueeze(1), [P, 4, C]) for b in LEVELS]
        eye = bc(ident[:, :].unsqueeze(1), [P, 4, P])

        def step(i, last=False):
            two = bass.ds(i * 2, 2)
            v = rkv[:, bass.ds(i * 2 + 2 * RW_T, 2), :]
            dve.wait_ge(sig("r_prep"), i + 1)
            dve.wait_ge(sig("r_y_out"), i * NC + CREDIT)
            V.tensor_copy(Pe[:, :, :], Pn[:, :, :])
            V.tensor_copy(kkZ[HALVES[0], :, 0:C], blk4(kkd[HALVES[0]])).then_inc(sig("r_kkZ_dve"), 1)
            dve.wait_ge(sig("r_bonus"), i + 1)
            V.tensor_tensor(kkT[:, two, :], bank(7, S), v, ALU.mult).then_inc(sig("r_bonus_out"), 1)
            dve.wait_ge(sig("r_AT"), i + 1)
            V.tensor_tensor(Xm[:, :, :], banks(0, 2, P), bc(msk("neg_up1").unsqueeze(1), [P, 8, P]), ALU.mult)
            settle()
            for g in range(2):
                V.tensor_tensor(Xm[:, 4 * g:4 * g + 4, :], Xm[:, 4 * g:4 * g + 4, :], eye, ALU.add).then_inc(sig("r_x"), 1)
            if not last:
                dve.wait_ge(sig("r_scan_in"), i + 1)
                scan().then_inc(sig("r_scan"), 1)
            incl = bc(msk("incl").unsqueeze(1), [P, 8, C])
            dve.wait_ge(sig("r_Qbp"), i + 1)
            V.tensor_tensor(Qb[:, :, :], bank(6, C), incl, ALU.mult)
            dve.wait_ge(sig("r_Qkp"), i + 1)
            V.tensor_tensor(Qk[:, :, :], bank(7, C), incl, ALU.mult).then_inc(sig("r_Q"), 1)
            for n in range(len(LEVELS)):
                for g in range(2):
                    dve.wait_ge(sig("r_AX"), i * 10 + 2 * n + g + 1)
                    if n == 0 and g == 0:
                        dve.wait_ge(sig("r_Ap"), i + 1)
                    V.tensor_tensor(Ym[:, 4 * g:4 * g + 4, :], bank(g, C)[:, 0:4, :], masks2[n], ALU.mult).then_inc(sig("r_Y"), 1)
                if n == 0:
                    dve.wait_ge(sig("r_Bmp"), i + 1)
                    V.tensor_tensor(Bm[:, :, :], banks(4, 2, P), bc(msk("strict").unsqueeze(1), [P, 8, P]),
                                    ALU.mult).then_inc(sig("r_gram_out"), 1)
                for g in range(2):
                    dve.wait_ge(sig("r_XY"), i * 10 + 2 * n + g + 1)
                    x = odd(Xm[:, 4 * g:4 * g + 4, :], LEVELS[n])
                    V.tensor_tensor(x, x, bank(2 + g, C)[:, 0:4, :].rearrange("p u (q b) -> p u q b", b=LEVELS[n]),
                                    ALU.subtract).then_inc(sig("r_x"), 1)
            for c in range(NC):
                dve.wait_ge(sig("r_W"), i * NC + c + 1)
                V.tensor_copy(Wc[:, :, :], bank(6, C)[:, 0:2, :]).then_inc(sig("r_Wc"), 1)
                if 0 < c < NC - 1:
                    V.tensor_tensor(Sp[:, :, :], Sc[:, :, :], bc(Pe[:, :, c:c + 1], [P, 2, C]), ALU.mult)
                dve.wait_ge(sig("r_U"), i * NC + c + 1)
                V.tensor_scalar(Uc[:, :, :], bank(7, C)[:, 0:2, :], -1.0, None, ALU.mult).then_inc(sig("r_Uc"), 1)
                if c < NC - 1:
                    dve.wait_ge(sig("r_dS"), i * 3 + c + 1)
                    pe_ = bc(Pe[:, :, c:c + 1], [P, 2, C])
                    if c == 0:
                        V.tensor_tensor(Sc[:, :, :], bank(0, C)[:, 0:2, :], pe_, ALU.mult).then_inc(sig("r_S"), 1)
                    else:
                        for j in range(2):
                            x = V.scalar_tensor_tensor(out=Sc[:, j, :], in0=ps[:, 0, j * C:(j + 1) * C],
                                                       scalar=Pe[:, j, c:c + 1], in1=Sp[:, j, :], op0=ALU.mult, op1=ALU.add)
                        x.then_inc(sig("r_S"), 1)
                    settle()
                    dve.wait_ge(sig("r_y"), i * NC + c + 1 + CREDIT)
                    for p, rr in enumerate(HALVES):
                        x = V.tensor_copy(SZ[rr, :, p * C:(p + 1) * C], Sc[rr, :, :])
                    x.then_inc(sig("r_SZ"), 1)

        with dve.Fori(0, RW_T // 2 - 1) as i:
            step(i)
        step(RW_T // 2 - 1, last=True)
        dve.wait_ge(sig("mean_spread"), 1)
        V.tensor_tensor(yR[:, :, :], yR[:, :, :], banks(4, 4, S), ALU.subtract)
        settle()
        V.tensor_tensor(sq8[:, :, :], yR[:, :, :], yR[:, :, :], ALU.mult).then_inc(sig("y_sq"), 1)
        dve.wait_ge(sig("sq_summed"), 1)
        V.tensor_scalar(nrm[0:16, 1, :], ps[0:16, 4, 0:S], 1.0 / HD, GN_EPS, ALU.mult, ALU.add).then_inc(sig("y_var"), 1)
        dve.wait_ge(sig("gn_root"), 1)
        V.reciprocal(nrm[0:16, 3, :], nrm[0:16, 2, :]).then_inc(sig("y_rstd"), 1)
        dve.wait_ge(sig("rstd_spread"), 1)
        V.tensor_tensor(yR[:, :, :], yR[:, :, :], banks(4, 4, S), ALU.mult)
        settle()
        for j in range(RW_T):
            V.tensor_scalar(yR[:, j, :], yR[:, j, :], col("ln_w", j), col("ln_b", j), ALU.mult, ALU.add)
        settle()
        V.tensor_tensor(yR[:, :, :], yR[:, :, :], kkT[:, :, :], ALU.add)
        settle()
        dve.wait_ge(sig("gate_done"), 1)
        V.tensor_tensor(yR[:, :, :], yR[:, :, :], banks(0, 4, S), ALU.mult).then_inc(sig("yR_ready"), 1)
        for n, src in enumerate((yR, yN)):
            dve.wait_ge(y_hi_ready, n + 1)
            ks = slice(n * RW_T, (n + 1) * RW_T)
            V.tensor_tensor(x_lo[:, ks, :], src[:, :, :], x_hi[:, ks, :].bitcast(F32), ALU.subtract).then_inc(y_lo_ready, 1)

    def out_pe(pe):
        b = Y_BASE["mix"]
        pe.wait_ge(y_lo_ready, 2)
        with pe.Fori(0, 2) as i:
            chunk_products(pe, S_OUT, i, PAIR, 0, NCH, 0)
            pe.wait_ge(y_copied, i * 2 + b + CREDIT)
            chunk_products(pe, S_OUT, i, PAIR, 8, NCH, 2)
            pe.wait_ge(y_copied, i * 2 + (b + 1) + CREDIT)

    def out_act(act):
        root_tables()
        with act.Fori(0, 2) as i:
            for k in range(PAIR):
                split_hi(act, S_OUT, i, PAIR, k, SLAB)
                if k == 13:
                    square_y(act, y_b, Y_BASE["mix"], i, 0)
            square_y(act, y_b, Y_BASE["mix"], i, 1)

    def out_dve(dve):
        with dve.Fori(0, 2) as i:
            for k in range(PAIR):
                split_lo(dve, S_OUT, i, PAIR, k, SLAB)
                if k == 11:
                    used(dve, S_OUT, i, PAIR, 7)
                    copy_y(dve, y_b, i, 0)
            used(dve, S_OUT, i, PAIR, PAIR - 1)
            copy_y(dve, y_b, i, 1)
        settle()

    def pe_fn(pe):
        pe.wait_ge(mc_in, 16)
        in_pe(pe)
        pre_pe(pe)
        nsa_pe(pe)
        kk_pe(pe)
        rec_pe(pe)
        out_pe(pe)

    def act_fn(act):
        in_act(act)
        pre_act(act)
        nsa_act(act)
        kk_act(act)
        rec_act(act)
        out_act(act)

    def dve_fn(dve):
        in_dve(dve)
        pre_dve(dve)
        nsa_dve(dve)
        kk_dve(dve)
        rec_dve(dve)
        out_dve(dve)

    return {"pe": pe_fn, "act": act_fn, "dve": dve_fn, "pool": pool_fn}


def memory_attention(nc, e):
    (ps, ident, qs, mqT, mp, mpT, memKT, memV, stat, x_hi, x_lo, y_b) = (e[n] for n in (
        "ps", "ident", "qs", "mqT", "mp", "mpT", "memKT", "memV", "stat", "x_hi", "x_lo", "y_b"))
    (sig, split_hi, split_lo, slab_products, chunk_products, used, square_y, copy_y, y_copied, y_squared, Y_BASE) = (
        e[n] for n in ("sig", "split_hi", "split_lo", "slab_products", "chunk_products", "used", "square_y", "copy_y",
                       "y_copied", "y_squared", "Y_BASE"))
    V, A, T = nc.vector, nc.scalar, nc.tensor
    SCALE = float(MEM_W // MH) ** -0.5
    AHEAD = e["AHEAD"]

    def banks(n, m, w):
        return ps[:, n:n + m, :].rearrange("p a (b w) -> p (a b) w", w=w)

    def pe_fn(pe):
        chunk_products(pe, S_MQ, None, 0, 0, NCH, 0, fresh=3)
        pe.wait_ge(sig("mq_rows"), 1)
        for a in range(MH):
            for tt in range(TT):
                t = T.transpose(ps[:, 2 + a // 2, (a % 2) * S + tt * P:(a % 2) * S + (tt + 1) * P],
                                qs[:, tt, a * P:(a + 1) * P], ident[:, :])
        t.then_inc(sig("mq_turned"), 1)
        pe.wait_ge(sig("mq_T"), 1)
        for tt in range(TT):
            for a in range(MH):
                m = T.matmul(ps[:, 4 + 2 * tt + a // 2, (a % 2) * S:(a % 2 + 1) * S], mqT[:, a, tt * P:(tt + 1) * P],
                             memKT[:, a, :], start=True, stop=True)
        m.then_inc(sig("m_scores"), 1)
        pe.wait_ge(sig("m_probs"), 1)
        for a in range(MH):
            for kb in range(2):
                for tt in range(TT):
                    t = T.transpose(ps[:, a, kb * S + tt * P:kb * S + (tt + 1) * P], mp[:, tt, a, kb * P:(kb + 1) * P],
                                    ident[:, :])
        t.then_inc(sig("m_turned"), 1)
        pe.wait_ge(sig("m_pT"), 1)
        for a in range(MH):
            for kb in range(2):
                m = T.matmul(ps[:, 4 + a // 2, (a % 2) * S:(a % 2 + 1) * S], memV[:, kb, a * P:(a + 1) * P],
                             mpT[:, a, kb, :], start=kb == 0, stop=kb == 1)
        m.then_inc(sig("m_o"), 1)
        pe.wait_ge(sig("m_o_lo"), 1)
        b = Y_BASE["mem"]
        for c in range(4):
            if c >= 2:
                pe.wait_ge(y_copied, b + c - 1 + CREDIT)
            for m in range(2):
                slab_products(pe, S_MO, None, 0, 2 * c + m, x_hi, x_lo, (2 * m, 2 * m + 1), NCH, 2 * (c % 2), m == 0, m == 1)

    def act_fn(act):
        for k in range(AHEAD, 8):
            split_hi(act, S_MQ, None, 0, k, SLAB)
        used(act, S_MQ, None, 0, 7)
        for tt in range(TT):
            a = A.activation(qs[:, tt, :], ps[:, tt, :], ACT.Copy)
        a.then_inc(sig("mq_rows"), 1)
        act.wait_ge(sig("mq_turned"), 1)
        A.activation(mqT[:, :, :], banks(2, 2, S), ACT.Copy).then_inc(sig("mq_T"), 1)
        act.wait_ge(sig("m_max"), 1)
        for tt in range(TT):
            for n in range(MH):
                c = 34 + 4 * tt + n
                a = A.activation(mp[:, tt, n, :], ps[:, 4 + 2 * tt + n // 2, (n % 2) * S:(n % 2 + 1) * S], ACT.Exp,
                                 scale=SCALE, bias=stat[:, c:c + 1], accum_out=stat[:, c + 8:c + 9])
        a.then_inc(sig("m_exp"), 1)
        act.wait_ge(sig("m_turned"), 1)
        A.activation(mpT[:, :, :, :].rearrange("p a k t -> p (a k) t"), banks(0, 4, S), ACT.Copy).then_inc(sig("m_pT"), 1)
        act.wait_ge(sig("m_o"), 1)
        A.activation(x_hi[:, 0:MH, :], banks(4, 2, S), ACT.Copy).then_inc(sig("m_o_hi"), 1)
        e["root_tables"]()
        for k in range(8):
            split_hi(act, S_MO, None, 0, k, SLAB)
        for c in range(4):
            square_y(act, y_b, Y_BASE["mem"], None, c)

    def dve_fn(dve):
        for k in range(AHEAD, 8):
            split_lo(dve, S_MQ, None, 0, k, SLAB)
        dve.wait_ge(sig("m_scores"), 1)
        V.tensor_reduce(stat[:, 50:58], banks(4, 4, S), AX.X, ALU.max)
        V.drain()
        V.tensor_scalar(stat[:, 34:42], stat[:, 50:58], -SCALE, None, ALU.mult).then_inc(sig("m_max"), 1)
        dve.wait_ge(sig("m_exp"), 1)
        V.reciprocal(stat[:, 50:58], stat[:, 42:50])
        V.drain()
        v = mp[:, :, :, :].rearrange("p t a n -> p (t a) n")
        V.tensor_tensor(v, v, bc(stat[:, 50:58].unsqueeze(2), [P, 8, S]), ALU.mult).then_inc(sig("m_probs"), 1)
        dve.wait_ge(sig("m_o_hi"), 1)
        V.tensor_tensor(x_lo[:, 0:MH, :], banks(4, 2, S), x_hi[:, 0:MH, :].bitcast(F32),
                        ALU.subtract).then_inc(sig("m_o_lo"), 1)
        for k in range(8):
            split_lo(dve, S_MO, None, 0, k, SLAB)
            if k in (5, 7):
                c = (k - 5) // 2
                used(dve, S_MO, None, 0, 2 * c + 1)
                copy_y(dve, y_b, None, c)
        for c in (2, 3):
            used(dve, S_MO, None, 0, 2 * c + 1)
            for tt in range(TT):
                x = V.tensor_copy(y_b[:, tt, c * NCH:(c + 1) * NCH], ps[:, 2 * (c % 2) + tt, :])
            x.then_inc(y_copied, 1)
        V.drain()

    return {"pe": pe_fn, "act": act_fn, "dve": dve_fn}



def build(nc, A, out):
    with ExitStack() as ctx:
        base = (nc.sbuf_base + 63) // 64 * 64
        end = nc.sbuf_usable_end
        ctx.enter_context(nc.sbuf_tensor("arena", [P, (end - base - 64) // 4], F32))

        def at(name, shape, offset, dt=F32):
            size = 4 * int(np.prod(shape[1:]))
            assert base + offset + size <= end, (name, base + offset + size, end)
            return nc.alloc_sbuf_tensor_at(name, shape, dt, offset=base + offset)

        o = 0

        def keep(name, shape, dt=F32):
            nonlocal o
            t = at(name, shape, o, dt)
            o += (4 * int(np.prod(shape[1:])) + 31) // 32 * 32
            return t

        raw = keep("raw", [P, RING, SLAB])
        w_hi = keep("w_hi", [P, RING, SLAB], F32R)
        w_lo = keep("w_lo", [P, RING, SLAB], F32R)
        h = keep("h", [P, TT, D])
        memKT = keep("memKT", [P, MH, S])
        memV = keep("memV", [P, TT, MEM_W])
        ident = keep("ident", [P, P])
        cols = keep("cols", [P, NCOLS])
        stat = keep("stat", [P, 64])
        x_hi = keep("x_hi", [P, DK, S], F32R)
        x_lo = keep("x_lo", [P, DK, S], F32R)
        XT = o - 2 * 4 * DK * S
        BIG = o

        hT_hi = at("hT_hi", [P, FK, S], BIG, F32R)
        hT_lo = at("hT_lo", [P, FK, S], BIG + 44032, F32R)
        sg = at("sg", [P, TT, NCH], BIG + 88064)
        prod = at("prod", [P, TT, NCH], BIG + 92160)
        gain = at("gain", [P, D], BIG + 88064)
        y_x = at("y_x", [P, TT, D], XT)
        y_b = at("y_b", [P, TT, D], BIG)
        y_last = at("y_last", [P, TT, NCH], BIG + 96256)
        xn = at("xn", [P, TT, D], BIG + 46592)
        mem_sb = at("mem_sb", [P, TT, D], BIG + 62976)
        k_rows = at("k_rows", [P, TT, MEM_W], BIG)

        W0 = 4 * RING * SLAB
        mc = at("mc", [P, NMC], BIG)
        R0 = BIG + 13824
        assert 4 * NMC <= 13824
        rkv = at("rkv", [P, 3 * RW_T, S], R0)
        yN = at("yN", [P, RW_T, S], R0 + 24576)
        lora = at("lora", [P, 3, S], R0 + 32768)
        F0 = R0 + 35840
        nf = at("nf", [P, TT, NSA_W], F0)
        T0 = F0 + 20864
        shb = at("shb", [P, 4, S + 1], T0)
        dif = at("dif", [P, 4, S], T0 + 4128)
        fst = at("fst", [P, TT, NCH], T0 + 8224)
        w1 = at("w1", [P, 2, 16, P], T0 + 12320)
        w2 = at("w2", [P, 3, HD], T0 + 28704)
        vblk = at("vblk", [P, G, 4, HD], XT + 28672)
        kdup = at("kdup", [P, 2, TT, G, 2, HD], R0 + 24576)
        kc2 = at("kc2", [P, 2, G + 1, S], W0 + 5632)
        hid = at("hid", [P, 8, 64], XT + 12288)
        hidrep = at("hidrep", [P, G, 4, 32], XT + 14336)
        qn = at("qn", [P, TT, 4, HD], XT)
        qr = at("qr", [P, TT, 4, HD], XT + 2048)
        kk2 = at("kk2", [P, 2, TT, 2, HD], XT + 4096)
        vv = at("vv", [P, 2, TT, HD], XT + 6144)
        qnT = at("qnT", [P, 2, S], XT + 7168)
        qrT = at("qrT", [P, 2, S], XT + 9216)
        kT = at("kT", [P, 2, S], XT + 11264)
        p0 = at("p0", [P, 2, 4, P], XT + 13312)
        p1 = at("p1", [P, 2, 4, S], XT + 17408)
        pc = at("pc", [P, TT, 4, 32], XT + 25600)
        pcT = at("pcT", [P, S], XT + 26624)
        vbg = at("vbg", [P, 4, HD], XT + 27648)
        pT0 = at("pT0", [P, 2, 4, S], T0)
        pT1 = at("pT1", [P, 2, 4, P], T0 + 8192)
        kcT = at("kcT", [P, G, 16], W0 + 5120)
        kcg = at("kcg", [P, 16], W0 + 5376)
        hb = at("hb", [P, 2], W0 + 5440)
        qrot = at("qrot", [P, TT, 16, 16], W0)
        rt = at("rt", [P, 4, 16, ROPE_H], W0 + 2048)
        gates = at("gates", [P, TT, 48], W0 + 4096)
        gg = at("gg", [P, TT, 3, 4], W0 + 4480)
        sm = at("sm", [P, 2, 4, 8], W0 + 4608)
        smc = at("smc", [P, 4, 8], W0 + 4864)

        kkT = at("kkT", [P, RW_T, S], T0 + 12320)
        aT = at("aT", [P, RW_T, S], 8 * RING * SLAB)
        wT = at("wT", [P, RW_T, S], 8 * RING * SLAB + 8192)
        yR = at("yR", [P, RW_T, S], F0)
        g_up = at("g_up", [P, 2, RW_W], F0 + 8192)
        L0 = T0 + 20512
        wa_up = at("wa_up", [P, RW_W], T0 + 29472)
        Am = at("Am", [P, 8, P], W0)
        Zm = at("Zm", [P, 8, P], W0 + 4096)
        Ym = at("Ym", [P, 8, C], W0 + 8192)
        vq = at("vq", [P, 2, S], W0 + 10240)
        bon = at("bon", [P, 2, S], W0 + 12288)
        Sp = at("Sp", [P, 2, C], W0 + 14336)
        sq8 = at("sq8", [P, RW_T, S], W0 + 8192)
        nrm = at("nrm", [16, 4, S], W0 + 4096)
        bZ = at("bZ", [P, 8, P], XT)
        kZ = at("kZ", [P, 8, P], XT + 4096)
        vZ = at("vZ", [P, 8, P], XT + 8192)
        kkZ = at("kkZ", [P, 8, P], XT + 12288)
        VtZ = at("VtZ", [P, 8, P], XT + 16384)
        KtZ = at("KtZ", [P, 8, P], XT + 20480)
        BtZ = at("BtZ", [P, 8, P], XT + 24576)
        Xm = at("Xm", [P, 8, P], XT + 28672)
        Pd = at("Pd", [P, 2, S], F0 + 18944)
        iP = at("iP", [P, 2, S], F0 + 20992)
        Bm = at("Bm", [P, 8, P], L0)
        kp = at("kp", [P, 2, S], F0 + 23040)
        tmp = at("tmp", [P, 2, S], F0 + 25088)
        rtn = at("rtn", [P, 2, S], F0 + 27136)
        kkd = at("kkd", [P, 2, S], F0 + 29184)
        Pn = at("Pn", [P, 2, NC], F0 + 31232)
        rt_ = at("rt_", [P, 2, S], L0 + 4096)
        Vt = at("Vt", [P, 8, C], L0 + 6144)
        Qb = at("Qb", [P, 8, C], L0 + 8192)
        Qk = at("Qk", [P, 8, C], L0 + 10240)
        UZ = at("UZ", [P, 2, P], L0 + 12288)
        Pe = at("Pe", [P, 2, NC], L0 + 13312)
        Sc = at("Sc", [P, 2, C], F0 + 16384)
        SZ = at("SZ", [P, 2, P], F0 + 16896)
        Wc = at("Wc", [P, 2, C], F0 + 17920)
        Uc = at("Uc", [P, 2, C], F0 + 18432)

        qs = at("qs", [P, TT, MEM_W], BIG)
        mqT = at("mqT", [P, MH, S], BIG + 4096)
        mp = at("mp", [P, TT, MH, S], BIG + 8192)
        mpT = at("mpT", [P, MH, 2, S], BIG + 16384)

        ps = ctx.enter_context(nc.psum_tensor("ps", [P, 8, NCH], F32))

        def sem(name):
            return ctx.enter_context(nc.semaphore(name))

        slab_in = [sem(f"slab_in{n}") for n in range(RING)]
        hi_ready = sem("hi_ready")
        lo_ready = sem("lo_ready")
        slab_used = sem("slab_used")
        x_in, mem_in = sem("x_in"), [sem(f"mem_in{k}") for k in range(4)]
        ident_in, cols_in = sem("ident_in"), sem("cols_in")
        mc_in, w1_in, loraw_in, gain_in = sem("mc_in"), sem("w1_in"), sem("loraw_in"), sem("gain_in")
        out_done = sem("out_done")
        sq_ready = sem("sq_ready")
        ms_ready = sem("ms_ready")
        root_ready = sem("root_ready")
        xn_ready = sem("xn_ready")
        x_turned = sem("x_turned")
        x_hi_ready, x_lo_ready = sem("x_hi_ready"), sem("x_lo_ready")
        kv_rows = sem("kv_rows")
        k_turned = sem("k_turned")
        mem_kv_ready = sem("mem_kv_ready")
        gate_ready = sem("gate_ready")
        prod_ready = sem("prod_ready")
        prod_turned = sem("prod_turned")
        hT_hi_ready, hT_lo_ready = sem("hT_hi_ready"), sem("hT_lo_ready")
        y_squared, y_copied = sem("y_squared"), sem("y_copied")
        h_ready = sem("h_ready")
        feat_rows = sem("feat_rows")
        feat_turned = sem("feat_turned")
        feat_T = sem("feat_T")
        shifted = sem("shifted")
        y_hi_ready, y_lo_ready = sem("y_hi_ready"), sem("y_lo_ready")

        made = {}

        def sig(name):
            if name not in made:
                made[name] = sem(name)
            return made[name]

        def col(name, n=0, w=1):
            return cols[:, COLS[name] + n:COLS[name] + n + w]

        def msk(name):
            a, n = MC[name]
            return mc[:, a:a + n]

        def load_slab(sp, s0, reg, step, k, src, width):
            s = s0 + k
            shift = 0 if reg is None else reg * step
            if reg is not None or s >= RING:
                sp.wait_ge(lo_ready, shift + (s - RING + 1))
            sp.dma_start(raw[:, s % RING, 0:width], src).then_inc(slab_in[s % RING], 16)

        def split_hi(act, s0, reg, step, k, width):
            s = s0 + k
            act.wait_ge(slab_in[s % RING],
                        16 * (s // RING + 1) + (0 if reg is None else reg * (16 * step // RING)))
            if reg is not None or s >= RING:
                act.wait_ge(slab_used, (0 if reg is None else reg * step) + (s - RING + 1))
            nc.scalar.activation(w_hi[:, s % RING, 0:width], raw[:, s % RING, 0:width], ACT.Copy).then_inc(hi_ready, 1)

        def split_lo(dve, s0, reg, step, k, width):
            s = s0 + k
            dve.wait_ge(hi_ready, (0 if reg is None else reg * step) + s + 1)
            nc.vector.tensor_tensor(w_lo[:, s % RING, 0:width], raw[:, s % RING, 0:width],
                                    w_hi[:, s % RING, 0:width].bitcast(F32), ALU.subtract).then_inc(lo_ready, 1)

        def slab_products(pe, s0, reg, step, k, hi, lo, kts, width, bank, first, last, fresh=None):
            s = s0 + k
            if fresh is not None:
                pe.wait_ge(x_lo_ready, DK * fresh + kts[-1] + 1)
            pe.wait_ge(lo_ready, (0 if reg is None else reg * step) + s + 1)
            for n, kt in enumerate(kts):
                wh = w_hi[:, s % RING, n * width:(n + 1) * width]
                wl = w_lo[:, s % RING, n * width:(n + 1) * width]
                for tt in range(TT):
                    acc = ps[:, bank + tt, 0:width]
                    xh = hi[:, kt, tt * P:(tt + 1) * P]
                    begin, finish = first and n == 0, last and n == len(kts) - 1
                    nc.tensor.matmul(acc, xh, wh, start=begin, stop=False)
                    nc.tensor.matmul(acc, xh, wl, start=False, stop=False)
                    mm = nc.tensor.matmul(acc, lo[:, kt, tt * P:(tt + 1) * P], wh, start=False, stop=finish)
            mm.then_inc(slab_used, 1)

        def used(eng, s0, reg, step, k):
            eng.wait_ge(slab_used, (0 if reg is None else reg * step) + s0 + k + 1)

        def chunk_products(pe, s0, reg, step, k0, width, bank, fresh=None):
            for m in range(DK // 2):
                slab_products(pe, s0, reg, step, k0 + m, x_hi, x_lo, (2 * m, 2 * m + 1), width, bank,
                              m == 0, m == DK // 2 - 1, fresh)

        HALF = [(tt, f) for tt in range(TT) for f in range(2)]
        N_BANKS = (4, 5, 6, 7, 2, 3)

        AHEAD = RING

        def norm_sums_act(act, n, src, half_ready):
            for k, (tt, f) in enumerate(HALF):
                half_ready(k)
                cs = slice(f * (D // 2), (f + 1) * (D // 2))
                nc.scalar.activation(xn[:, tt, cs], src[:, tt, cs], ACT.Square,
                                     accum_out=stat[:, k:k + 1]).then_inc(sq_ready, 1)
            act.wait_ge(ms_ready, n + 1)
            nc.scalar.activation(stat[:, 8:10], stat[:, 4:6], ACT.Sqrt).then_inc(root_ready, 1)

        def norm_turn_act(act, n, gname, s0, done=0):
            for b in range(DK // 2):
                if b in (3, 4, 5, 6) and b - 3 >= done:
                    split_hi(act, s0, None, 0, b - 3, SLAB)
                act.wait_ge(x_turned, 8 * n + b + 1)
                for m in range(2):
                    kt = 2 * b + m
                    nc.scalar.activation(x_hi[:, kt, :], ps[:, N_BANKS[b % 6], m * S:(m + 1) * S], ACT.Copy,
                                         scale=col(gname, kt)).then_inc(x_hi_ready, 1)

        def norm_rows_dve(dve, n, src):
            dve.wait_ge(sq_ready, 4 * (n + 1))
            nc.vector.tensor_reduce(stat[:, 10:12], stat[:, 0:4].rearrange("p (t f) -> p t f", f=2), AX.X, ALU.add)
            nc.vector.drain()
            nc.vector.tensor_scalar(stat[:, 4:6], stat[:, 10:12], 1.0 / D, EPS, ALU.mult, ALU.add).then_inc(ms_ready, 1)
            dve.wait_ge(root_ready, n + 1)
            nc.vector.reciprocal(stat[:, 6:8], stat[:, 8:10])
            nc.vector.drain()
            for q in range(4):
                for tt in range(TT):
                    cs = slice(q * (D // 4), (q + 1) * (D // 4))
                    nc.vector.tensor_scalar(xn[:, tt, cs], src[:, tt, cs], stat[:, 6 + tt:7 + tt], None,
                                            ALU.mult).then_inc(xn_ready, 1)

        def norm_turn_dve(dve, n, gname, s0):
            for kt in range(DK):
                if kt >= 2 and kt % 4 == 2:
                    split_lo(dve, s0, None, 0, kt // 4, SLAB)
                dve.wait_ge(x_hi_ready, DK * n + 2 * (kt // 2) + 2)
                b = N_BANKS[kt // 2 % 6]
                nc.vector.scalar_tensor_tensor(out=x_lo[:, kt, :], in0=ps[:, b, (kt % 2) * S:(kt % 2 + 1) * S],
                                               scalar=col(gname, kt), in1=x_hi[:, kt, :].bitcast(F32),
                                               op0=ALU.mult, op1=ALU.subtract).then_inc(x_lo_ready, 1)

        def norm_pe(pe, n):
            for b in range(DK // 2):
                if b >= 6:
                    pe.wait_ge(x_lo_ready, DK * n + 2 * (b - 5))
                for m in range(2):
                    for tt in range(TT):
                        pe.wait_ge(xn_ready, 8 * n + 2 * (b // 2) + tt + 1)
                        t = nc.tensor.transpose(ps[:, N_BANKS[b % 6], m * S + tt * P:m * S + (tt + 1) * P],
                                                xn[:, tt, (2 * b + m) * P:(2 * b + m + 1) * P], ident[:, :])
                t.then_inc(x_turned, 1)

        def square_y(act, y, base, reg, k):
            nc.scalar.drain()
            act.wait_ge(y_copied, (0 if reg is None else 2 * reg) + base + k + 1 + CREDIT)
            for tt in range(TT):
                idx = stat[:, bass.ds(16 + (0 if reg is None else 4 * reg) + 2 * k + tt, 1)]
                c0 = (0 if reg is None else reg * (2 * NCH)) + k * NCH
                a = nc.scalar.activation(ps[:, 6 + tt, :], y[:, tt, bass.ds(c0, NCH)], ACT.Square, accum_out=idx)
            a.then_inc(y_squared, 1)

        def copy_y(dve, y, reg, k):
            for tt in range(TT):
                c0 = (0 if reg is None else reg * (2 * NCH)) + k * NCH
                v = nc.vector.tensor_copy(y[:, tt, bass.ds(c0, NCH)], ps[:, 2 * (k % 2) + tt, :])
            v.then_inc(y_copied, 1)

        def scale_y(pool, m, y):
            pool.wait_ge(gain_in, 16 * (m + 1))
            for k in range(3):
                pool.wait_ge(y_squared, 4 * m + k + 1)
                for tt in range(TT):
                    c = slice(k * NCH, (k + 1) * NCH)
                    x = nc.gpsimd.tensor_tensor(y[:, tt, c], y[:, tt, c], gain[:, c], ALU.mult)
                x.then_inc(y_scaled, 1)

        def post_norm_dve(dve, m, y, half):
            dve.wait_ge(gain_in, 16 * (m + 1))
            for tt in range(TT):
                nc.vector.tensor_tensor(y_last[:, tt, :], y[:, tt, 3 * NCH:], gain[:, 3 * NCH:], ALU.mult)
            dve.wait_ge(y_squared, 4 * (m + 1))
            nc.vector.tensor_reduce(stat[:, 24:26], stat[:, 16:24].rearrange("p (n t) -> p t n", t=TT), AX.X, ALU.add)
            nc.vector.drain()
            nc.vector.tensor_scalar(stat[:, 26:28], stat[:, 24:26], 1.0 / D, EPS, ALU.mult, ALU.add).then_inc(y_ms, 1)
            dve.wait_ge(y_root, m + 1)
            nc.vector.reciprocal(stat[:, 30:32], stat[:, 28:30])
            nc.vector.drain()
            nc.vector.tensor_scalar(stat[:, 32:34], stat[:, 30:32], half, None, ALU.mult)
            nc.vector.drain()
            dve.wait_ge(y_scaled, 3 * (m + 1))
            for tt in range(TT):
                r = stat[:, 32 + tt:33 + tt]
                for src, c in ((y[:, tt, 0:2 * NCH], slice(0, 2 * NCH)), (y[:, tt, 2 * NCH:3 * NCH], slice(2 * NCH, 3 * NCH)),
                               (y_last[:, tt, :], slice(3 * NCH, 4 * NCH))):
                    v = nc.vector.scalar_tensor_tensor(out=h[:, tt, c], in0=src, scalar=r, in1=h[:, tt, c],
                                                       op0=ALU.mult, op1=ALU.add)
                    if c.start != 2 * NCH:
                        v.then_inc(h_ready, 1)
            nc.vector.drain()

        def root_tables():
            nc.scalar.activation(stat[:, 60:61], cols[:, 0:1], ACT.Square)
            nc.scalar.drain()
            nc.scalar.activation(stat[:, 61:62], stat[:, 60:61], ACT.Sqrt)

        def post_norm_act(act, m):
            act.wait_ge(y_ms, m + 1)
            nc.scalar.activation(stat[:, 28:30], stat[:, 26:28], ACT.Sqrt).then_inc(y_root, 1)

        def from_residual(act, m):
            return lambda k: act.wait_ge(h_ready, 4 * m + k + 1)

        y_ms, y_root, y_scaled = sem("y_ms"), sem("y_root"), sem("y_scaled")

        FFN_NORM = (1, 4)

        def ffn_pair_pe(pe, f, s0, i, reg, width):
            b = FFN_PAIRS * f
            n = reg if reg is not None else i
            for k in range(PAIR // 2):
                if k == 0 and (reg is not None or i > 0):
                    pe.wait_ge(gate_ready, n + b)
                slab_products(pe, s0, reg, PAIR, k, x_hi, x_lo, (2 * k, 2 * k + 1), width, 0, k == 0, k == 7,
                              fresh=FFN_NORM[f] if reg is None and n == 0 else None)
                if k == 4 and (reg is not None or i > 0):
                    turn_prod(pe, f, n, NCH // P)
            if reg is not None or i > 0:
                pe.wait_ge(prod_ready, n + b)
            for k in range(PAIR // 2):
                slab_products(pe, s0, reg, PAIR, 8 + k, x_hi, x_lo, (2 * k, 2 * k + 1), width, 2, k == 0, k == 7)

        def turn_prod(pe, f, n, blocks):
            b = FFN_PAIRS * f
            pe.wait_ge(prod_ready, n + b)
            pe.wait_ge(hT_lo_ready, n + (b - 1) + CREDIT)
            for tt in range(TT):
                for m in range(blocks):
                    t = nc.tensor.transpose(ps[:, 4 + tt, m * P:(m + 1) * P], prod[:, tt, m * P:(m + 1) * P], ident[:, :])
            t.then_inc(prod_turned, 1)

        def ffn_pair_act(act, f, s0, i, reg, width):
            n = reg if reg is not None else i
            for k in range(AHEAD if i == 0 else 0, PAIR):
                split_hi(act, s0, reg, PAIR, k, 2 * width)
                if k == 8 and (reg is not None or i > 0):
                    hT_hi_evict(act, f, n, NCH // P)
                if k == 11:
                    gate_act(act, f, s0, i, reg, width)

        def hT_hi_evict(act, f, n, blocks):
            act.wait_ge(prod_turned, n + FFN_PAIRS * f + CREDIT)
            for tt in range(TT):
                a = nc.scalar.activation(hT_hi[:, bass.ds((n - 1) * 4, blocks), tt * P:(tt + 1) * P],
                                         ps[:, 4 + tt, 0:blocks * P].rearrange("p (m t) -> p m t", t=P), ACT.Copy)
            a.then_inc(hT_hi_ready, 1)

        def gate_act(act, f, s0, i, reg, width):
            n = reg if reg is not None else i
            used(act, s0, reg, PAIR, 7)
            if reg is not None or i > 0:
                act.wait_ge(prod_ready, n + FFN_PAIRS * f)
            for tt in range(TT):
                a = nc.scalar.activation(sg[:, tt, 0:width], ps[:, tt, 0:width], ACT.Silu)
            a.then_inc(gate_ready, 1)

        def ffn_pair_dve(dve, f, s0, i, reg, width):
            n = reg if reg is not None else i
            for k in range(AHEAD if i == 0 else 0, PAIR):
                split_lo(dve, s0, reg, PAIR, k, 2 * width)
                if k == 3 and (reg is not None or i > 0):
                    make_prod(dve, f, s0, n, reg, -1, NCH)
                if k == 8 and (reg is not None or i > 0):
                    hT_lo_evict(dve, f, n, NCH // P)

        def make_prod(dve, f, s0, n, reg, last_slab, width):
            b = FFN_PAIRS * f
            dve.wait_ge(gate_ready, n + b)
            used(dve, s0, reg, PAIR, last_slab)
            dve.wait_ge(prod_turned, n + (b - 1) + CREDIT)
            for tt in range(TT):
                v = nc.vector.tensor_tensor(prod[:, tt, 0:width], ps[:, 2 + tt, 0:width], sg[:, tt, 0:width], ALU.mult)
            v.then_inc(prod_ready, 1)

        def hT_lo_evict(dve, f, n, blocks):
            dve.wait_ge(hT_hi_ready, n + FFN_PAIRS * f)
            for tt in range(TT):
                kt = bass.ds((n - 1) * 4, blocks)
                v = nc.vector.tensor_tensor(hT_lo[:, kt, tt * P:(tt + 1) * P],
                                            ps[:, 4 + tt, 0:blocks * P].rearrange("p (m t) -> p m t", t=P),
                                            hT_hi[:, kt, tt * P:(tt + 1) * P].bitcast(F32), ALU.subtract)
            v.then_inc(hT_lo_ready, 1)

        def pair_base(s0, i):
            return s0 + PAIR * i

        LASTP = FFN_PAIRS - 1

        def down_width(k):
            return (NCH if k % DOWN == DOWN - 1 else 2 * NCH)

        def ffn_sp(sp, s0, gu, gu_t, dn):
            for k in range(PAIR):
                load_slab(sp, s0, None, 0, k, gu[0, k], SLAB)
            with sp.Fori(1, LASTP) as i:
                for k in range(PAIR):
                    load_slab(sp, s0, i, PAIR, k, gu[bass.ds(i, 1), k].rearrange("a p w -> (a p) w"), SLAB)
            for k in range(PAIR):
                load_slab(sp, pair_base(s0, LASTP), None, 0, k, gu_t[k], 2 * TAIL_F)
            s1 = pair_base(s0, FFN_PAIRS)
            with sp.Fori(0, 2) as i:
                for k in range(2 * DOWN):
                    w = down_width(k)
                    load_slab(sp, s1, i, 2 * DOWN, k, dn[bass.ds(i, 1), k].rearrange("a p w -> (a p) w")[:, 0:w], w)

        def ffn_pe(pe, f, s0):
            ffn_pair_pe(pe, f, s0, 0, None, NCH)
            with pe.Fori(1, LASTP) as i:
                ffn_pair_pe(pe, f, s0, None, i, NCH)
            ffn_pair_pe(pe, f, pair_base(s0, LASTP), LASTP, None, TAIL_F)
            turn_prod(pe, f, FFN_PAIRS, TAIL_F // P)
            s1 = pair_base(s0, FFN_PAIRS)
            b = Y_BASE[f]
            pe.wait_ge(hT_lo_ready, FFN_PAIRS * (f + 1) + CREDIT)
            with pe.Fori(0, 2) as i:
                for c in range(2):
                    if c == 1:
                        pe.wait_ge(y_copied, i * 2 + b + CREDIT)
                    for m in range(DOWN):
                        kts = tuple(k for k in (2 * m, 2 * m + 1) if k < FK)
                        slab_products(pe, s1, i, 2 * DOWN, c * DOWN + m, hT_hi, hT_lo, kts, NCH, 2 * c,
                                      m == 0, m == DOWN - 1)
                pe.wait_ge(y_copied, i * 2 + (b + 1) + CREDIT)

        def ffn_act(act, f, s0):
            ffn_pair_act(act, f, s0, 0, None, NCH)
            with act.Fori(1, LASTP) as i:
                ffn_pair_act(act, f, s0, None, i, NCH)
            ffn_pair_act(act, f, pair_base(s0, LASTP), LASTP, None, TAIL_F)
            s1 = pair_base(s0, FFN_PAIRS)
            hT_hi_evict(act, f, FFN_PAIRS, TAIL_F // P)
            root_tables()
            with act.Fori(0, 2) as i:
                for k in range(2 * DOWN):
                    split_hi(act, s1, i, 2 * DOWN, k, down_width(k))
                    if k == DOWN + 5:
                        square_y(act, y_x, Y_BASE[f], i, 0)
                square_y(act, y_x, Y_BASE[f], i, 1)

        def ffn_dve(dve, f, s0):
            ffn_pair_dve(dve, f, s0, 0, None, NCH)
            with dve.Fori(1, LASTP) as i:
                ffn_pair_dve(dve, f, s0, None, i, NCH)
            ffn_pair_dve(dve, f, pair_base(s0, LASTP), LASTP, None, TAIL_F)
            make_prod(dve, f, pair_base(s0, LASTP), FFN_PAIRS, None, PAIR - 1, TAIL_F)
            hT_lo_evict(dve, f, FFN_PAIRS, TAIL_F // P)
            s1 = pair_base(s0, FFN_PAIRS)
            with dve.Fori(0, 2) as i:
                for k in range(2 * DOWN):
                    split_lo(dve, s1, i, 2 * DOWN, k, down_width(k))
                    if k == DOWN + 3:
                        used(dve, s1, i, 2 * DOWN, DOWN - 1)
                        copy_y(dve, y_x, i, 0)
                used(dve, s1, i, 2 * DOWN, 2 * DOWN - 1)
                copy_y(dve, y_x, i, 1)
            nc.vector.drain()

        Y_BASE = {0: 0, "mix": 4, "mem": 8, 1: 12}

        drams_of = A.get
        env = dict(locals())
        mix = mixing(nc, env)
        mat = memory_attention(nc, env)

        block = ctx.enter_context(nc.Block())
        drams = A

        @block.sync
        def _(sp):
            sp.dma_start(cols[:, :], drams["cols"]).then_inc(cols_in, 16)
            sp.dma_start(ident[:, :], drams["ident"]).then_inc(ident_in, 16)
            for k, (tt, f) in enumerate(HALF):
                cs = slice(f * (D // 2), (f + 1) * (D // 2))
                sp.dma_start(mem_sb[:, tt, cs], drams["mem"][0, tt * P:(tt + 1) * P, cs]).then_inc(mem_in[k], 16)
            for k in range(PAIR):
                load_slab(sp, S_KV, None, 0, k, drams["w_kv"][k], SLAB)
            ffn_sp(sp, S_GU1, drams["gu1"], drams["gu1_t"], drams["dn1"])
            with sp.Fori(0, 5) as i:
                for k in range(PAIR):
                    load_slab(sp, S_IN, i, PAIR, k, drams["w_in"][bass.ds(i, 1), k].rearrange("a p w -> (a p) w"), SLAB)
            for k in range(PAIR // 2):
                load_slab(sp, S_IN + 5 * PAIR, None, 0, k, drams["w_in5"][k], SLAB)
            for k in range(PAIR // 2):
                load_slab(sp, S_IN + 5 * PAIR, None, 0, 8 + k, drams["w_in_t"][k], 2 * TAIL_IN)
            with sp.Fori(0, 2) as i:
                for k in range(PAIR):
                    load_slab(sp, S_OUT, i, PAIR, k, drams["w_out"][bass.ds(i, 1), k].rearrange("a p w -> (a p) w"), SLAB)
            for k in range(8):
                load_slab(sp, S_MQ, None, 0, k, drams["w_mq"][k], SLAB)
            for k in range(8):
                load_slab(sp, S_MO, None, 0, k, drams["w_mo"][k], SLAB)
            ffn_sp(sp, S_GU2, drams["gu2"], drams["gu2_t"], drams["dn2"])
            for k, (tt, f) in enumerate(HALF):
                cs = slice(f * (D // 2), (f + 1) * (D // 2))
                sp.wait_ge(h_ready, 4 * 3 + k + 1)
                sp.dma_start(out[0, tt * P:(tt + 1) * P, cs], h[:, tt, cs]).then_inc(out_done, 16)
            sp.wait_ge(out_done, 16 * len(HALF))

        @block.gpsimd
        def _(pool):
            pool.wait_ge(mem_in[3], 16)
            pool.dma_start(h[:, :, :], drams["x"].rearrange("a (t p) d -> p (a t) d", p=P)).then_inc(x_in, 16)
            pool.wait_ge(hT_hi_ready, FFN_PAIRS)
            pool.wait_ge(hT_lo_ready, FFN_PAIRS + CREDIT)
            pool.dma_start(gain[:, :], drams["post1"].partition_broadcast(P)).then_inc(gain_in, 16)
            scale_y(pool, 0, y_x)
            pool.wait_ge(slab_used, S_IN)
            pool.wait_ge(h_ready, 4)
            pool.dma_start(mc[:, :], drams["mc"]).then_inc(mc_in, 16)
            pool.dma_start(w1[:, 0], drams["w1_k"]).then_inc(w1_in, 16)
            pool.dma_start(w1[:, 1], drams["w1_v"]).then_inc(w1_in, 16)
            pool.dma_start(w2[:, 0, :], drams["w2_k"]).then_inc(w1_in, 16)
            pool.dma_start(w2[:, 1, :], drams["w2_k"]).then_inc(w1_in, 16)
            pool.dma_start(w2[:, 2, :], drams["w2_v"]).then_inc(w1_in, 16)
            mix["pool"](pool)
            pool.dma_start(gain[:, :], drams["post2"].partition_broadcast(P)).then_inc(gain_in, 16)
            scale_y(pool, 1, y_b)
            pool.wait_ge(h_ready, 2 * 4)
            pool.dma_start(gain[:, :], drams["post3"].partition_broadcast(P)).then_inc(gain_in, 16)
            scale_y(pool, 2, y_b)
            pool.wait_ge(hT_hi_ready, 2 * FFN_PAIRS)
            pool.wait_ge(hT_lo_ready, 2 * FFN_PAIRS + CREDIT)
            pool.dma_start(gain[:, :], drams["post4"].partition_broadcast(P)).then_inc(gain_in, 16)
            scale_y(pool, 3, y_x)

        @block.scalar
        def _(act):
            for name in ("feat_rows", "feat_T"):
                act.sem_inc(env[name], CREDIT)
            for name in ("g_o_out", "r_y_out"):
                act.sem_inc(sig(name), CREDIT)
            act.wait_ge(cols_in, 16)
            root_tables()
            norm_sums_act(act, 0, mem_sb, lambda k: act.wait_ge(mem_in[k], 16))
            norm_turn_act(act, 0, "mem", S_KV)
            for k in range(AHEAD, PAIR):
                split_hi(act, S_KV, None, 0, k, SLAB)
                if k == 9:
                    act.wait_ge(x_in, 16)
                    act.wait_ge(x_turned, 8)
                    norm_sums_act(act, 1, h, lambda k: None)
                if k == 11:
                    used(act, S_KV, None, 0, 7)
                    for tt in range(TT):
                        a = nc.scalar.activation(k_rows[:, tt, :], ps[:, tt, :], ACT.Copy)
                    a.then_inc(kv_rows, 1)
            used(act, S_KV, None, 0, PAIR - 1)
            for tt in range(TT):
                a = nc.scalar.activation(memV[:, tt, :], ps[:, 2 + tt, :], ACT.Copy)
            a.then_inc(kv_rows, 1)
            act.wait_ge(k_turned, 1)
            for b in range(2):
                a = nc.scalar.activation(memKT[:, 2 * b:2 * b + 2, :], ps[:, 4 + b, :].rearrange("p (m t) -> p m t", t=S), ACT.Copy)
            a.then_inc(mem_kv_ready, 1)
            norm_turn_act(act, 1, "ffn1", S_GU1)
            ffn_act(act, 0, S_GU1)
            post_norm_act(act, 0)
            for k in range(2):
                split_hi(act, S_IN, None, 0, k, SLAB)
            norm_sums_act(act, 2, h, from_residual(act, 0))
            norm_turn_act(act, 2, "mix", S_IN, done=2)
            mix["act"](act)
            post_norm_act(act, 1)
            for k in range(2):
                split_hi(act, S_MQ, None, 0, k, SLAB)
            norm_sums_act(act, 3, h, from_residual(act, 1))
            norm_turn_act(act, 3, "mattn", S_MQ, done=2)
            mat["act"](act)
            post_norm_act(act, 2)
            for k in range(2):
                split_hi(act, S_GU2, None, 0, k, SLAB)
            norm_sums_act(act, 4, h, from_residual(act, 2))
            norm_turn_act(act, 4, "ffn2", S_GU2, done=2)
            ffn_act(act, 1, S_GU2)
            post_norm_act(act, 3)

        @block.vector
        def _(dve):
            for name in ("hT_lo_ready", "y_copied", "shifted"):
                dve.sem_inc(env[name], CREDIT)
            dve.wait_ge(cols_in, 16)
            norm_rows_dve(dve, 0, mem_sb)
            norm_turn_dve(dve, 0, "mem", S_KV)
            for k in range(AHEAD, PAIR):
                split_lo(dve, S_KV, None, 0, k, SLAB)
                if k == 9:
                    dve.wait_ge(x_in, 16)
                    norm_rows_dve(dve, 1, h)
            norm_turn_dve(dve, 1, "ffn1", S_GU1)
            ffn_dve(dve, 0, S_GU1)
            post_norm_dve(dve, 0, y_x, 0.5)
            norm_rows_dve(dve, 2, h)
            norm_turn_dve(dve, 2, "mix", S_IN)
            mix["dve"](dve)
            post_norm_dve(dve, 1, y_b, 1.0)
            norm_rows_dve(dve, 3, h)
            norm_turn_dve(dve, 3, "mattn", S_MQ)
            mat["dve"](dve)
            post_norm_dve(dve, 2, y_b, 1.0)
            norm_rows_dve(dve, 4, h)
            norm_turn_dve(dve, 4, "ffn2", S_GU2)
            ffn_dve(dve, 1, S_GU2)
            post_norm_dve(dve, 3, y_x, 0.5)

        @block.tensor
        def _(pe):
            for name in ("prod_turned", "feat_turned"):
                pe.sem_inc(env[name], CREDIT)
            for name in ("g_o", "r_y"):
                pe.sem_inc(sig(name), CREDIT)
            pe.wait_ge(ident_in, 16)
            norm_pe(pe, 0)
            for c in range(2):
                chunk_products(pe, S_KV, None, 0, 8 * c, NCH, 2 * c, fresh=0 if c == 0 else None)
            pe.wait_ge(kv_rows, 1)
            for hh in range(MH):
                for tt in range(TT):
                    t = nc.tensor.transpose(ps[:, 4 + hh // 2, (hh % 2) * S + tt * P:(hh % 2) * S + (tt + 1) * P],
                                            k_rows[:, tt, hh * P:(hh + 1) * P], ident[:, :])
            t.then_inc(k_turned, 1)
            pe.wait_ge(kv_rows, 2)
            pe.wait_ge(mem_kv_ready, 1)
            norm_pe(pe, 1)
            ffn_pe(pe, 0, S_GU1)
            norm_pe(pe, 2)
            mix["pe"](pe)
            norm_pe(pe, 3)
            mat["pe"](pe)
            norm_pe(pe, 4)
            ffn_pe(pe, 1, S_GU2)


def weight_slabs(w, widths):
    K, N = w.shape
    out, c0 = [], 0
    for wd in widths:
        c = w[:, c0:c0 + wd]
        out.append(c.reshape(K // (2 * P), 2, P, wd).transpose(0, 2, 1, 3).reshape(K // (2 * P), P, 2 * wd))
        c0 += wd
    return out


def down_slabs(w):
    out = np.zeros((4, DOWN, P, SLAB), w.dtype)
    for c in range(4):
        x = w[:, c * NCH:(c + 1) * NCH].reshape(FK, P, NCH)
        out[c, :DOWN - 1] = x[:FK - 1].reshape(DOWN - 1, 2, P, NCH).transpose(0, 2, 1, 3).reshape(DOWN - 1, P, SLAB)
        out[c, DOWN - 1, :, :NCH] = x[FK - 1]
    return out.reshape(2, 2 * DOWN, P, SLAB)


def gate_up_slabs(wg, wu):
    widths = [NCH] * (FFN_PAIRS - 1) + [TAIL_F]
    g, u = weight_slabs(wg, widths), weight_slabs(wu, widths)
    main = np.stack([np.concatenate([a, b]) for a, b in zip(g[:-1], u[:-1])])
    return main, np.concatenate([g[-1], u[-1]])


def channel_columns(parts):
    done = []
    for v, n in parts:
        v = v.reshape(-1)
        x = np.zeros(n * P, v.dtype)
        x[:v.size] = v
        done.append(x.reshape(n, P).T)
    return np.concatenate(done, axis=1)


def kernel(**inputs):
    import concourse.bacc as bacc
    from concourse.bass_utils import run_bass_kernel_spmd

    z = {n: np.asarray(a) for n, a in inputs.items()}
    t = {"x": z["x"], "mem": z["mem"]}
    t["w_kv"] = np.concatenate(weight_slabs(z["mem_w_kv"], [NCH, NCH]))
    t["gu1"], t["gu1_t"] = gate_up_slabs(z["ffn1_w_gate"], z["ffn1_w_up"])
    t["gu2"], t["gu2_t"] = gate_up_slabs(z["ffn2_w_gate"], z["ffn2_w_up"])
    t["dn1"], t["dn2"] = down_slabs(z["ffn1_w_down"]), down_slabs(z["ffn2_w_down"])
    w_in = z["w_in"]
    nsa0 = RW_MAIN + LORA
    w_in = np.concatenate([w_in[:, :RW_MAIN], w_in[:, nsa0:nsa0 + NSA_MAIN], w_in[:, RW_MAIN:nsa0],
                           w_in[:, nsa0 + NSA_MAIN:]], axis=1)
    s = weight_slabs(w_in, [NCH] * 11 + [TAIL_IN])
    t["w_in"] = np.stack([np.concatenate(s[2 * i:2 * i + 2]) for i in range(5)])
    t["w_in5"], t["w_in_t"] = s[10], s[11]
    s = weight_slabs(z["w_out"], [NCH] * 4)
    t["w_out"] = np.stack([np.concatenate(s[2 * i:2 * i + 2]) for i in range(2)])
    t["w_mq"] = weight_slabs(z["mem_w_q"], [NCH])[0]
    t["w_mo"] = np.concatenate(weight_slabs(z["mem_w_o"], [NCH] * 4))
    t["cols"] = channel_columns([
        (z["mem_norm_g"], 16), (z["ffn1_pre_g"], 16), (z["mix_pre_g"], 16), (z["mem_pre_g"], 16), (z["ffn2_pre_g"], 16),
        (z["cmp_pe_k"], 16), (z["cmp_pe_v"], 16), (z["rw_mu"], 27), (z["rw_w0"], 8), (z["rw_a0"], 8), (z["rw_k_k"], 8),
        (z["rw_k_a"], 8), (z["rw_r_k"], 8), (z["rw_ln_w"], 8), (z["rw_ln_b"], 8)])
    t["ident"] = np.eye(P, dtype=np.float32)
    t["mc"] = shape_constants()
    for a in "kv":
        t["w1_" + a] = np.ascontiguousarray(z["cmp_w1_" + a].reshape(16, P, P).transpose(1, 0, 2))
        t["w2_" + a] = z["cmp_w2_" + a]
    t["loraw_wa"] = np.concatenate([z["rw_w_up"], z["rw_a_up"]])
    t["loraw_g"] = z["rw_g_up"]
    for n, a in enumerate(("ffn1_post_g", "mix_post_g", "mem_post_g", "ffn2_post_g")):
        t[f"post{n + 1}"] = z[a]

    nc = bacc.Bacc("TRN2", target_bir_lowering=False, num_devices=1)
    arrays, drams = {}, {}
    for name, a in t.items():
        a = np.ascontiguousarray(a)
        arrays[f"in_{name}_dram"] = a
        drams[name] = nc.dram_tensor(f"in_{name}_dram", a.shape, mybir.dt.from_np(a.dtype), kind="ExternalInput").ap()
    out = nc.dram_tensor("out_0_dram", (1, S, D), F32, kind="ExternalOutput").ap()
    build(nc, drams, out)
    r = run_bass_kernel_spmd(nc, [arrays], core_ids=[0])
    return r.results[0]["out_0_dram"]
```

```python
from contextlib import ExitStack

import numpy as np
import concourse.bass as bass
from concourse import mybir

F32 = mybir.dt.float32
F32R = mybir.dt.float32r
ALU = mybir.AluOpType
ACT = mybir.ActivationFunctionType
AX = mybir.AxisListType

P = 128
D = 2048
S = 256
TT = S // P
DK = D // P
FF = 5504
FK = FF // P
NCH = 512
EPS = 1e-6

RW_HEADS = 16
RW_W = 1024
RW_T = RW_W // P
GN_EPS = 64e-5
C = 64
NC = S // C
RW_MAIN = 3 * RW_W
LORA = 64 + 64 + 160
HD = 64

G = 4
HPG = 4
N_CMP = 15
NSA_MAIN = 1024 + 6 * 256
NSA_W = NSA_MAIN + 48
OFF_KC, OFF_VC, OFF_KS, OFF_VS, OFF_KW, OFF_VW, OFF_GL = (1024 + 256 * n for n in range(7))
ROPE_H = 8
NEG = -1e30

MH = 4
MEM_W = 512

CREDIT = 1
RING = 4
SLAB = 2 * NCH
TAIL_F = FF - 10 * NCH
TAIL_IN = LORA + 48

FFN_PAIRS = 11
PAIR = 2 * (DK // 2)
DOWN = (FK + 1) // 2

S_KV = 0
S_GU1 = S_KV + PAIR
S_DN1 = S_GU1 + FFN_PAIRS * PAIR
S_IN = S_DN1 + 4 * DOWN
S_OUT = S_IN + 6 * PAIR
S_MQ = S_OUT + 2 * PAIR
S_MO = S_MQ + PAIR // 2
S_GU2 = S_MO + 8
S_DN2 = S_GU2 + FFN_PAIRS * PAIR
S_END = S_DN2 + 4 * DOWN

COLS = {}
_at = 0
for _name, _n in (("mem", 16), ("ffn1", 16), ("mix", 16), ("mattn", 16), ("ffn2", 16), ("pe_k", 16), ("pe_v", 16),
                  ("mu", 27), ("w0", 8), ("a0", 8), ("k_k", 8), ("k_a", 8), ("r_k", 8), ("ln_w", 8), ("ln_b", 8)):
    COLS[_name] = _at
    _at += _n
NCOLS = _at

MC = {}
_at = 0
for _name, _n in (("hsel", 8 * 16), ("bones", 128), ("bmean", 128), ("hselT", 8 * 128), ("neg_up1", 128), ("up2", 64),
                  ("up4", 64), ("up8", 64), ("up16", 64), ("up32", 64), ("strict", 128), ("incl", 64),
                  ("causal", 256), ("cmp_add", 2 * 15), ("cmp_mul", 2 * 15), ("cos", 16), ("sin", 16),
                  ("blk", 4), ("start", 256), ("notstart", 256)):
    MC[_name] = (_at, _n)
    _at += _n
NMC = _at


def shape_constants():
    m = np.zeros((P, NMC), np.float32)

    def put(name, a):
        at, n = MC[name]
        m[:a.shape[0], at:at + n] = a.reshape(a.shape[0], n)

    p = np.arange(P)
    half, loc = p // C, p % C
    put("hsel", (np.arange(16)[None, None, :] == 2 * np.arange(8)[None, :, None] + half[:, None, None]).astype("f"))
    put("hselT", (np.arange(16)[:, None, None] == 2 * np.arange(8)[None, :, None] + half[None, None, :]).astype("f"))
    same = half[:, None] == half[None, :]
    put("bones", same.astype("f"))
    put("bmean", same.astype("f") / C)
    row, col = loc[:, None], loc[None, :]

    def up(b):
        return same & (row < col) & (row // (2 * b) == col // (2 * b)) & (row // b != col // b)

    put("neg_up1", -up(1).astype("f"))
    for b in (2, 4, 8, 16, 32):
        put(f"up{b}", up(b)[:, p // b % 2 == 1].astype("f"))
    put("strict", (same & (row < col)).astype("f"))
    put("incl", (row <= np.arange(C)[None, :]).astype("f"))
    causal = np.zeros((P, 2 * P), np.float32)
    causal[:, P:] = np.where(np.arange(P)[None, :] <= p[:, None], 0.0, NEG)
    put("causal", causal)
    t = p[:, None, None] + P * np.arange(TT)[None, :, None]
    seen = 16 * np.arange(N_CMP)[None, None, :] + 31 <= t
    put("cmp_add", np.where(seen, 0.0, NEG).astype("f"))
    put("cmp_mul", seen.astype("f"))
    inv = (np.float32(500000.0) ** (-np.arange(ROPE_H, dtype=np.float32) * np.float32(2.0) / np.float32(16))).astype("f")
    ang = (t.astype("f") * inv[None, None, :]).astype("f")
    put("cos", np.cos(ang))
    put("sin", np.sin(ang))
    put("blk", (p[:, None] // 32 == np.arange(4)[None, :]).astype("f"))
    start = np.broadcast_to((np.arange(S) % C == 0).astype("f"), (P, S))
    put("start", start)
    put("notstart", 1 - start)
    return m


def bc(ap, shape):
    return ap.to_broadcast(list(shape))


def mixing(nc, e):
    g_ = e
    (raw, ps, ident, cols, h) = (g_[n] for n in ("raw", "ps", "ident", "cols", "h"))
    (x_hi, x_lo, mc, rkv, yN, lora, nf, shb, dif, fst, w1, w2, vblk) = (g_[n] for n in (
        "x_hi", "x_lo", "mc", "rkv", "yN", "lora", "nf", "shb", "dif", "fst", "w1", "w2", "vblk"))
    (kdup, kc2, hid, hb, hidrep, qn, qr, kk2, vv, qnT, qrT, kT, p0, p1, pc, pcT, vbg, pT0, pT1, kcT, kcg, qrot, rt, gates,
     gg, sm, smc) = (g_[n] for n in (
         "kdup", "kc2", "hid", "hb", "hidrep", "qn", "qr", "kk2", "vv", "qnT", "qrT", "kT", "p0", "p1", "pc", "pcT", "vbg",
         "pT0", "pT1", "kcT", "kcg", "qrot", "rt", "gates", "gg", "sm", "smc"))
    (kkT, aT, wT, yR, wa_up, g_up, sq8, nrm, bZ, kZ, vZ, kkZ, Am, Zm, Ym, VtZ, KtZ, BtZ, Xm, Pd, iP, Bm, kp, tmp, rt_, Vt,
     Qb, Qk, Sc, SZ, Wc, Uc, UZ, Pe, vq, Sp, rtn, kkd, bon, Pn, sqb, rb, s4) = (g_[n] for n in (
         "kkT", "aT", "wT", "yR", "wa_up", "g_up", "sq8", "nrm", "bZ", "kZ", "vZ", "kkZ", "Am", "Zm", "Ym", "VtZ", "KtZ",
         "BtZ", "Xm", "Pd", "iP", "Bm", "kp", "tmp", "rt_", "Vt", "Qb", "Qk", "Sc", "SZ", "Wc", "Uc", "UZ", "Pe",
         "vq", "Sp", "rtn", "kkd", "bon", "Pn", "sqb", "rb", "s4"))
    root_tables, AHEAD = g_["root_tables"], g_["AHEAD"]
    (sig, col, msk, split_hi, split_lo, slab_products, chunk_products, used, square_y, copy_y) = (g_[n] for n in (
        "sig", "col", "msk", "split_hi", "split_lo", "slab_products", "chunk_products", "used", "square_y", "copy_y"))
    (feat_rows, feat_turned, feat_T, shifted, mc_in, w1_in, loraw_in, y_copied, y_squared, h_ready, slab_used,
     y_hi_ready, y_lo_ready, Y_BASE, y_b) = (g_[n] for n in (
         "feat_rows", "feat_turned", "feat_T", "shifted", "mc_in", "w1_in", "loraw_in", "y_copied", "y_squared",
         "h_ready", "slab_used", "y_hi_ready", "y_lo_ready", "Y_BASE", "y_b"))
    V, A, T = nc.vector, nc.scalar, nc.tensor
    TL0 = S_IN + 5 * PAIR
    LEVELS = (2, 4, 8, 16, 32)
    DECAY = -float(np.exp(-0.5))
    cmp_add = msk("cmp_add").rearrange("p (t n) -> p t n", t=TT)
    cmp_mul = msk("cmp_mul").rearrange("p (t n) -> p t n", t=TT)
    cos = msk("cos").rearrange("p (t n) -> p t n", t=TT)
    sin = msk("sin").rearrange("p (t n) -> p t n", t=TT)

    def bank(n, w):
        return ps[:, n, :].rearrange("p (b w) -> p b w", w=w)

    def banks(n, m, w):
        return ps[:, n:n + m, :].rearrange("p a (b w) -> p (a b) w", w=w)

    def settle():
        V.drain()

    def pool_fn(pool):
        G_ = nc.gpsimd
        pool.dma_start(wa_up[:, :], e["drams_of"]("loraw_wa")).then_inc(loraw_in, 16)
        pool.wait_ge(feat_rows, 9 + CREDIT)
        for n, off in enumerate((OFF_KC, OFF_VC)):
            for tt in range(TT):
                src = nf[:, tt, off:off + G * HD].rearrange("p (g d) -> p g d", g=G).unsqueeze(2)
                v = G_.tensor_copy(kdup[:, n, tt], bc(src, [P, G, 2, HD]))
        v.then_inc(sig("c_dup"), 1)
        nsa_pool(pool)
        pool.wait_ge(sig("g_values"), G)
        pool.dma_start(g_up[:, 0, :], e["drams_of"]("loraw_g")[0:P, :]).then_inc(loraw_in, 16)
        pool.dma_start(g_up[0:32, 1, :], e["drams_of"]("loraw_g")[P:160, :]).then_inc(loraw_in, 16)
        prepare_keys(0).then_inc(sig("r_keys"), 1)
        pool.wait_ge(sig("g_scores"), 2 * G)
        G_.memset(bZ[:, :, :], 0.0)
        G_.memset(vZ[:, :, :], 0.0)
        G_.memset(UZ[:, :, :], 0.0)
        pool.wait_ge(sig("g_p_turned"), 2 * G)
        G_.memset(kkZ[:, :, :], 0.0)
        pool.wait_ge(sig("g_o_out"), G + CREDIT)
        G_.memset(SZ[:, :, :], 0.0)
        G_.memset(kZ[:, :, :], 0.0).then_inc(sig("r_cleared"), 1)
        rec_pool(pool)
        pool.wait_ge(y_lo_ready, 6)

    def turn(blocks):
        for m in range(blocks):
            w = P if m < 2 or blocks == 4 else 32
            for tt in range(TT):
                t = T.transpose(ps[0:w, 4 + m // 2, (m % 2) * S + tt * P:(m % 2) * S + (tt + 1) * P],
                                fst[:, tt, m * P:m * P + w], ident[:, :])
        t.then_inc(feat_turned, 1)

    def in_last_turn(pe):
        pe.wait_ge(feat_rows, 12 + CREDIT)
        pe.wait_ge(feat_T, 6 + CREDIT)
        turn(3)

    RKV = 3

    def in_pe(pe):
        def pair(i, turned, last_turned):
            for k in range(PAIR):
                if k == 0:
                    pe.wait_ge(feat_rows, i * 2 - 1 + CREDIT)
                if k == 4 and last_turned:
                    pe.wait_ge(feat_rows, i * 2 + CREDIT)
                    pe.wait_ge(feat_T, i * 2 - 1 + CREDIT)
                    turn(4)
                if k == 8:
                    pe.wait_ge(feat_rows, i * 2 + CREDIT)
                m = k % (PAIR // 2)
                slab_products(pe, S_IN, i, PAIR, k, x_hi, x_lo, (2 * m, 2 * m + 1), NCH, 2 * (k // 8), m == 0, m == 7)
                if k == 12 and turned:
                    pe.wait_ge(feat_rows, i * 2 + 1 + CREDIT)
                    pe.wait_ge(feat_T, i * 2 + CREDIT)
                    turn(4)

        for k in range(PAIR):
            m = k % (PAIR // 2)
            slab_products(pe, S_IN, None, 0, k, x_hi, x_lo, (2 * m, 2 * m + 1), NCH, 2 * (k // 8), m == 0, m == 7,
                          fresh=2 if k < 8 else None)
            if k == 12:
                pe.wait_ge(feat_rows, 1 + CREDIT)
                turn(4)
        with pe.Fori(1, RKV) as i:
            pair(i, True, True)
        pair(3, False, True)
        pair(4, False, False)
        pe.wait_ge(feat_rows, 9 + CREDIT)
        chunk_products(pe, TL0, None, 0, 0, NCH, 0)
        pe.wait_ge(feat_rows, 10 + CREDIT)
        chunk_products(pe, TL0, None, 0, 8, TAIL_IN, 2)

    def in_act(act):
        def rows(dst, bank0, w=NCH):
            for tt in range(TT):
                a = A.activation(dst(tt), ps[:, bank0 + tt, 0:w], ACT.Copy, scale=g_["rstd"](2, tt))
            a.then_inc(feat_rows, 1)

        def turned_out():
            for b in range(2):
                a = A.activation(shb[:, 2 * b:2 * b + 2, 1:S + 1], bank(4 + b, S), ACT.Copy)
            a.then_inc(feat_T, 1)

        def pair(i, turned, last_turned, last_rows, done=0, tail=False):
            for k in range(done, PAIR):
                split_hi(act, S_IN, i, PAIR, k, 2 * TAIL_IN if tail and k >= 8 else SLAB)
                if k == 3 and last_rows:
                    used(act, S_IN, i, PAIR, -1)
                    if last_turned:
                        act.wait_ge(feat_turned, i * 2 - 1 + CREDIT)
                        rows(lambda tt: fst[:, tt, :], 2)
                    else:
                        rows(lambda tt: nf[:, tt, ((i - 3) * 2 - 1) * NCH:(i - 3) * 2 * NCH], 2)
                if k == 7 and last_turned:
                    act.wait_ge(feat_turned, i * 2 + CREDIT)
                    act.wait_ge(shifted, i * 2 - 1 + CREDIT)
                    turned_out()
                if k == 11:
                    used(act, S_IN, i, PAIR, 7)
                    if turned:
                        act.wait_ge(feat_turned, i * 2 + CREDIT)
                        rows(lambda tt: fst[:, tt, :], 0)
                    else:
                        rows(lambda tt: nf[:, tt, (i - 3) * 2 * NCH:((i - 3) * 2 + 1) * NCH], 0)
                if k == 15 and turned:
                    act.wait_ge(feat_turned, i * 2 + 1 + CREDIT)
                    act.wait_ge(shifted, i * 2 + CREDIT)
                    turned_out()

        pair(0, True, False, False, done=AHEAD)
        with act.Fori(1, RKV) as i:
            pair(i, True, True, True)
        pair(3, False, True, True)
        pair(4, False, False, True)
        pair(5, False, False, True, tail=True)
        used(act, TL0, None, 0, PAIR - 1)
        for tt in range(TT):
            r = g_["rstd"](2, tt)
            A.activation(fst[:, tt, 0:LORA], ps[:, 2 + tt, 0:LORA], ACT.Copy, scale=r)
            a = A.activation(nf[:, tt, OFF_GL:OFF_GL + 48], ps[:, 2 + tt, LORA:TAIL_IN], ACT.Copy, scale=r)
        a.then_inc(feat_rows, 1)

    def in_last_turned(act):
        act.wait_ge(feat_turned, 7 + CREDIT)
        act.wait_ge(shifted, 6 + CREDIT)
        A.activation(shb[:, 0:2, 1:S + 1], bank(4, S), ACT.Copy)
        A.activation(shb[0:32, 2, 1:S + 1], ps[0:32, 5, 0:S], ACT.Copy).then_inc(feat_T, 1)

    MU = COLS["mu"]

    def shift(dst, mu0, q, n):
        V.tensor_tensor(dif[0:q, 0:n, :], shb[0:q, 0:n, 0:S], shb[0:q, 0:n, 1:S + 1], ALU.subtract)
        settle()
        mu = cols[0:q, bass.ds(mu0, n)].unsqueeze(2)
        V.tensor_tensor(dif[0:q, 0:n, :], dif[0:q, 0:n, :], bc(mu, [q, n, S]), ALU.mult)
        settle()
        return V.tensor_tensor(dst, dif[0:q, 0:n, :], shb[0:q, 0:n, 1:S + 1], ALU.add)

    def in_dve(dve):
        V.memset(shb[:, :, 0:1], 0.0)
        settle()
        def shift_chunk(n):
            dve.wait_ge(feat_T, n + 1 + CREDIT)
            shift(rkv[:, bass.ds(n * 4, 4), :], n * 4 + MU, P, 4).then_inc(shifted, 1)

        def pair(i, last_turned, done=0, tail=False):
            for k in range(done, PAIR):
                split_lo(dve, S_IN, i, PAIR, k, 2 * TAIL_IN if tail and k >= 8 else SLAB)
                if k == 1 and last_turned:
                    shift_chunk(i * 2 - 2)
                if k == 10 and last_turned:
                    shift_chunk(i * 2 - 1)

        pair(0, False, done=AHEAD)
        with dve.Fori(1, RKV) as i:
            pair(i, True)
        pair(3, True)
        pair(4, False)
        pair(5, False, tail=True)

    def in_last_shift(dve):
        dve.wait_ge(feat_T, 7 + CREDIT)
        shift(lora[:, 0:2, :], MU + 24, P, 2)
        settle()
        V.tensor_tensor(dif[0:32, 0, :], shb[0:32, 2, 0:S], shb[0:32, 2, 1:S + 1], ALU.subtract)
        settle()
        V.scalar_tensor_tensor(out=lora[0:32, 2, :], in0=dif[0:32, 0, :], scalar=cols[0:32, MU + 26:MU + 27],
                               in1=shb[0:32, 2, 1:S + 1], op0=ALU.mult, op1=ALU.add).then_inc(shifted, 1)

    W = G * N_CMP

    def lora_up(k):
        for j in range(RW_T):
            m = T.matmul(ps[:, 4 + j // 2, (j % 2) * S:(j % 2 + 1) * S], wa_up[64 * k:64 * k + 64, P * j:P * (j + 1)],
                         lora[64 * k:64 * k + 64, 0, :], start=True, stop=True)
        m.then_inc(sig("wa_done"), 1)

    def sigmoids(act, k, dst, bias):
        act.wait_ge(sig("wa_done"), k + 1)
        for j in range(RW_T):
            a = A.activation(dst[:, j, :], ps[:, 4 + j // 2, (j % 2) * S:(j % 2 + 1) * S], ACT.Sigmoid, bias=col(bias, j))
        a.then_inc(sig("wa_out"), 1)

    def pre_pe(pe):
        pe.wait_ge(sig("c_dup"), 1)
        for n in range(2):
            for g in range(G):
                for tt in range(TT):
                    t = T.transpose(ps[:, 6 * n + g // 2, (g % 2) * S + tt * P:(g % 2) * S + (tt + 1) * P],
                                    kdup[:, n, tt, g].rearrange("p a d -> p (a d)"), ident[:, :])
            t.then_inc(sig("c_turned"), 1)
        in_last_turn(pe)
        pe.wait_ge(w1_in, 80)
        pe.wait_ge(sig("c_pe"), 1)
        for n in range(2):
            pe.wait_ge(sig("c_T"), n + 1)
            for j in range(16):
                m = T.matmul(ps[:, 3, n * S:n * S + W + N_CMP], w1[:, n, j, :], kc2[:, n, :, 2 * j:2 * j + 16 * 14 + 1:16],
                             start=j == 0, stop=j == 15)
        m.then_inc(sig("c_hidden"), 1)
        pe.wait_ge(loraw_in, 16)
        pe.wait_ge(sig("lora_act"), 1)
        lora_up(0)
        pe.wait_ge(sig("c_gelu"), 1)
        T.matmul(ps[:, 3, 0:W], w2[:, 0:2, :].rearrange("p a d -> p (a d)"), hid[:, 6, 0:W],
                 start=True, stop=True).then_inc(sig("kc_done"), 1)
        for g in range(G):
            m = T.matmul(ps[:, 2, g * HD:(g + 1) * HD], hidrep[:, g].rearrange("p a n -> p (a n)"), w2[:, 2, :],
                         start=True, stop=True)
        m.then_inc(sig("vc_done"), 1)
        pe.wait_ge(sig("vblk_ready"), 1)

    def pre_act(act):
        for n in range(2):
            act.wait_ge(sig("c_turned"), n + 1)
            v = banks(6 * n, 2, S)
            A.activation(kc2[0:HD, n, 0:G, :], v[0:HD], ACT.Copy)
            A.activation(kc2[HD:P, n, 0:G, 0:S - 1], v[HD:P, :, 1:S], ACT.Copy).then_inc(sig("c_T"), 1)
            if n == 0:
                in_last_turned(act)
        act.wait_ge(shifted, 7 + CREDIT)
        A.activation(lora[0:64, 0, :], lora[0:64, 0, :], ACT.Tanh)
        A.activation(lora[:, 1, :], lora[:, 1, :], ACT.Sigmoid)
        A.activation(lora[0:32, 2, :], lora[0:32, 2, :], ACT.Sigmoid).then_inc(sig("lora_act"), 1)
        A.activation(gates[:, :, :], nf[:, :, OFF_GL:OFF_GL + 48], ACT.Sigmoid).then_inc(sig("gates_ready"), 1)
        act.wait_ge(sig("c_inner"), 1)
        A.activation(hid[:, 4:6, 0:W], hid[:, 2:4, 0:W], ACT.Tanh, scale=0.7978845608028654).then_inc(sig("c_tanh"), 1)
        sigmoids(act, 0, wT, "w0")
        act.wait_ge(sig("kc_done"), 1)
        A.activation(kcT[:, :, 0:N_CMP], ps[:, 3, 0:W].rearrange("p (g n) -> p g n", g=G),
                     ACT.Copy).then_inc(sig("kcT_ready"), 1)

    def pre_dve(dve):
        dve.wait_ge(mc_in, 16)
        dve.wait_ge(feat_rows, 12 + CREDIT)
        V.memset(kc2[:, :, G, :], 0.0)
        settle()
        V.tensor_copy(kc2[:, :, G, 0:32:2], cols[:, COLS["pe_k"]:COLS["pe_k"] + 32].rearrange("p (n j) -> p n j", n=2)
                      ).then_inc(sig("c_pe"), 1)
        in_last_shift(dve)
        for tt in range(TT):
            for kind in ("q", "k"):
                if kind == "q":
                    heads = nf[:, tt, 0:1024].rearrange("p (h d) -> p h d", d=HD)
                    x1, x2 = heads[:, :, 0:ROPE_H], heads[:, :, ROPE_H:2 * ROPE_H]
                    o1, o2 = qrot[:, tt, :, 0:ROPE_H], qrot[:, tt, :, ROPE_H:2 * ROPE_H]
                    cs, sn = (bc(a[:, tt].unsqueeze(1), [P, 16, ROPE_H]) for a in (cos, sin))
                    views = [(x1, x2, o1, o2, [rt[:, m, 0:16, :] for m in range(4)])]
                else:
                    views = []
                    for off in (OFF_KS, OFF_KW):
                        heads = nf[:, tt, off:off + 256].rearrange("p (h d) -> p h d", d=HD)
                        x1, x2 = heads[:, :, 0:ROPE_H], heads[:, :, ROPE_H:2 * ROPE_H]
                        views.append((x1, x2, x1, x2, [rt[:, m, 0:4, :] for m in range(4)]))
                    cs, sn = (bc(a[:, tt].unsqueeze(1), [P, 4, ROPE_H]) for a in (cos, sin))
                for x1, x2, o1, o2, tb in views:
                    settle()
                    V.tensor_tensor(tb[0], x1, cs, ALU.mult)
                    V.tensor_tensor(tb[1], x2, sn, ALU.mult)
                    V.tensor_tensor(tb[2], x2, cs, ALU.mult)
                    V.tensor_tensor(tb[3], x1, sn, ALU.mult)
                    settle()
                    V.tensor_tensor(o1, tb[0], tb[1], ALU.subtract)
                    v = V.tensor_tensor(o2, tb[2], tb[3], ALU.add)
        v.then_inc(sig("nsa_prepared"), 1)
        V.memset(pc[:, :, :, :], 0.0)
        V.memset(hidrep[:, :, :, :], 0.0)
        dve.wait_ge(sig("c_hidden"), 1)
        x, t, y = hid[:, 0:2, 0:W], hid[:, 2:4, 0:W], hid[:, 6:8, 0:W]
        V.tensor_copy(hb[:, :], bank(3, S)[:, :, W])
        settle()
        V.tensor_tensor(x, bank(3, S)[:, :, 0:W], bc(hb[:, :].unsqueeze(2), [P, 2, W]), ALU.add)
        settle()
        V.tensor_tensor(t, x, x, ALU.mult)
        settle()
        V.tensor_tensor(t, t, x, ALU.mult)
        settle()
        V.scalar_tensor_tensor(out=t, in0=t, scalar=0.044715, in1=x, op0=ALU.mult, op1=ALU.add).then_inc(sig("c_inner"), 1)
        dve.wait_ge(sig("c_tanh"), 1)
        V.scalar_tensor_tensor(out=y, in0=hid[:, 4:6, 0:W], scalar=1.0, in1=x, op0=ALU.add, op1=ALU.mult)
        settle()
        V.tensor_scalar(y, y, 0.5, None, ALU.mult)
        settle()
        V.tensor_copy(hidrep[:, :, :, 0:N_CMP],
                      bc(hid[:, 7, 0:W].rearrange("p (g n) -> p g n", g=G).unsqueeze(2), [P, G, 4, N_CMP])
                      ).then_inc(sig("c_gelu"), 1)
        dve.wait_ge(sig("vc_done"), 1)
        V.tensor_tensor(vblk[:, :, :, :],
                        bc(ps[:, 2, 0:G * HD].rearrange("p (g d) -> p g d", g=G).unsqueeze(2), [P, G, 4, HD]),
                        bc(msk("blk").unsqueeze(1).unsqueeze(3), [P, G, 4, HD]), ALU.mult).then_inc(sig("vblk_ready"), 1)

    def hsum(src, dst):
        for j in range(RW_T):
            m = T.matmul(dst, msk("hsel")[:, 16 * j:16 * j + 16], src[:, j, :], start=j == 0, stop=j == RW_T - 1)
        return m

    def hspread(src, bank0):
        for j in range(RW_T):
            m = T.matmul(ps[:, bank0 + j // 2, (j % 2) * S:(j % 2 + 1) * S], msk("hselT")[0:16, P * j:P * (j + 1)], src,
                         start=True, stop=True)
        return m

    def nsa_pool(pool):
        def rows(n):
            q = nf[:, :, bass.ds(n * 256, 256)].rearrange("p t (a d) -> p t a d", a=4)
            nc.gpsimd.tensor_copy(qr[:, :, :, 2 * ROPE_H:], q[:, :, :, 2 * ROPE_H:])
            nc.gpsimd.tensor_copy(qr[:, :, :, 0:2 * ROPE_H], qrot[:, :, bass.ds(n * 4, 4), :])
            for b, off in enumerate((OFF_KS, OFF_KW)):
                for tt in range(TT):
                    nc.gpsimd.tensor_copy(kk2[:, b, tt], bc(nf[:, tt, bass.ds(n * HD + off, HD)].unsqueeze(1), [P, 2, HD]))
            nc.gpsimd.tensor_copy(qn[:, :, :, :], q).then_inc(sig("g_rows"), 1)

        def values(n):
            for b, off in enumerate((OFF_VS, OFF_VW)):
                nc.gpsimd.tensor_copy(vv[:, b], nf[:, :, bass.ds(n * HD + off, HD)])
            for tt in range(TT):
                nc.gpsimd.tensor_copy(gg[:, tt], gates[:, tt, :].rearrange("p (b h) -> p b h", b=3)[:, :, bass.ds(n * 4, 4)])
            nc.gpsimd.tensor_copy(vbg[:, :, :], vblk[:, bass.ds(n, 1)].rearrange("p a b d -> p (a b) d")
                                  ).then_inc(sig("g_values"), 1)

        def keys(n):
            nc.gpsimd.tensor_copy(kcg[:, 0:N_CMP], kcT[:, bass.ds(n, 1), 0:N_CMP].rearrange("p a n -> p (a n)")
                                  ).then_inc(sig("g_keys"), 1)

        def next_rows(n):
            pool.wait_ge(sig("g_turned"), n)
            rows(n)
            pool.wait_ge(sig("g_scores"), n * 2 - 1)
            keys(n)

        def next_values(n):
            pool.wait_ge(sig("g_o"), n + CREDIT)
            values(n)

        pool.wait_ge(sig("nsa_prepared"), 1)
        rows(0)
        pool.wait_ge(sig("kcT_ready"), 1)
        keys(0)
        pool.wait_ge(sig("gates_ready"), 1)
        pool.wait_ge(sig("vblk_ready"), 1)
        values(0)
        next_rows(1)
        nc.gpsimd.tensor_tensor(kkT[:, :, :], rkv[:, RW_T:2 * RW_T, :], bc(col("k_k", 0, 8).unsqueeze(2), [P, RW_T, S]),
                                ALU.mult).then_inc(sig("kk_made"), 1)
        pool.wait_ge(sig("kk_made"), 1)
        nc.gpsimd.tensor_tensor(sq8[:, :, :], kkT[:, :, :], kkT[:, :, :], ALU.mult).then_inc(sig("kk_squared"), 1)
        with pool.Fori(1, G - 1) as n:
            next_rows(n + 1)
            next_values(n)
        next_values(G - 1)

    def nsa_pe(pe):
        def turn_rows(n):
            pe.wait_ge(sig("g_rows"), n + 1)
            for src, b in ((qn, 0), (qr, 1)):
                for j in range(2):
                    for tt in range(TT):
                        T.transpose(ps[:, b, j * S + tt * P:j * S + (tt + 1) * P],
                                    src[:, tt, 2 * j:2 * j + 2, :].rearrange("p a d -> p (a d)"), ident[:, :])
            for b in range(2):
                for tt in range(TT):
                    t = T.transpose(ps[:, 2, b * S + tt * P:b * S + (tt + 1) * P],
                                    kk2[:, b, tt].rearrange("p a d -> p (a d)"), ident[:, :])
            t.then_inc(sig("g_turned"), 1)

        def scores(b):
            for p in range(2):
                r = slice(64 * p, 64 * p + 64)
                for j in range(2):
                    T.matmul(ps[:, p, j * P:(j + 1) * P], qrT[r, j, 0:P], kT[r, b, 0:P], start=True, stop=True)
                    m = T.matmul(ps[:, 2 + p, j * S:(j + 1) * S], qrT[r, j, P:S], kT[r, b, :], start=True, stop=True)
                    if b == 0:
                        for tt in range(TT):
                            c0 = S + (2 * tt + j) * 16
                            m = T.matmul(ps[:, p, c0:c0 + N_CMP], qnT[r, j, tt * P:(tt + 1) * P], kcg[r, 0:N_CMP],
                                         start=True, stop=True)
            m.then_inc(sig("g_scores"), 1)

        def turn_probs(n, b):
            pe.wait_ge(sig("g_probs"), n * 2 + b + 1)
            if b == 0:
                pe.wait_ge(sig("g_o_out"), n + CREDIT)
                for tt in range(TT):
                    T.transpose(ps[:, 7, tt * P:(tt + 1) * P], pc[:, tt].rearrange("p a n -> p (a n)"), ident[:, :])
            for j in range(2):
                for p in range(2):
                    T.transpose(ps[:, 4 + j, p * S:p * S + P], p0[:, b, 2 * p + j, :], ident[:, :])
                    T.transpose(ps[:, 4 + j, p * S + P:(p + 1) * S], p1[:, b, 2 * p + j, 0:P], ident[:, :])
                    t = T.transpose(ps[:, 6, (2 * j + p) * P:(2 * j + p + 1) * P], p1[:, b, 2 * p + j, P:S], ident[:, :])
            t.then_inc(sig("g_p_turned"), 1)

        def outputs(n, b):
            pe.wait_ge(sig("g_pT_act"), n * 2 + b + 1)
            pe.wait_ge(sig("g_pT_dve"), n * 2 + b + 1)
            if b == 0:
                pe.wait_ge(sig("g_values"), n + 1)
                for j in range(2):
                    T.matmul(ps[:, 7, j * S:(j + 1) * S], vbg[:, 2 * j:2 * j + 2, :].rearrange("p a d -> p (a d)"),
                             pcT[:, :], start=j == 0, stop=False, skip_group_check=True)
            for j in range(2):
                for p in range(2):
                    r = slice(64 * p, 64 * p + 64)
                    T.matmul(ps[r, 7, j * S:(j + 1) * S], vv[:, b, 0, :], pT0[:, b, 2 * j + p, :],
                             start=False, stop=False, skip_group_check=True)
                    m = T.matmul(ps[r, 7, j * S + P:(j + 1) * S], vv[:, b, 1, :], pT1[:, b, 2 * j + p, :],
                                 start=False, stop=b == 1, skip_group_check=True)
            if b == 1:
                m.then_inc(sig("g_o"), 1)

        def group(n, last=False):
            if not last:
                pe.wait_ge(sig("g_masked"), n * 2 + 2)
                turn_rows(n + 1)
            turn_probs(n, 0)
            if not last:
                pe.wait_ge(sig("g_keys"), n + 2)
                pe.wait_ge(sig("g_T"), n + 2)
                scores(0)
            else:
                pe.wait_ge(sig("kk_squared"), 1)
                pe.wait_ge(sig("g_masked"), n * 2 + 2)
                hsum(sq8, ps[0:16, 0, 0:S]).then_inc(sig("kk_summed"), 1)
            outputs(n, 0)
            if not last:
                pe.wait_ge(sig("g_masked"), n * 2 + 3)
                scores(1)
            turn_probs(n, 1)
            if last:
                pe.wait_ge(sig("kk_rnorm"), 1)
                hspread(nrm[0:16, 1, :], 0).then_inc(sig("kk_spread"), 1)
            outputs(n, 1)

        turn_rows(0)
        pe.wait_ge(sig("wa_out"), 1)
        lora_up(1)
        pe.wait_ge(sig("g_keys"), 1)
        pe.wait_ge(sig("g_T"), 1)
        scores(0)
        pe.wait_ge(sig("g_masked"), 1)
        scores(1)
        with pe.Fori(0, G - 1) as n:
            group(n)
        group(G - 1, last=True)

    def nsa_act(act):
        def rows_T(n):
            act.wait_ge(sig("g_turned"), n + 1)
            A.activation(qrT[:, :, :], bank(1, S), ACT.Copy, scale=HD ** -0.5)
            A.activation(kT[:, :, :], bank(2, S), ACT.Copy)
            A.activation(qnT[:, :, :], bank(0, S), ACT.Copy, scale=HD ** -0.5).then_inc(sig("g_T"), 1)

        def exps(n, b):
            act.wait_ge(sig("g_max"), n * 2 + b + 1)
            if b == 0:
                cmp = pc[:, :, :, 0:N_CMP].rearrange("p t a n -> p (t a) n")
                A.activation(cmp, cmp, ACT.Exp)
            for k in range(4):
                A.activation(p0[:, b, k, :], p0[:, b, k, :], ACT.Exp, bias=sm[:, b, 0, k:k + 1],
                             accum_out=sm[:, b, 1, k:k + 1])
                a = A.activation(p1[:, b, k, :], p1[:, b, k, :], ACT.Exp, bias=sm[:, b, 0, 4 + k:5 + k],
                                 accum_out=sm[:, b, 1, 4 + k:5 + k])
            a.then_inc(sig("g_exp"), 1)

        def probs_T(n, b):
            act.wait_ge(sig("g_p_turned"), n * 2 + b + 1)
            if b == 0:
                A.activation(pcT[:, :], ps[:, 7, 0:S], ACT.Copy)
            A.activation(pT0[:, b], banks(4, 2, S), ACT.Copy).then_inc(sig("g_pT_act"), 1)

        def group(n, last=False):
            if not last:
                rows_T(n + 1)
            exps(n, 1)
            probs_T(n, 0)
            if not last:
                exps(n + 1, 0)
            if last:
                act.wait_ge(sig("kk_clamped"), 1)
                A.activation(nrm[0:16, 2, :], nrm[0:16, 0, :], ACT.Sqrt).then_inc(sig("kk_root"), 1)
            probs_T(n, 1)
            act.wait_ge(sig("g_o"), n + 1 + CREDIT)
            A.activation(yN[:, bass.ds(n * 2, 2), :], bank(7, S), ACT.Copy).then_inc(sig("g_o_out"), 1)

        rows_T(0)
        sigmoids(act, 1, aT, "a0")
        A.activation(wT[:, :, :], wT[:, :, :], ACT.Exp, scale=DECAY)
        exps(0, 0)
        with act.Fori(0, G - 1) as n:
            group(n)
        group(G - 1, last=True)

    def nsa_dve(dve):
        causal = msk("causal")
        cmp = pc[:, :, :, 0:N_CMP].rearrange("p t a n -> p (t a) n")

        def masked(n, b):
            dve.wait_ge(sig("g_scores"), n * 2 + b + 1)
            for p in range(2):
                V.tensor_tensor(p0[:, b, 2 * p:2 * p + 2, :], ps[:, p, 0:S].rearrange("p (j k) -> p j k", j=2),
                                bc(causal[:, P:2 * P].unsqueeze(1), [P, 2, P]), ALU.add)
                x = V.tensor_tensor(p1[:, b, 2 * p:2 * p + 2, :], bank(2 + p, S), bc(causal.unsqueeze(1), [P, 2, S]), ALU.add)
                if b == 0:
                    s = ps[:, p, S:S + 64].rearrange("p (t j n) -> p t j n", t=TT, j=2)[:, :, :, 0:N_CMP]
                    x = V.tensor_tensor(pc[:, :, :, :].rearrange("q t (j p) n -> q t j p n", p=2)[:, :, :, p, 0:N_CMP], s,
                                        bc(cmp_add.unsqueeze(2), [P, TT, 2, N_CMP]), ALU.add)
            x.then_inc(sig("g_masked"), 1)
            settle()
            V.tensor_reduce(sm[:, b, 0, 0:4], p0[:, b], AX.X, ALU.max, negate=True)
            x = V.tensor_reduce(sm[:, b, 0, 4:8], p1[:, b], AX.X, ALU.max, negate=True)
            if b == 0:
                V.tensor_reduce(smc[:, 0, :], cmp, AX.X, ALU.max, negate=True)
                settle()
                x = V.tensor_tensor(cmp, cmp, bc(smc[:, 0, :].unsqueeze(2), [P, 8, N_CMP]), ALU.add)
            x.then_inc(sig("g_max"), 1)

        def probs(n, b):
            dve.wait_ge(sig("g_exp"), n * 2 + b + 1)
            if b == 0:
                dve.wait_ge(sig("g_values"), n + 1)
                V.tensor_reduce(smc[:, 1, :], cmp, AX.X, ALU.add)
            V.reciprocal(sm[:, b, 2, :], sm[:, b, 1, :])
            settle()
            V.tensor_tensor(sm[:, b, 3, :].rearrange("q (t p j) -> q t p j", t=TT, p=2),
                            sm[:, b, 2, :].rearrange("q (t p j) -> q t p j", t=TT, p=2),
                            gg[:, :, 1 + b, :].rearrange("q t (j p) -> q t p j", p=2), ALU.mult)
            if b == 0:
                V.reciprocal(smc[:, 2, :], smc[:, 1, :])
                V.tensor_tensor(pc[:, :, :, 0:N_CMP], pc[:, :, :, 0:N_CMP], bc(cmp_mul.unsqueeze(2), [P, TT, 4, N_CMP]),
                                ALU.mult)
            settle()
            if b == 0:
                V.tensor_tensor(smc[:, 3, :].rearrange("p (t a) -> p t a", t=TT),
                                smc[:, 2, :].rearrange("p (t a) -> p t a", t=TT), gg[:, :, 0, :], ALU.mult)
            V.tensor_tensor(p0[:, b], p0[:, b], bc(sm[:, b, 3, 0:4].unsqueeze(2), [P, 4, P]), ALU.mult)
            x = V.tensor_tensor(p1[:, b], p1[:, b], bc(sm[:, b, 3, 4:8].unsqueeze(2), [P, 4, S]), ALU.mult)
            if b == 0:
                settle()
                x = V.tensor_tensor(cmp, cmp, bc(smc[:, 3, :].unsqueeze(2), [P, 8, N_CMP]), ALU.mult)
            x.then_inc(sig("g_probs"), 1)

        def probs_T(n, b):
            dve.wait_ge(sig("g_p_turned"), n * 2 + b + 1)
            V.tensor_copy(pT1[:, b], bank(6, P)).then_inc(sig("g_pT_dve"), 1)

        def group(n, last=False):
            masked(n, 1)
            probs(n, 0)
            probs_T(n, 0)
            if not last:
                masked(n + 1, 0)
            else:
                dve.wait_ge(sig("r_scan_in"), 1)
                scan().then_inc(sig("r_scan"), 1)
                dve.wait_ge(sig("kk_summed"), 1)
                V.tensor_scalar(nrm[0:16, 0, :], ps[0:16, 0, 0:S], 1e-24, None, ALU.max).then_inc(sig("kk_clamped"), 1)
            probs(n, 1)
            if last:
                dve.wait_ge(sig("kk_root"), 1)
                V.reciprocal(nrm[0:16, 1, :], nrm[0:16, 2, :]).then_inc(sig("kk_rnorm"), 1)
            probs_T(n, 1)

        masked(0, 0)
        with dve.Fori(0, G - 1) as n:
            group(n)
        group(G - 1, last=True)

    def kk_dve(dve):
        dve.wait_ge(sig("kk_spread"), 1)
        V.tensor_tensor(kkT[:, :, :], kkT[:, :, :], banks(0, 4, S), ALU.mult)
        settle()
        dve.wait_ge(sig("r_cleared"), 1)
        dve.wait_ge(sig("r_keys"), 1)
        prepare_blocks(V, 0)

    HALVES = (slice(0, C), slice(C, P))
    UNITS = [(j, c) for j in range(2) for c in range(NC)]

    def blk4(ap):
        return ap.rearrange("p j (c t) -> p (j c) t", t=C)

    def odd(ap, b):
        if len(ap.shape) == 2:
            return ap.rearrange("p (q s b) -> p q s b", s=2, b=b)[:, :, 1, :]
        return ap.rearrange("p u (q s b) -> p u q s b", s=2, b=b)[:, :, :, 1, :]

    def prepare_keys(n):
        eng = nc.gpsimd
        two = bass.ds(n * 2, 2)
        r, k, v = rkv[:, two, :], rkv[:, bass.ds(n * 2 + RW_T, 2), :], rkv[:, bass.ds(n * 2 + 2 * RW_T, 2), :]
        w, a = wT[:, two, :], aT[:, two, :]
        ka = bc(cols[:, bass.ds(n * 2 + COLS["k_a"], 2)].unsqueeze(2), [P, 2, S])
        rk = bc(cols[:, bass.ds(n * 2 + COLS["r_k"], 2)].unsqueeze(2), [P, 2, S])
        eng.tensor_copy(kp[:, :, :], k)
        eng.tensor_tensor(tmp[:, :, :], w, bc(msk("notstart").unsqueeze(1), [P, 2, S]), ALU.mult)
        eng.tensor_tensor(iP[:, :, :], w, bc(msk("start").unsqueeze(1), [P, 2, S]), ALU.mult).then_inc(sig("r_scan_in"), 1)
        eng.tensor_tensor(rtn[:, :, :], a, ka, ALU.mult)
        eng.drain()
        eng.tensor_tensor(kp[:, :, :], kp[:, :, :], ka, ALU.mult)
        eng.drain()
        eng.tensor_tensor(rtn[:, :, :], rtn[:, :, :], k, ALU.mult)
        eng.tensor_tensor(kp[:, :, :], k, kp[:, :, :], ALU.subtract)
        eng.drain()
        eng.tensor_tensor(kp[:, :, :], kp[:, :, :], rtn[:, :, :], ALU.add)
        eng.drain()
        if isinstance(n, int):
            eng.wait_ge(sig("kk_summed"), 1)
        eng.tensor_tensor(bon[:, :, :], r, kp[:, :, :], ALU.mult)
        eng.drain()
        eng.tensor_tensor(bon[:, :, :], bon[:, :, :], rk, ALU.mult)
        eng.wait_ge(sig("r_scan"), n + 1)
        eng.tensor_copy(vq[:, :, :], v)
        eng.tensor_copy(Pn[:, :, :], Pd[:, :, C - 1:S:C])
        return eng.tensor_tensor(rtn[:, :, :], r, Pd[:, :, :], ALU.mult)

    def prepare_blocks(eng, n):
        pool = eng is nc.gpsimd
        two = bass.ds(n * 2, 2)
        a, kk = aT[:, two, :], kkT[:, two, :]
        eng.tensor_tensor(tmp[:, :, :], kk, a, ALU.mult)
        kd = kkd[:, :, :].rearrange("p j (c t) -> p j c t", t=C)
        kk4 = kk.rearrange("p j (c t) -> p j c t", t=C)
        pd4 = Pd[:, :, :].rearrange("p j (c t) -> p j c t", t=C)
        for j in range(2):
            eng.tensor_tensor(kd[:, j, :, 1:C], kk4[:, j, :, 1:C], pd4[:, j, :, 0:C - 1], ALU.mult)
        eng.tensor_copy(kd[:, :, :, 0:1], kk4[:, :, :, 0:1])
        for p, rr in enumerate(HALVES):
            cs = slice(p * C, (p + 1) * C)
            eng.drain()
            if pool and p == 0:
                eng.wait_ge(sig("r_turned"), n * 3)
            eng.tensor_tensor(bZ[rr, :, cs], blk4(tmp[rr]), blk4(iP[rr]), ALU.mult)
            x = eng.tensor_tensor(kZ[rr, :, cs], blk4(kp[rr]), blk4(iP[rr]), ALU.mult)
        x.then_inc(sig("r_prep"), 1)

    def scan(part=None):
        if part in (1, 2):
            return V.reciprocal(iP[:, part - 1, :], Pd[:, part - 1, :])
        V.tensor_tensor_scan(Pd[:, :, :].rearrange("p j t -> p (j t)"), tmp[:, :, :].rearrange("p j t -> p (j t)"),
                             iP[:, :, :].rearrange("p j t -> p (j t)"), 0.0, ALU.mult, ALU.add)
        settle()
        if part is None:
            return V.reciprocal(iP[:, :, :], Pd[:, :, :])

    def rec_pool(pool):
        with pool.Fori(1, RW_T // 2) as n:
            pool.wait_ge(sig("r_prep"), n)
            pool.wait_ge(sig("r_kkZ_dve"), n)
            pool.wait_ge(sig("r_kkZ_act"), n)
            pool.wait_ge(sig("r_bonus"), n)
            pool.wait_ge(sig("r_vZ"), n)
            prepare_keys(n)
            prepare_blocks(nc.gpsimd, n)

    def rec_pe(pe):
        with pe.Fori(0, RW_T // 2) as i:
            pe.wait_ge(sig("r_prep"), i + 1)
            pe.wait_ge(sig("r_y_out"), i * NC + CREDIT)
            T.matmul(ps[:, 7, :], msk("bones"), bon[:, :, :].rearrange("p j t -> p (j t)"), start=True,
                     stop=True).then_inc(sig("r_bonus"), 1)

            def gram(bank0, lhs, rhs, w, name):
                for u in range(8):
                    n = u * w // NCH
                    m = T.matmul(ps[:, bank0 + n, u * w - n * NCH:(u + 1) * w - n * NCH], lhs[:, u, :], rhs(u),
                                 start=True, stop=True)
                m.then_inc(sig(name), 1)

            pe.wait_ge(sig("r_kkZ_act"), i + 1)
            pe.wait_ge(sig("r_kkZ_dve"), i + 1)
            gram(0, bZ, lambda u: kkZ[:, u, :], P, "r_AT")
            gram(2, kkZ, lambda u: bZ[:, u, :], P, "r_Ap")
            gram(6, bZ, lambda u: rt_[:, u // NC, (u % NC) * C:(u % NC + 1) * C], C, "r_Qbp")
            pe.wait_ge(sig("r_bonus_out"), i + 1)
            gram(7, kZ, lambda u: rt_[:, u // NC, (u % NC) * C:(u % NC + 1) * C], C, "r_Qkp")
            gram(4, kZ, lambda u: kkZ[:, u, :], P, "r_Bmp")

            def turn(src, n):
                if n == 0:
                    pe.wait_ge(sig("r_vZ"), i + 1)
                    pe.wait_ge(sig("r_gram_out"), i + 1)
                else:
                    pe.wait_ge(sig("r_t"), i * 3 + n)
                for u in range(8):
                    t = T.transpose(ps[:, 4 + u // 4, (u % 4) * P:(u % 4 + 1) * P], src[:, u, :], ident[:, :])
                t.then_inc(sig("r_turned"), 1)

            pe.wait_ge(sig("r_A"), i + 1)
            pe.wait_ge(sig("r_Q"), i + 1)
            for n in range(len(LEVELS)):
                for g in range(2):
                    pe.wait_ge(sig("r_x"), i * 12 + 2 * n + g + 1)
                    for u in range(4 * g, 4 * g + 4):
                        m = T.matmul(ps[:, g, (u % 4) * C:(u % 4 + 1) * C], Am[:, u, :], odd(Xm[:, u, :], LEVELS[n]),
                                     start=True, stop=True)
                    m.then_inc(sig("r_AX"), 1)
                    for u in range(4 * g, 4 * g + 4):
                        m = T.transpose(ps[:, 6 + g, (u % 4) * P:(u % 4 + 1) * P], Xm[:, u, :], ident[:, :])
                    m.then_inc(sig("r_XT"), 1)
                if 1 <= n <= 3:
                    turn((vZ, kZ, bZ)[n - 1], n - 1)
                for g in range(2):
                    pe.wait_ge(sig("r_Y"), i * 10 + 2 * n + g + 1)
                    pe.wait_ge(sig("r_Z"), i * 10 + 2 * n + g + 1)
                    for u in range(4 * g, 4 * g + 4):
                        m = T.matmul(ps[:, 2 + g, (u % 4) * C:(u % 4 + 1) * C], Zm[:, u, :], Ym[:, u, :], start=True, stop=True)
                    m.then_inc(sig("r_XY"), 1)
            pe.wait_ge(sig("r_t"), i * 3 + 3)
            for c in range(NC):
                for j in range(2):
                    u, js = j * NC + c, slice(j * C, (j + 1) * C)
                    m = T.matmul(ps[:, 6, js], Bm[:, u, :], Vt[:, u, :], start=j == 0, stop=c == 0, skip_group_check=True)
                if c:
                    pe.wait_ge(sig("r_S"), i * 3 + c)
                    for j in range(2):
                        m = T.matmul(ps[:, 6, j * C:(j + 1) * C], kkZ[:, j * NC + c, :], Sc[:, j, :], start=False, stop=True,
                                     skip_group_check=True)
                m.then_inc(sig("r_W"), 1)
                if c < NC - 1:
                    for j in range(2):
                        u, js = j * NC + c, slice(j * C, (j + 1) * C)
                        T.matmul(ps[:, 0, js], KtZ[:, u, :], Vt[:, u, :], start=j == 0, stop=False, skip_group_check=True)
                if c == 0:
                    pe.wait_ge(sig("r_x"), i * 12 + 12)
                pe.wait_ge(sig("r_Wc"), i * NC + c + 1)
                for j in range(2):
                    m = T.matmul(ps[:, 7, j * C:(j + 1) * C], Xm[:, j * NC + c, :], Wc[:, j, :], start=True, stop=True)
                m.then_inc(sig("r_U"), 1)
                if c:
                    pe.wait_ge(sig("r_SZ"), i * 3 + c)
                if c >= 2:
                    pe.wait_ge(sig("r_y_out"), i * NC + c - 1 + CREDIT)
                for j in range(2):
                    u = j * NC + c
                    T.matmul(ps[:, 2 + c % 2, j * C:(j + 1) * C], VtZ[:, u, :], Qk[:, u, :], start=j == 0, stop=False,
                             skip_group_check=True)
                    if c:
                        T.matmul(ps[:, 2 + c % 2, j * C:(j + 1) * C], SZ[:, j, :], rt_[:, j, c * C:(c + 1) * C],
                                 start=False, stop=False, skip_group_check=True)
                pe.wait_ge(sig("r_Uc"), i * NC + c + 1)
                if c < NC - 1:
                    for j in range(2):
                        m = T.matmul(ps[:, 0, j * C:(j + 1) * C], BtZ[:, j * NC + c, :], Uc[:, j, :], start=False, stop=True,
                                     skip_group_check=True)
                    m.then_inc(sig("r_dS"), 1)
                pe.wait_ge(sig("r_UZ"), i * NC + c + 1)
                for j in range(2):
                    m = T.matmul(ps[:, 2 + c % 2, j * C:(j + 1) * C], UZ[:, j, :], Qb[:, j * NC + c, :], start=False,
                                 stop=True, skip_group_check=True)
                m.then_inc(sig("r_y"), 1)

    def rec_act(act):
        with act.Fori(0, RW_T // 2) as i:
            act.wait_ge(sig("r_prep"), i + 1)
            act.wait_ge(sig("r_y"), i * NC + CREDIT)
            A.activation(rt_[:, :, :], rtn[:, :, :], ACT.Copy)
            A.activation(kkZ[HALVES[1], :, C:P], blk4(kkd[HALVES[1]]), ACT.Copy).then_inc(sig("r_kkZ_act"), 1)
            for p, r in enumerate(HALVES):
                a = A.activation(vZ[r, :, p * C:(p + 1) * C], blk4(vq[r]), ACT.Copy)
            a.then_inc(sig("r_vZ"), 1)
            act.wait_ge(sig("r_Ap"), i + 1)
            A.activation(Am[:, :, :], banks(2, 2, P), ACT.Copy).then_inc(sig("r_A"), 1)
            for n in range(len(LEVELS)):
                for g in range(2):
                    act.wait_ge(sig("r_XT"), i * 10 + 2 * n + g + 1)
                    A.activation(Zm[:, 4 * g:4 * g + 4, :], bank(6 + g, P), ACT.Copy).then_inc(sig("r_Z"), 1)
                if 1 <= n <= 3:
                    act.wait_ge(sig("r_turned"), i * 3 + n)
                    if n == 1:
                        for p, r in enumerate(HALVES):
                            A.activation(Vt[r, :, :], banks(4, 2, P)[r, :, p * C:(p + 1) * C], ACT.Copy)
                    A.activation((VtZ, KtZ, BtZ)[n - 1][:, :, :], banks(4, 2, P), ACT.Copy).then_inc(sig("r_t"), 1)
            for c in range(NC):
                act.wait_ge(sig("r_Uc"), i * NC + c + 1)
                act.wait_ge(sig("r_y"), i * NC + c + CREDIT)
                for p, r in enumerate(HALVES):
                    a = A.activation(UZ[r, :, p * C:(p + 1) * C], bank(7, C)[r, 0:2, :], ACT.Copy, scale=-1.0)
                a.then_inc(sig("r_UZ"), 1)
                act.wait_ge(sig("r_y"), i * NC + c + 1 + CREDIT)
                A.activation(yR[:, bass.ds(i * 2, 2), c * C:(c + 1) * C], bank(2 + c % 2, C)[:, 0:2, :],
                             ACT.Copy).then_inc(sig("r_y_out"), 1)

    def rec_dve(dve):
        masks2 = [bc(msk(f"up{b}").unsqueeze(1), [P, 4, C]) for b in LEVELS]
        eye = bc(ident[:, :].unsqueeze(1), [P, 4, P])

        def step(i, last=False):
            two = bass.ds(i * 2, 2)
            v = rkv[:, bass.ds(i * 2 + 2 * RW_T, 2), :]
            dve.wait_ge(sig("r_prep"), i + 1)
            dve.wait_ge(sig("r_y_out"), i * NC + CREDIT)
            V.tensor_copy(Pe[:, :, :], Pn[:, :, :])
            V.tensor_copy(kkZ[HALVES[0], :, 0:C], blk4(kkd[HALVES[0]])).then_inc(sig("r_kkZ_dve"), 1)
            dve.wait_ge(sig("r_bonus"), i + 1)
            V.tensor_tensor(kkT[:, two, :], bank(7, S), v, ALU.mult).then_inc(sig("r_bonus_out"), 1)
            dve.wait_ge(sig("r_AT"), i + 1)
            V.tensor_tensor(Xm[:, :, :], banks(0, 2, P), bc(msk("neg_up1").unsqueeze(1), [P, 8, P]), ALU.mult)
            settle()
            for g in range(2):
                V.tensor_tensor(Xm[:, 4 * g:4 * g + 4, :], Xm[:, 4 * g:4 * g + 4, :], eye, ALU.add).then_inc(sig("r_x"), 1)
            incl = bc(msk("incl").unsqueeze(1), [P, 8, C])
            dve.wait_ge(sig("r_Qbp"), i + 1)
            V.tensor_tensor(Qb[:, :, :], bank(6, C), incl, ALU.mult)
            dve.wait_ge(sig("r_Qkp"), i + 1)
            V.tensor_tensor(Qk[:, :, :], bank(7, C), incl, ALU.mult).then_inc(sig("r_Q"), 1)
            for n in range(len(LEVELS)):
                for g in range(2):
                    dve.wait_ge(sig("r_AX"), i * 10 + 2 * n + g + 1)
                    if n == 0 and g == 0:
                        dve.wait_ge(sig("r_Ap"), i + 1)
                    V.tensor_tensor(Ym[:, 4 * g:4 * g + 4, :], bank(g, C)[:, 0:4, :], masks2[n], ALU.mult).then_inc(sig("r_Y"), 1)
                if n == 0:
                    dve.wait_ge(sig("r_Bmp"), i + 1)
                    V.tensor_tensor(Bm[:, :, :], banks(4, 2, P), bc(msk("strict").unsqueeze(1), [P, 8, P]),
                                    ALU.mult).then_inc(sig("r_gram_out"), 1)
                for g in range(2):
                    dve.wait_ge(sig("r_XY"), i * 10 + 2 * n + g + 1)
                    x = odd(Xm[:, 4 * g:4 * g + 4, :], LEVELS[n])
                    V.tensor_tensor(x, x, bank(2 + g, C)[:, 0:4, :].rearrange("p u (q b) -> p u q b", b=LEVELS[n]),
                                    ALU.subtract).then_inc(sig("r_x"), 1)
                if n < 3 and not last:
                    if n == 0:
                        dve.wait_ge(sig("r_scan_in"), i + 2)
                    x = scan(part=n)
                    if n == 2:
                        x.then_inc(sig("r_scan"), 1)
            for c in range(NC):
                dve.wait_ge(sig("r_W"), i * NC + c + 1)
                V.tensor_copy(Wc[:, :, :], bank(6, C)[:, 0:2, :]).then_inc(sig("r_Wc"), 1)
                if 0 < c < NC - 1:
                    V.tensor_tensor(Sp[:, :, :], Sc[:, :, :], bc(Pe[:, :, c:c + 1], [P, 2, C]), ALU.mult)
                dve.wait_ge(sig("r_U"), i * NC + c + 1)
                V.tensor_scalar(Uc[:, :, :], bank(7, C)[:, 0:2, :], -1.0, None, ALU.mult).then_inc(sig("r_Uc"), 1)
                if c < NC - 1:
                    dve.wait_ge(sig("r_dS"), i * 3 + c + 1)
                    pe_ = bc(Pe[:, :, c:c + 1], [P, 2, C])
                    if c == 0:
                        V.tensor_tensor(Sc[:, :, :], bank(0, C)[:, 0:2, :], pe_, ALU.mult).then_inc(sig("r_S"), 1)
                    else:
                        for j in range(2):
                            x = V.scalar_tensor_tensor(out=Sc[:, j, :], in0=ps[:, 0, j * C:(j + 1) * C],
                                                       scalar=Pe[:, j, c:c + 1], in1=Sp[:, j, :], op0=ALU.mult, op1=ALU.add)
                        x.then_inc(sig("r_S"), 1)
                    settle()
                    dve.wait_ge(sig("r_y"), i * NC + c + 1 + CREDIT)
                    for p, rr in enumerate(HALVES):
                        x = V.tensor_copy(SZ[rr, :, p * C:(p + 1) * C], Sc[rr, :, :])
                    x.then_inc(sig("r_SZ"), 1)

        with dve.Fori(0, RW_T // 2 - 1) as i:
            step(i)
        step(RW_T // 2 - 1, last=True)

    STEPS = RW_T // 2
    A_SLABS = 3 * STEPS
    NSA_READY = 2

    def out_slab(pe, s):
        if s < A_SLABS:
            c, m, first, last = s % 3, STEPS + s // 3, s < 3, False
            pe.wait_ge(y_lo_ready, 1 + s // 6)
        elif s < 2 * A_SLABS:
            c, m, first, last = (s - A_SLABS) // STEPS, (s - A_SLABS) % STEPS, False, s % STEPS == STEPS - 1
            pe.wait_ge(y_lo_ready, NSA_READY + m + 1)
        else:
            c, m, first, last = 3, s - 2 * A_SLABS, s == 2 * A_SLABS, s == 2 * PAIR - 1
        slab_products(pe, S_OUT, None, 0, s, x_hi, x_lo, (2 * m, 2 * m + 1), NCH, 2 * (c % 3), first, last)

    def out_pe(pe):
        pe.wait_ge(sig("r_y_out"), STEPS * NC + CREDIT)
        pe.wait_ge(loraw_in, 48)
        for q in range(STEPS):
            two = slice(2 * q, 2 * q + 2)
            if q:
                pe.wait_ge(sig("n_y"), q)
            T.matmul(ps[:, 6, :], msk("bmean"), yR[:, two, :].rearrange("p j t -> p (j t)"), start=True,
                     stop=True).then_inc(sig("n_mean"), 1)
            out_slab(pe, 3 * q)
            pe.wait_ge(sig("n_sq"), q + 1)
            for j in range(2):
                for tt in range(TT):
                    c0 = 2 * (2 * j + tt)
                    m = T.matmul(ps[:, 7, c0:c0 + 2], sqb[:, j, tt * P:(tt + 1) * P], msk("hsel")[:, 0:2], start=True,
                                 stop=True)
            m.then_inc(sig("n_var"), 1)
            out_slab(pe, 3 * q + 1)
            for j in range(2):
                acc, ch = ps[:, 6, j * S:(j + 1) * S], slice((2 * q + j) * P, (2 * q + j + 1) * P)
                T.matmul(acc, g_up[:, 0, ch], lora[:, 1, :], start=True, stop=False)
                T.matmul(acc, g_up[0:32, 1, ch], lora[0:32, 2, :], start=False, stop=True)
            pe.wait_ge(sig("n_rstd"), q + 1)
            for j in range(2):
                for tt in range(TT):
                    t = T.transpose(ps[:, 7, j * S + tt * P:j * S + (tt + 1) * P], rb[:, 2 * j + tt, :], ident[:, :])
            t.then_inc(sig("n_spread"), 1)
            out_slab(pe, 3 * q + 2)
        for s in range(A_SLABS, 2 * PAIR):
            if s == 2 * A_SLABS:
                pe.wait_ge(y_copied, Y_BASE["mix"] + 1 + CREDIT)
            out_slab(pe, s)

    def out_act(act):
        split_hi(act, S_OUT, None, 0, 0, SLAB)
        for n in range(2):
            A.activation(x_hi[:, RW_T + 4 * n:RW_T + 4 * n + 4, :], yN[:, 4 * n:4 * n + 4, :], ACT.Copy).then_inc(y_hi_ready, 1)
            split_hi(act, S_OUT, None, 0, 1 + n, SLAB)
        split_hi(act, S_OUT, None, 0, 3, SLAB)
        root_tables()
        for q in range(STEPS):
            split_hi(act, S_OUT, None, 0, 3 * q + 4, SLAB)
            act.wait_ge(sig("n_ms"), q + 1)
            A.activation(s4[:, 1, :], s4[:, 0, :], ACT.Sqrt).then_inc(sig("n_root"), 1)
            split_hi(act, S_OUT, None, 0, 3 * q + 5, SLAB)
            act.wait_ge(sig("n_y"), q + 1)
            A.activation(x_hi[:, 2 * q:2 * q + 2, :], yR[:, 2 * q:2 * q + 2, :], ACT.Copy).then_inc(y_hi_ready, 1)
            split_hi(act, S_OUT, None, 0, 3 * q + 6, SLAB)
        for k in range(A_SLABS + 4, 2 * PAIR):
            split_hi(act, S_OUT, None, 0, k, SLAB)
            if k >= 21 and k % 4 == 1:
                square_y(act, y_b, Y_BASE["mix"], None, k // 4 - 5)
        square_y(act, y_b, Y_BASE["mix"], None, 3)

    def out_dve(dve):
        def rest(n, src, dst):
            dve.wait_ge(y_hi_ready, n)
            V.tensor_tensor(x_lo[:, dst, :], src, x_hi[:, dst, :].bitcast(F32), ALU.subtract).then_inc(y_lo_ready, 1)

        split_lo(dve, S_OUT, None, 0, 0, SLAB)
        for n in range(2):
            rest(n + 1, yN[:, 4 * n:4 * n + 4, :], slice(RW_T + 4 * n, RW_T + 4 * n + 4))
            split_lo(dve, S_OUT, None, 0, 1 + n, SLAB)
        for q in range(STEPS):
            y = yR[:, 2 * q:2 * q + 2, :]
            dve.wait_ge(sig("n_mean"), q + 1)
            V.tensor_tensor(y, y, bank(6, S), ALU.subtract)
            settle()
            V.tensor_tensor(sqb[:, :, :], y, y, ALU.mult).then_inc(sig("n_sq"), 1)
            split_lo(dve, S_OUT, None, 0, 3 * q + 3, SLAB)
            dve.wait_ge(sig("n_var"), q + 1)
            V.tensor_scalar(s4[:, 0, :], ps[:, 7, 0:8], 1.0 / HD, GN_EPS, ALU.mult, ALU.add).then_inc(sig("n_ms"), 1)
            dve.wait_ge(sig("n_root"), q + 1)
            V.reciprocal(s4[:, 2, :], s4[:, 1, :])
            settle()
            V.tensor_copy(rb[:, :, :].rearrange("p b (h d) -> p (b h) d", h=2), bc(s4[:, 2, :].unsqueeze(2), [P, 8, HD])
                          ).then_inc(sig("n_rstd"), 1)
            split_lo(dve, S_OUT, None, 0, 3 * q + 4, SLAB)
            dve.wait_ge(sig("n_spread"), q + 1)
            V.tensor_tensor(y, y, bank(7, S), ALU.mult)
            settle()
            for j in range(2 * q, 2 * q + 2):
                V.tensor_scalar(yR[:, j, :], yR[:, j, :], col("ln_w", j), col("ln_b", j), ALU.mult, ALU.add)
            settle()
            V.tensor_tensor(y, y, kkT[:, 2 * q:2 * q + 2, :], ALU.add)
            settle()
            V.tensor_tensor(y, y, bank(6, S), ALU.mult).then_inc(sig("n_y"), 1)
            split_lo(dve, S_OUT, None, 0, 3 * q + 5, SLAB)
            rest(3 + q, y, slice(2 * q, 2 * q + 2))
        for k in range(A_SLABS + 3, 2 * PAIR):
            split_lo(dve, S_OUT, None, 0, k, SLAB)
            if k >= 19 and k % 4 == 3 and k < 31:
                used(dve, S_OUT, None, 0, k - 4)
                copy_y(dve, y_b, None, k // 4 - 4, bank=2 * (k // 4 - 4))
        used(dve, S_OUT, None, 0, 2 * PAIR - 1)
        copy_y(dve, y_b, None, 3, bank=0)
        settle()

    def pe_fn(pe):
        in_pe(pe)
        pre_pe(pe)
        nsa_pe(pe)
        rec_pe(pe)
        out_pe(pe)

    def act_fn(act):
        in_act(act)
        pre_act(act)
        nsa_act(act)
        rec_act(act)
        out_act(act)

    def dve_fn(dve):
        in_dve(dve)
        pre_dve(dve)
        nsa_dve(dve)
        kk_dve(dve)
        rec_dve(dve)
        out_dve(dve)

    return {"pe": pe_fn, "act": act_fn, "dve": dve_fn, "pool": pool_fn}


def memory_attention(nc, e):
    (ps, ident, qs, mqT, mp, mpT, memKT, memV, stat, x_hi, x_lo, y_b) = (e[n] for n in (
        "ps", "ident", "qs", "mqT", "mp", "mpT", "memKT", "memV", "stat", "x_hi", "x_lo", "y_b"))
    (sig, split_hi, split_lo, slab_products, chunk_products, used, square_y, copy_y, y_copied, y_squared, Y_BASE) = (
        e[n] for n in ("sig", "split_hi", "split_lo", "slab_products", "chunk_products", "used", "square_y", "copy_y",
                       "y_copied", "y_squared", "Y_BASE"))
    V, A, T = nc.vector, nc.scalar, nc.tensor
    SCALE = float(MEM_W // MH) ** -0.5
    AHEAD = e["AHEAD"]

    def banks(n, m, w):
        return ps[:, n:n + m, :].rearrange("p a (b w) -> p (a b) w", w=w)

    def bank(n):
        return ps[:, n, :].rearrange("p (a t) -> p a t", t=S)

    def pe_fn(pe):
        chunk_products(pe, S_MQ, None, 0, 0, NCH, 0, fresh=3)
        pe.wait_ge(sig("mq_rows"), 1)
        for a in range(MH):
            for tt in range(TT):
                t = T.transpose(ps[:, 2 + a // 2, (a % 2) * S + tt * P:(a % 2) * S + (tt + 1) * P],
                                qs[:, tt, a * P:(a + 1) * P], ident[:, :])
        t.then_inc(sig("mq_turned"), 1)
        pe.wait_ge(sig("mq_T"), 1)
        for tt in range(TT):
            for a in range(MH):
                m = T.matmul(ps[:, 4 + 2 * tt + a // 2, (a % 2) * S:(a % 2 + 1) * S], mqT[:, a, tt * P:(tt + 1) * P],
                             memKT[:, a, :], start=True, stop=True)
            m.then_inc(sig("m_scores"), 1)
        for tt in range(TT):
            pe.wait_ge(sig("m_probs"), tt + 1)
            for a in range(MH):
                for kb in range(2):
                    t = T.transpose(ps[:, a, kb * S + tt * P:kb * S + (tt + 1) * P], mp[:, tt, a, kb * P:(kb + 1) * P],
                                    ident[:, :])
        t.then_inc(sig("m_turned"), 1)
        pe.wait_ge(sig("m_pT"), 1)
        for a in range(MH):
            for kb in range(2):
                m = T.matmul(ps[:, 4 + a // 2, (a % 2) * S:(a % 2 + 1) * S], memV[:, kb, a * P:(a + 1) * P],
                             mpT[:, a, kb, :], start=kb == 0, stop=kb == 1)
        m.then_inc(sig("m_o"), 1)
        b = Y_BASE["mem"]
        for c in range(4):
            if c >= 2:
                pe.wait_ge(y_copied, b + c - 1 + CREDIT)
            for m in range(2):
                pe.wait_ge(sig("m_o_lo"), m + 1)
                slab_products(pe, S_MO, None, 0, 2 * c + m, x_hi, x_lo, (2 * m, 2 * m + 1), NCH, 2 * (c % 2), m == 0, m == 1)

    def act_fn(act):
        for k in range(AHEAD, 8):
            split_hi(act, S_MQ, None, 0, k, SLAB)
        used(act, S_MQ, None, 0, 7)
        for tt in range(TT):
            a = A.activation(qs[:, tt, :], ps[:, tt, :], ACT.Copy, scale=e["rstd"](3, tt))
        a.then_inc(sig("mq_rows"), 1)
        act.wait_ge(sig("mq_turned"), 1)
        A.activation(mqT[:, :, :], banks(2, 2, S), ACT.Copy).then_inc(sig("mq_T"), 1)
        for tt in range(TT):
            act.wait_ge(sig("m_max"), tt + 1)
            for n in range(MH):
                c = 34 + 4 * tt + n
                a = A.activation(mp[:, tt, n, :], ps[:, 4 + 2 * tt + n // 2, (n % 2) * S:(n % 2 + 1) * S], ACT.Exp,
                                 scale=SCALE, bias=stat[:, c:c + 1], accum_out=stat[:, c + 8:c + 9])
            a.then_inc(sig("m_exp"), 1)
        for k in range(2):
            split_hi(act, S_MO, None, 0, k, SLAB)
        act.wait_ge(sig("m_turned"), 1)
        A.activation(mpT[:, :, :, :].rearrange("p a k t -> p (a k) t"), banks(0, 4, S), ACT.Copy).then_inc(sig("m_pT"), 1)
        e["root_tables"]()
        for k in range(2, 4):
            split_hi(act, S_MO, None, 0, k, SLAB)
        act.wait_ge(sig("m_o"), 1)
        for n in range(2):
            A.activation(x_hi[:, 2 * n:2 * n + 2, :], bank(4 + n), ACT.Copy).then_inc(sig("m_o_hi"), 1)
        for k in range(4, 8):
            split_hi(act, S_MO, None, 0, k, SLAB)
        for c in range(4):
            square_y(act, y_b, Y_BASE["mem"], None, c)

    def dve_fn(dve):
        for k in range(AHEAD, 8):
            split_lo(dve, S_MQ, None, 0, k, SLAB)
        for tt in range(TT):
            c = 4 * tt
            dve.wait_ge(sig("m_scores"), tt + 1)
            V.tensor_reduce(stat[:, 50 + c:54 + c], banks(4 + 2 * tt, 2, S), AX.X, ALU.max)
            V.drain()
            V.tensor_scalar(stat[:, 34 + c:38 + c], stat[:, 50 + c:54 + c], -SCALE, None, ALU.mult).then_inc(sig("m_max"), 1)
        for tt in range(TT):
            c = 4 * tt
            dve.wait_ge(sig("m_exp"), tt + 1)
            V.reciprocal(stat[:, 50 + c:54 + c], stat[:, 42 + c:46 + c])
            V.drain()
            V.tensor_tensor(mp[:, tt], mp[:, tt], bc(stat[:, 50 + c:54 + c].unsqueeze(2), [P, MH, S]),
                            ALU.mult).then_inc(sig("m_probs"), 1)
        for k in range(4):
            split_lo(dve, S_MO, None, 0, k, SLAB)
        for n in range(2):
            dve.wait_ge(sig("m_o_hi"), n + 1)
            V.tensor_tensor(x_lo[:, 2 * n:2 * n + 2, :], bank(4 + n), x_hi[:, 2 * n:2 * n + 2, :].bitcast(F32),
                            ALU.subtract).then_inc(sig("m_o_lo"), 1)
        for k in range(4, 8):
            split_lo(dve, S_MO, None, 0, k, SLAB)
            if k in (5, 7):
                c = (k - 5) // 2
                used(dve, S_MO, None, 0, 2 * c + 1)
                copy_y(dve, y_b, None, c)
        for c in (2, 3):
            used(dve, S_MO, None, 0, 2 * c + 1)
            for tt in range(TT):
                x = V.tensor_copy(y_b[:, tt, c * NCH:(c + 1) * NCH], ps[:, 2 * (c % 2) + tt, :])
            x.then_inc(y_copied, 1)
        V.drain()

    return {"pe": pe_fn, "act": act_fn, "dve": dve_fn}



def build(nc, A, out):
    with ExitStack() as ctx:
        base = (nc.sbuf_base + 63) // 64 * 64
        end = nc.sbuf_usable_end
        ctx.enter_context(nc.sbuf_tensor("arena", [P, (end - base - 64) // 4], F32))

        def at(name, shape, offset, dt=F32):
            size = 4 * int(np.prod(shape[1:]))
            assert base + offset + size <= end, (name, base + offset + size, end)
            return nc.alloc_sbuf_tensor_at(name, shape, dt, offset=base + offset)

        o = 0

        def keep(name, shape, dt=F32):
            nonlocal o
            t = at(name, shape, o, dt)
            o += (4 * int(np.prod(shape[1:])) + 31) // 32 * 32
            return t

        raw = keep("raw", [P, RING, SLAB])
        w_hi = keep("w_hi", [P, RING, SLAB], F32R)
        w_lo = keep("w_lo", [P, RING, SLAB], F32R)
        h = keep("h", [P, TT, D])
        memKT = keep("memKT", [P, MH, S])
        memV = keep("memV", [P, TT, MEM_W])
        ident = keep("ident", [P, P])
        cols = keep("cols", [P, NCOLS])
        stat = keep("stat", [P, 80])
        x_hi = keep("x_hi", [P, DK, S], F32R)
        x_lo = keep("x_lo", [P, DK, S], F32R)
        XT = o - 2 * 4 * DK * S
        BIG = o

        hT_hi = at("hT_hi", [P, FK, S], BIG, F32R)
        hT_lo = at("hT_lo", [P, FK, S], BIG + 44032, F32R)
        sg = at("sg", [P, TT, NCH], BIG + 88064)
        prod = at("prod", [P, TT, NCH], BIG + 92160)
        gain = at("gain", [P, D], BIG + 88064)
        y_x = at("y_x", [P, TT, D], XT)
        y_b = at("y_b", [P, TT, D], BIG)
        y_last = at("y_last", [P, TT, NCH], BIG + 96256)
        squares = at("squares", [P, TT, D], BIG + 46592)
        mem_sb = at("mem_sb", [P, TT, D], BIG + 62976)
        k_rows = at("k_rows", [P, TT, MEM_W], BIG)

        W0 = 4 * RING * SLAB
        mc = at("mc", [P, NMC], BIG)
        R0 = BIG + 13824
        assert 4 * NMC <= 13824
        rkv = at("rkv", [P, 3 * RW_T, S], R0)
        yN = at("yN", [P, RW_T, S], R0 + 24576)
        lora = at("lora", [P, 3, S], R0 + 32768)
        F0 = R0 + 35840
        nf = at("nf", [P, TT, NSA_W], F0)
        T0 = F0 + 20864
        shb = at("shb", [P, 4, S + 1], T0)
        dif = at("dif", [P, 4, S], T0 + 4128)
        fst = at("fst", [P, TT, NCH], T0 + 8224)
        w1 = at("w1", [P, 2, 16, P], T0 + 12320)
        w2 = at("w2", [P, 3, HD], T0 + 28704)
        vblk = at("vblk", [P, G, 4, HD], XT + 28672)
        kdup = at("kdup", [P, 2, TT, G, 2, HD], R0 + 24576)
        kc2 = at("kc2", [P, 2, G + 1, S], W0 + 5632)
        hid = at("hid", [P, 8, 64], XT + 12288)
        hidrep = at("hidrep", [P, G, 4, 32], XT + 14336)
        qn = at("qn", [P, TT, 4, HD], XT)
        qr = at("qr", [P, TT, 4, HD], XT + 2048)
        kk2 = at("kk2", [P, 2, TT, 2, HD], XT + 4096)
        vv = at("vv", [P, 2, TT, HD], XT + 6144)
        qnT = at("qnT", [P, 2, S], XT + 7168)
        qrT = at("qrT", [P, 2, S], XT + 9216)
        kT = at("kT", [P, 2, S], XT + 11264)
        p0 = at("p0", [P, 2, 4, P], XT + 13312)
        p1 = at("p1", [P, 2, 4, S], XT + 17408)
        pc = at("pc", [P, TT, 4, 32], XT + 25600)
        pcT = at("pcT", [P, S], XT + 26624)
        vbg = at("vbg", [P, 4, HD], XT + 27648)
        pT0 = at("pT0", [P, 2, 4, S], T0 + 20512)
        pT1 = at("pT1", [P, 2, 4, P], T0 + 8192)
        kcT = at("kcT", [P, G, 16], W0 + 5120)
        kcg = at("kcg", [P, 16], W0 + 5376)
        hb = at("hb", [P, 2], W0 + 5440)
        qrot = at("qrot", [P, TT, 16, 16], W0)
        rt = at("rt", [P, 4, 16, ROPE_H], W0 + 2048)
        gates = at("gates", [P, TT, 48], W0 + 4096)
        gg = at("gg", [P, TT, 3, 4], W0 + 4480)
        sm = at("sm", [P, 2, 4, 8], W0 + 4608)
        smc = at("smc", [P, 4, 8], W0 + 4864)

        kkT = at("kkT", [P, RW_T, S], T0 + 12320)
        aT = at("aT", [P, RW_T, S], 8 * RING * SLAB)
        wT = at("wT", [P, RW_T, S], 8 * RING * SLAB + 8192)
        yR = at("yR", [P, RW_T, S], F0)
        g_up = at("g_up", [P, 2, RW_W], F0 + 8192)
        L0 = T0 + 20512
        wa_up = at("wa_up", [P, RW_W], T0 + 29472)
        Am = at("Am", [P, 8, P], W0)
        Zm = at("Zm", [P, 8, P], W0 + 4096)
        Ym = at("Ym", [P, 8, C], W0 + 8192)
        vq = at("vq", [P, 2, S], W0 + 10240)
        bon = at("bon", [P, 2, S], W0 + 12288)
        Sp = at("Sp", [P, 2, C], W0 + 14336)
        sq8 = at("sq8", [P, RW_T, S], W0 + 8192)
        nrm = at("nrm", [16, 3, S], T0 + 29472)
        bZ = at("bZ", [P, 8, P], XT)
        kZ = at("kZ", [P, 8, P], XT + 4096)
        vZ = at("vZ", [P, 8, P], XT + 8192)
        kkZ = at("kkZ", [P, 8, P], XT + 12288)
        VtZ = at("VtZ", [P, 8, P], XT + 16384)
        KtZ = at("KtZ", [P, 8, P], XT + 20480)
        BtZ = at("BtZ", [P, 8, P], XT + 24576)
        Xm = at("Xm", [P, 8, P], XT + 28672)
        Pd = at("Pd", [P, 2, S], F0 + 16384)
        iP = at("iP", [P, 2, S], F0 + 18432)
        Bm = at("Bm", [P, 8, P], L0)
        kp = at("kp", [P, 2, S], F0 + 20480)
        tmp = at("tmp", [P, 2, S], F0 + 22528)
        rtn = at("rtn", [P, 2, S], F0 + 24576)
        kkd = at("kkd", [P, 2, S], F0 + 26624)
        Pn = at("Pn", [P, 2, NC], F0 + 28672)
        sqb = at("sqb", [P, 2, S], F0 + 18944)
        rb = at("rb", [P, 4, P], F0 + 20992)
        s4 = at("s4", [P, 4, 8], F0 + 23040)
        rt_ = at("rt_", [P, 2, S], L0 + 4096)
        Vt = at("Vt", [P, 8, C], L0 + 6144)
        Qb = at("Qb", [P, 8, C], L0 + 8192)
        Qk = at("Qk", [P, 8, C], L0 + 10240)
        UZ = at("UZ", [P, 2, P], L0 + 12288)
        Pe = at("Pe", [P, 2, NC], L0 + 13312)
        Sc = at("Sc", [P, 2, C], F0 + 28704)
        SZ = at("SZ", [P, 2, P], F0 + 29216)
        Wc = at("Wc", [P, 2, C], F0 + 30240)
        Uc = at("Uc", [P, 2, C], F0 + 30752)

        qs = at("qs", [P, TT, MEM_W], BIG)
        mqT = at("mqT", [P, MH, S], BIG + 4096)
        mp = at("mp", [P, TT, MH, S], BIG + 8192)
        mpT = at("mpT", [P, MH, 2, S], BIG + 16384)

        ps = ctx.enter_context(nc.psum_tensor("ps", [P, 8, NCH], F32))

        def sem(name):
            return ctx.enter_context(nc.semaphore(name))

        slab_in = [sem(f"slab_in{n}") for n in range(RING)]
        hi_ready = sem("hi_ready")
        lo_ready = sem("lo_ready")
        slab_used = sem("slab_used")
        x_in, mem_in = sem("x_in"), [sem(f"mem_in{k}") for k in range(4)]
        ident_in, cols_in = sem("ident_in"), sem("cols_in")
        mc_in, w1_in, loraw_in, gain_in = sem("mc_in"), sem("w1_in"), sem("loraw_in"), sem("gain_in")
        out_done = sem("out_done")
        sq_ready = sem("sq_ready")
        ms_ready = sem("ms_ready")
        root_ready = sem("root_ready")
        x_turned = sem("x_turned")
        x_hi_ready, x_lo_ready = sem("x_hi_ready"), sem("x_lo_ready")
        kv_rows = sem("kv_rows")
        k_turned = sem("k_turned")
        mem_kv_ready = sem("mem_kv_ready")
        gate_ready = sem("gate_ready")
        prod_ready = sem("prod_ready")
        prod_turned = sem("prod_turned")
        hT_hi_ready, hT_lo_ready = sem("hT_hi_ready"), sem("hT_lo_ready")
        y_squared, y_copied = sem("y_squared"), sem("y_copied")
        h_ready = sem("h_ready")
        feat_rows = sem("feat_rows")
        feat_turned = sem("feat_turned")
        feat_T = sem("feat_T")
        shifted = sem("shifted")
        y_hi_ready, y_lo_ready = sem("y_hi_ready"), sem("y_lo_ready")

        made = {}

        def sig(name):
            if name not in made:
                made[name] = sem(name)
            return made[name]

        def col(name, n=0, w=1):
            return cols[:, COLS[name] + n:COLS[name] + n + w]

        def msk(name):
            a, n = MC[name]
            return mc[:, a:a + n]

        turn_rest = {}

        def load_slab(sp, s0, reg, step, k, src, width):
            s = s0 + k
            shift = 0 if reg is None else reg * step
            if reg is not None or s >= RING:
                sp.wait_ge(lo_ready, shift + (s - RING + 1))
            sp.dma_start(raw[:, s % RING, 0:width], src).then_inc(slab_in[s % RING], 16)

        def split_hi(act, s0, reg, step, k, width):
            s = s0 + k
            act.wait_ge(slab_in[s % RING],
                        16 * (s // RING + 1) + (0 if reg is None else reg * (16 * step // RING)))
            if reg is not None or s >= RING:
                act.wait_ge(slab_used, (0 if reg is None else reg * step) + (s - RING + 1))
            nc.scalar.activation(w_hi[:, s % RING, 0:width], raw[:, s % RING, 0:width], ACT.Copy).then_inc(hi_ready, 1)

        def split_lo(dve, s0, reg, step, k, width):
            s = s0 + k
            dve.wait_ge(hi_ready, (0 if reg is None else reg * step) + s + 1)
            nc.vector.tensor_tensor(w_lo[:, s % RING, 0:width], raw[:, s % RING, 0:width],
                                    w_hi[:, s % RING, 0:width].bitcast(F32), ALU.subtract).then_inc(lo_ready, 1)

        def slab_products(pe, s0, reg, step, k, hi, lo, kts, width, bank, first, last, fresh=None):
            s = s0 + k
            if fresh is not None:
                pe.wait_ge(x_lo_ready, DK * fresh + kts[-1] + 1)
            pe.wait_ge(lo_ready, (0 if reg is None else reg * step) + s + 1)
            for n, kt in enumerate(kts):
                wh = w_hi[:, s % RING, n * width:(n + 1) * width]
                wl = w_lo[:, s % RING, n * width:(n + 1) * width]
                for tt in range(TT):
                    acc = ps[:, bank + tt, 0:width]
                    xh = hi[:, kt, tt * P:(tt + 1) * P]
                    begin, finish = first and n == 0, last and n == len(kts) - 1
                    nc.tensor.matmul(acc, xh, wh, start=begin, stop=False)
                    nc.tensor.matmul(acc, xh, wl, start=False, stop=False)
                    mm = nc.tensor.matmul(acc, lo[:, kt, tt * P:(tt + 1) * P], wh, start=False, stop=finish)
            mm.then_inc(slab_used, 1)
            if fresh is not None and kts[-1] in (1, 3):
                turn_rest[fresh](6 + kts[-1] // 2)

        def used(eng, s0, reg, step, k):
            eng.wait_ge(slab_used, (0 if reg is None else reg * step) + s0 + k + 1)

        def chunk_products(pe, s0, reg, step, k0, width, bank, fresh=None):
            for m in range(DK // 2):
                slab_products(pe, s0, reg, step, k0 + m, x_hi, x_lo, (2 * m, 2 * m + 1), width, bank,
                              m == 0, m == DK // 2 - 1, fresh)

        HALF = [(tt, f) for tt in range(TT) for f in range(2)]
        N_BANKS = (4, 5, 6, 7, 2, 3)
        AHEAD = RING

        def rstd(n, tt):
            c = 64 + 2 * n + tt
            return stat[:, c:c + 1]

        def norm_sums_act(act, n, src, half_ready):
            for k, (tt, f) in enumerate(HALF):
                half_ready(k)
                cs = slice(f * (D // 2), (f + 1) * (D // 2))
                nc.scalar.activation(squares[:, tt, cs], src[:, tt, cs], ACT.Square,
                                     accum_out=stat[:, k:k + 1]).then_inc(sq_ready, 1)
            act.wait_ge(ms_ready, n + 1)
            nc.scalar.activation(stat[:, 8:10], stat[:, 4:6], ACT.Sqrt).then_inc(root_ready, 1)
            act.wait_ge(rstd_ready, n + 1)

        def norm_rstd_dve(dve, n):
            dve.wait_ge(sq_ready, 4 * (n + 1))
            nc.vector.tensor_reduce(stat[:, 10:12], stat[:, 0:4].rearrange("p (t f) -> p t f", f=2), AX.X, ALU.add)
            nc.vector.drain()
            nc.vector.tensor_scalar(stat[:, 4:6], stat[:, 10:12], 1.0 / D, EPS, ALU.mult, ALU.add).then_inc(ms_ready, 1)
            dve.wait_ge(root_ready, n + 1)
            nc.vector.reciprocal(stat[:, 64 + 2 * n:66 + 2 * n], stat[:, 8:10]).then_inc(rstd_ready, 1)
            nc.vector.drain()

        def norm_turn_act(act, n, gname, s0, done=0):
            for b in range(DK // 2):
                if b in (3, 4, 5, 6) and b - 3 >= done:
                    split_hi(act, s0, None, 0, b - 3, SLAB)
                if n == 2 and b in (1, 2):
                    act.wait_ge(h_ready, 2 * b + 1)
                act.wait_ge(x_turned, 8 * n + b + 1)
                for m in range(2):
                    kt = 2 * b + m
                    nc.scalar.activation(x_hi[:, kt, :], ps[:, N_BANKS[b % 6], m * S:(m + 1) * S], ACT.Copy,
                                         scale=col(gname, kt)).then_inc(x_hi_ready, 1)

        def norm_turn_dve(dve, n, gname, s0):
            for kt in range(DK):
                if kt >= 2 and kt % 4 == 2:
                    split_lo(dve, s0, None, 0, kt // 4, SLAB)
                dve.wait_ge(x_hi_ready, DK * n + 2 * (kt // 2) + 2)
                b = N_BANKS[kt // 2 % 6]
                nc.vector.scalar_tensor_tensor(out=x_lo[:, kt, :], in0=ps[:, b, (kt % 2) * S:(kt % 2 + 1) * S],
                                               scalar=col(gname, kt), in1=x_hi[:, kt, :].bitcast(F32),
                                               op0=ALU.mult, op1=ALU.subtract).then_inc(x_lo_ready, 1)

        def norm_pe(pe, n, src, rows_ready):
            def turn_blocks(b):
                if b >= 6:
                    pe.wait_ge(x_lo_ready, DK * n + 2 * (b - 5))
                for m in range(2):
                    for tt in range(TT):
                        rows_ready(tt, 2 * b + m)
                        t = nc.tensor.transpose(ps[:, N_BANKS[b % 6], m * S + tt * P:m * S + (tt + 1) * P],
                                                src[:, tt, (2 * b + m) * P:(2 * b + m + 1) * P], ident[:, :])
                t.then_inc(x_turned, 1)

            for b in range(8):
                turn_blocks(b)
            turn_rest[n] = lambda b: None

        def residual_rows(pe, m):
            return lambda tt, kt: pe.wait_ge(h_ready, 8 * m + 2 * (kt // 4) + tt + 1)

        def square_y(act, y, base, reg, k):
            nc.scalar.drain()
            act.wait_ge(y_copied, (0 if reg is None else 2 * reg) + base + k + 1 + CREDIT)
            for tt in range(TT):
                idx = stat[:, bass.ds(16 + (0 if reg is None else 4 * reg) + 2 * k + tt, 1)]
                c0 = (0 if reg is None else reg * (2 * NCH)) + k * NCH
                a = nc.scalar.activation(ps[:, 6 + tt, :], y[:, tt, bass.ds(c0, NCH)], ACT.Square, accum_out=idx)
            a.then_inc(y_squared, 1)

        def copy_y(dve, y, reg, k, bank=None):
            bank = 2 * (k % 2) if bank is None else bank
            for tt in range(TT):
                c0 = (0 if reg is None else reg * (2 * NCH)) + k * NCH
                v = nc.vector.tensor_copy(y[:, tt, bass.ds(c0, NCH)], ps[:, bank + tt, :])
            v.then_inc(y_copied, 1)

        def scale_y(pool, m, y):
            pool.wait_ge(gain_in, 16 * (m + 1))
            for k in range(3):
                pool.wait_ge(y_squared, 4 * m + k + 1)
                for tt in range(TT):
                    c = slice(k * NCH, (k + 1) * NCH)
                    x = nc.gpsimd.tensor_tensor(y[:, tt, c], y[:, tt, c], gain[:, c], ALU.mult)
                x.then_inc(y_scaled, 1)

        def post_norm_dve(dve, m, y, half):
            dve.wait_ge(gain_in, 16 * (m + 1))
            for tt in range(TT):
                nc.vector.tensor_tensor(y_last[:, tt, :], y[:, tt, 3 * NCH:], gain[:, 3 * NCH:], ALU.mult)
            dve.wait_ge(y_squared, 4 * (m + 1))
            nc.vector.tensor_reduce(stat[:, 24:26], stat[:, 16:24].rearrange("p (n t) -> p t n", t=TT), AX.X, ALU.add)
            nc.vector.drain()
            nc.vector.tensor_scalar(stat[:, 26:28], stat[:, 24:26], 1.0 / D, EPS, ALU.mult, ALU.add).then_inc(y_ms, 1)
            dve.wait_ge(y_root, m + 1)
            nc.vector.reciprocal(stat[:, 30:32], stat[:, 28:30])
            nc.vector.drain()
            nc.vector.tensor_scalar(stat[:, 32:34], stat[:, 30:32], half, None, ALU.mult)
            nc.vector.drain()
            dve.wait_ge(y_scaled, 3 * (m + 1))
            for k in range(4):
                c = slice(k * NCH, (k + 1) * NCH)
                for tt in range(TT):
                    src = y[:, tt, c] if k < 3 else y_last[:, tt, :]
                    nc.vector.scalar_tensor_tensor(out=h[:, tt, c], in0=src, scalar=stat[:, 32 + tt:33 + tt],
                                                   in1=h[:, tt, c], op0=ALU.mult, op1=ALU.add).then_inc(h_ready, 1)
            nc.vector.drain()

        def root_tables():
            nc.scalar.activation(stat[:, 60:61], cols[:, 0:1], ACT.Square)
            nc.scalar.drain()
            nc.scalar.activation(stat[:, 61:62], stat[:, 60:61], ACT.Sqrt)

        def post_norm_act(act, m):
            act.wait_ge(y_ms, m + 1)
            nc.scalar.activation(stat[:, 28:30], stat[:, 26:28], ACT.Sqrt).then_inc(y_root, 1)

        def from_residual(act, m):
            return lambda k: act.wait_ge(h_ready, 8 * (m + 1))

        y_ms, y_root, y_scaled = sem("y_ms"), sem("y_root"), sem("y_scaled")
        rstd_ready = sem("rstd_ready")

        FFN_NORM = (1, 4)

        def ffn_pair_pe(pe, f, s0, i, reg, width):
            b = FFN_PAIRS * f
            n = reg if reg is not None else i
            for k in range(PAIR // 2):
                if k == 0 and (reg is not None or i > 0):
                    pe.wait_ge(gate_ready, n + b)
                slab_products(pe, s0, reg, PAIR, k, x_hi, x_lo, (2 * k, 2 * k + 1), width, 0, k == 0, k == 7,
                              fresh=FFN_NORM[f] if reg is None and n == 0 else None)
                if k == 4 and (reg is not None or i > 0):
                    turn_prod(pe, f, n, NCH // P)
            if reg is not None or i > 0:
                pe.wait_ge(prod_ready, n + b)
            for k in range(PAIR // 2):
                slab_products(pe, s0, reg, PAIR, 8 + k, x_hi, x_lo, (2 * k, 2 * k + 1), width, 2, k == 0, k == 7)

        def turn_prod(pe, f, n, blocks):
            b = FFN_PAIRS * f
            pe.wait_ge(prod_ready, n + b)
            pe.wait_ge(hT_lo_ready, n + (b - 1) + CREDIT)
            for tt in range(TT):
                for m in range(blocks):
                    t = nc.tensor.transpose(ps[:, 4 + tt, m * P:(m + 1) * P], prod[:, tt, m * P:(m + 1) * P], ident[:, :])
            t.then_inc(prod_turned, 1)

        def ffn_pair_act(act, f, s0, i, reg, width):
            n = reg if reg is not None else i
            for k in range(AHEAD if i == 0 else 0, PAIR):
                split_hi(act, s0, reg, PAIR, k, 2 * width)
                if k == 8 and (reg is not None or i > 0):
                    hT_hi_evict(act, f, n, NCH // P)
                if k == 11:
                    gate_act(act, f, s0, i, reg, width)

        def hT_hi_evict(act, f, n, blocks):
            act.wait_ge(prod_turned, n + FFN_PAIRS * f + CREDIT)
            for tt in range(TT):
                a = nc.scalar.activation(hT_hi[:, bass.ds((n - 1) * 4, blocks), tt * P:(tt + 1) * P],
                                         ps[:, 4 + tt, 0:blocks * P].rearrange("p (m t) -> p m t", t=P), ACT.Copy)
            a.then_inc(hT_hi_ready, 1)

        def gate_act(act, f, s0, i, reg, width):
            n = reg if reg is not None else i
            used(act, s0, reg, PAIR, 7)
            if reg is not None or i > 0:
                act.wait_ge(prod_ready, n + FFN_PAIRS * f)
            for tt in range(TT):
                a = nc.scalar.activation(sg[:, tt, 0:width], ps[:, tt, 0:width], ACT.Silu, scale=rstd(FFN_NORM[f], tt))
            a.then_inc(gate_ready, 1)

        def ffn_pair_dve(dve, f, s0, i, reg, width):
            n = reg if reg is not None else i
            for k in range(AHEAD if i == 0 else 0, PAIR):
                split_lo(dve, s0, reg, PAIR, k, 2 * width)
                if k == 3 and (reg is not None or i > 0):
                    make_prod(dve, f, s0, n, reg, -1, NCH)
                if k == 8 and (reg is not None or i > 0):
                    hT_lo_evict(dve, f, n, NCH // P)

        def make_prod(dve, f, s0, n, reg, last_slab, width):
            b = FFN_PAIRS * f
            dve.wait_ge(gate_ready, n + b)
            used(dve, s0, reg, PAIR, last_slab)
            dve.wait_ge(prod_turned, n + (b - 1) + CREDIT)
            for tt in range(TT):
                v = nc.vector.scalar_tensor_tensor(out=prod[:, tt, 0:width], in0=ps[:, 2 + tt, 0:width],
                                                   scalar=rstd(FFN_NORM[f], tt), in1=sg[:, tt, 0:width],
                                                   op0=ALU.mult, op1=ALU.mult)
            v.then_inc(prod_ready, 1)

        def hT_lo_evict(dve, f, n, blocks):
            dve.wait_ge(hT_hi_ready, n + FFN_PAIRS * f)
            for tt in range(TT):
                kt = bass.ds((n - 1) * 4, blocks)
                v = nc.vector.tensor_tensor(hT_lo[:, kt, tt * P:(tt + 1) * P],
                                            ps[:, 4 + tt, 0:blocks * P].rearrange("p (m t) -> p m t", t=P),
                                            hT_hi[:, kt, tt * P:(tt + 1) * P].bitcast(F32), ALU.subtract)
            v.then_inc(hT_lo_ready, 1)

        def pair_base(s0, i):
            return s0 + PAIR * i

        LASTP = FFN_PAIRS - 1

        def down_width(k):
            return (NCH if k % DOWN == DOWN - 1 else 2 * NCH)

        def ffn_sp(sp, s0, gu, gu_t, dn):
            for k in range(PAIR):
                load_slab(sp, s0, None, 0, k, gu[0, k], SLAB)
            with sp.Fori(1, LASTP) as i:
                for k in range(PAIR):
                    load_slab(sp, s0, i, PAIR, k, gu[bass.ds(i, 1), k].rearrange("a p w -> (a p) w"), SLAB)
            for k in range(PAIR):
                load_slab(sp, pair_base(s0, LASTP), None, 0, k, gu_t[k], 2 * TAIL_F)
            s1 = pair_base(s0, FFN_PAIRS)
            with sp.Fori(0, 2) as i:
                for k in range(2 * DOWN):
                    w = down_width(k)
                    load_slab(sp, s1, i, 2 * DOWN, k, dn[bass.ds(i, 1), k].rearrange("a p w -> (a p) w")[:, 0:w], w)

        def ffn_pe(pe, f, s0):
            ffn_pair_pe(pe, f, s0, 0, None, NCH)
            with pe.Fori(1, LASTP) as i:
                ffn_pair_pe(pe, f, s0, None, i, NCH)
            ffn_pair_pe(pe, f, pair_base(s0, LASTP), LASTP, None, TAIL_F)
            s1 = pair_base(s0, FFN_PAIRS)
            b = Y_BASE[f]
            last = FFN_PAIRS * (f + 1)
            pe.wait_ge(gate_ready, last)
            pe.wait_ge(hT_lo_ready, last - 1 + CREDIT)
            for c in range(4):
                if c >= 2:
                    pe.wait_ge(y_copied, b + c - 1 + CREDIT)
                for m in range(DOWN):
                    if c == 0 and m == 3:
                        turn_prod(pe, f, FFN_PAIRS, TAIL_F // P)
                    if c == 0 and m == (LASTP * NCH) // (2 * P):
                        pe.wait_ge(hT_lo_ready, last + CREDIT)
                    if c == 1 and m == 0:
                        pe.wait_ge(prod_ready, last)
                    kts = tuple(k for k in (2 * m, 2 * m + 1) if k < FK)
                    slab_products(pe, s1, None, 0, c * DOWN + m, hT_hi, hT_lo, kts, NCH, 2 * (c % 2),
                                  m == 0, m == DOWN - 1)

        def ffn_act(act, f, s0):
            ffn_pair_act(act, f, s0, 0, None, NCH)
            with act.Fori(1, LASTP) as i:
                ffn_pair_act(act, f, s0, None, i, NCH)
            ffn_pair_act(act, f, pair_base(s0, LASTP), LASTP, None, TAIL_F)
            s1 = pair_base(s0, FFN_PAIRS)
            for k in range(4 * DOWN):
                split_hi(act, s1, None, 0, k, down_width(k))
                if k == 3:
                    hT_hi_evict(act, f, FFN_PAIRS, TAIL_F // P)
                    root_tables()
                if k >= DOWN and k % DOWN == 5:
                    square_y(act, y_x, Y_BASE[f], None, k // DOWN - 1)
            square_y(act, y_x, Y_BASE[f], None, 3)

        def ffn_dve(dve, f, s0):
            ffn_pair_dve(dve, f, s0, 0, None, NCH)
            with dve.Fori(1, LASTP) as i:
                ffn_pair_dve(dve, f, s0, None, i, NCH)
            ffn_pair_dve(dve, f, pair_base(s0, LASTP), LASTP, None, TAIL_F)
            s1 = pair_base(s0, FFN_PAIRS)
            for k in range(4 * DOWN):
                split_lo(dve, s1, None, 0, k, down_width(k))
                if k == 1:
                    make_prod(dve, f, pair_base(s0, LASTP), FFN_PAIRS, None, PAIR - 1, TAIL_F)
                if k == 4:
                    hT_lo_evict(dve, f, FFN_PAIRS, TAIL_F // P)
                if k >= DOWN and k % DOWN == 3:
                    used(dve, s1, None, 0, k // DOWN * DOWN - 1)
                    copy_y(dve, y_x, None, k // DOWN - 1)
            used(dve, s1, None, 0, 4 * DOWN - 1)
            copy_y(dve, y_x, None, 3)
            nc.vector.drain()

        Y_BASE = {0: 0, "mix": 4, "mem": 8, 1: 12}

        drams_of = A.get
        env = dict(locals())
        mix = mixing(nc, env)
        mat = memory_attention(nc, env)

        block = ctx.enter_context(nc.Block())
        drams = A

        @block.sync
        def _(sp):
            sp.dma_start(cols[:, :], drams["cols"]).then_inc(cols_in, 16)
            sp.dma_start(ident[:, :], drams["ident"]).then_inc(ident_in, 16)
            for k, (tt, f) in enumerate(HALF):
                cs = slice(f * (D // 2), (f + 1) * (D // 2))
                sp.dma_start(mem_sb[:, tt, cs], drams["mem"][0, tt * P:(tt + 1) * P, cs]).then_inc(mem_in[k], 16)
            for k in range(PAIR):
                load_slab(sp, S_KV, None, 0, k, drams["w_kv"][k], SLAB)
            ffn_sp(sp, S_GU1, drams["gu1"], drams["gu1_t"], drams["dn1"])
            with sp.Fori(0, 5) as i:
                for k in range(PAIR):
                    load_slab(sp, S_IN, i, PAIR, k, drams["w_in"][bass.ds(i, 1), k].rearrange("a p w -> (a p) w"), SLAB)
            for k in range(PAIR // 2):
                load_slab(sp, S_IN + 5 * PAIR, None, 0, k, drams["w_in5"][k], SLAB)
            for k in range(PAIR // 2):
                load_slab(sp, S_IN + 5 * PAIR, None, 0, 8 + k, drams["w_in_t"][k], 2 * TAIL_IN)
            with sp.Fori(0, 2) as i:
                for k in range(PAIR):
                    load_slab(sp, S_OUT, i, PAIR, k, drams["w_out"][bass.ds(i, 1), k].rearrange("a p w -> (a p) w"), SLAB)
            for k in range(8):
                load_slab(sp, S_MQ, None, 0, k, drams["w_mq"][k], SLAB)
            for k in range(8):
                load_slab(sp, S_MO, None, 0, k, drams["w_mo"][k], SLAB)
            ffn_sp(sp, S_GU2, drams["gu2"], drams["gu2_t"], drams["dn2"])
            for k in range(4):
                cs = slice(k * NCH, (k + 1) * NCH)
                sp.wait_ge(h_ready, 8 * 3 + 2 * (k + 1))
                sp.dma_start(out[0, :, cs].rearrange("(t p) d -> p t d", p=P), h[:, :, cs]).then_inc(out_done, 16)
            sp.wait_ge(out_done, 16 * 4)

        @block.gpsimd
        def _(pool):
            pool.wait_ge(mem_in[3], 16)
            pool.dma_start(h[:, :, :], drams["x"].rearrange("a (t p) d -> p (a t) d", p=P)).then_inc(x_in, 16)
            pool.wait_ge(hT_hi_ready, FFN_PAIRS)
            pool.wait_ge(hT_lo_ready, FFN_PAIRS + CREDIT)
            pool.dma_start(gain[:, :], drams["post1"].partition_broadcast(P)).then_inc(gain_in, 16)
            scale_y(pool, 0, y_x)
            pool.wait_ge(slab_used, S_IN)
            pool.wait_ge(h_ready, 8)
            pool.dma_start(mc[:, :], drams["mc"]).then_inc(mc_in, 16)
            pool.dma_start(w1[:, 0], drams["w1_k"]).then_inc(w1_in, 16)
            pool.dma_start(w1[:, 1], drams["w1_v"]).then_inc(w1_in, 16)
            pool.dma_start(w2[:, 0, :], drams["w2_k"]).then_inc(w1_in, 16)
            pool.dma_start(w2[:, 1, :], drams["w2_k"]).then_inc(w1_in, 16)
            pool.dma_start(w2[:, 2, :], drams["w2_v"]).then_inc(w1_in, 16)
            mix["pool"](pool)
            pool.dma_start(gain[:, :], drams["post2"].partition_broadcast(P)).then_inc(gain_in, 16)
            scale_y(pool, 1, y_b)
            pool.wait_ge(h_ready, 2 * 8)
            pool.dma_start(gain[:, :], drams["post3"].partition_broadcast(P)).then_inc(gain_in, 16)
            scale_y(pool, 2, y_b)
            pool.wait_ge(hT_hi_ready, 2 * FFN_PAIRS)
            pool.wait_ge(hT_lo_ready, 2 * FFN_PAIRS + CREDIT)
            pool.dma_start(gain[:, :], drams["post4"].partition_broadcast(P)).then_inc(gain_in, 16)
            scale_y(pool, 3, y_x)

        @block.scalar
        def _(act):
            for name in ("feat_rows", "feat_T"):
                act.sem_inc(env[name], CREDIT)
            for name in ("g_o_out", "r_y_out"):
                act.sem_inc(sig(name), CREDIT)
            act.wait_ge(cols_in, 16)
            root_tables()
            norm_turn_act(act, 0, "mem", S_KV)
            norm_sums_act(act, 0, mem_sb, lambda k: act.wait_ge(mem_in[k], 16))
            for k in range(AHEAD, PAIR):
                split_hi(act, S_KV, None, 0, k, SLAB)
                if k == 9:
                    act.wait_ge(x_in, 16)
                    norm_sums_act(act, 1, h, lambda k: None)
                if k == 11:
                    used(act, S_KV, None, 0, 7)
                    for tt in range(TT):
                        a = nc.scalar.activation(k_rows[:, tt, :], ps[:, tt, :], ACT.Copy, scale=rstd(0, tt))
                    a.then_inc(kv_rows, 1)
            used(act, S_KV, None, 0, PAIR - 1)
            for tt in range(TT):
                a = nc.scalar.activation(memV[:, tt, :], ps[:, 2 + tt, :], ACT.Copy, scale=rstd(0, tt))
            a.then_inc(kv_rows, 1)
            act.wait_ge(k_turned, 1)
            for b in range(2):
                a = nc.scalar.activation(memKT[:, 2 * b:2 * b + 2, :], ps[:, 4 + b, :].rearrange("p (m t) -> p m t", t=S), ACT.Copy)
            a.then_inc(mem_kv_ready, 1)
            norm_turn_act(act, 1, "ffn1", S_GU1)
            ffn_act(act, 0, S_GU1)
            post_norm_act(act, 0)
            for k in range(2):
                split_hi(act, S_IN, None, 0, k, SLAB)
            norm_turn_act(act, 2, "mix", S_IN, done=2)
            norm_sums_act(act, 2, h, from_residual(act, 0))
            mix["act"](act)
            post_norm_act(act, 1)
            for k in range(2):
                split_hi(act, S_MQ, None, 0, k, SLAB)
            norm_turn_act(act, 3, "mattn", S_MQ, done=2)
            norm_sums_act(act, 3, h, from_residual(act, 1))
            mat["act"](act)
            post_norm_act(act, 2)
            for k in range(2):
                split_hi(act, S_GU2, None, 0, k, SLAB)
            norm_turn_act(act, 4, "ffn2", S_GU2, done=2)
            norm_sums_act(act, 4, h, from_residual(act, 2))
            ffn_act(act, 1, S_GU2)
            post_norm_act(act, 3)

        @block.vector
        def _(dve):
            for name in ("hT_lo_ready", "y_copied", "shifted"):
                dve.sem_inc(env[name], CREDIT)
            dve.wait_ge(cols_in, 16)
            norm_turn_dve(dve, 0, "mem", S_KV)
            norm_rstd_dve(dve, 0)
            for k in range(AHEAD, PAIR):
                split_lo(dve, S_KV, None, 0, k, SLAB)
                if k == 9:
                    norm_rstd_dve(dve, 1)
            norm_turn_dve(dve, 1, "ffn1", S_GU1)
            ffn_dve(dve, 0, S_GU1)
            post_norm_dve(dve, 0, y_x, 0.5)
            norm_turn_dve(dve, 2, "mix", S_IN)
            norm_rstd_dve(dve, 2)
            mix["dve"](dve)
            post_norm_dve(dve, 1, y_b, 1.0)
            norm_turn_dve(dve, 3, "mattn", S_MQ)
            norm_rstd_dve(dve, 3)
            mat["dve"](dve)
            post_norm_dve(dve, 2, y_b, 1.0)
            norm_turn_dve(dve, 4, "ffn2", S_GU2)
            norm_rstd_dve(dve, 4)
            ffn_dve(dve, 1, S_GU2)
            post_norm_dve(dve, 3, y_x, 0.5)

        @block.tensor
        def _(pe):
            for name in ("prod_turned", "feat_turned"):
                pe.sem_inc(env[name], CREDIT)
            for name in ("g_o", "r_y"):
                pe.sem_inc(sig(name), CREDIT)
            pe.wait_ge(ident_in, 16)
            norm_pe(pe, 0, mem_sb, lambda tt, kt: pe.wait_ge(mem_in[2 * tt + kt // 8], 16))
            for c in range(2):
                chunk_products(pe, S_KV, None, 0, 8 * c, NCH, 2 * c, fresh=0 if c == 0 else None)
            pe.wait_ge(kv_rows, 1)
            for hh in range(MH):
                for tt in range(TT):
                    t = nc.tensor.transpose(ps[:, 4 + hh // 2, (hh % 2) * S + tt * P:(hh % 2) * S + (tt + 1) * P],
                                            k_rows[:, tt, hh * P:(hh + 1) * P], ident[:, :])
            t.then_inc(k_turned, 1)
            pe.wait_ge(kv_rows, 2)
            pe.wait_ge(mem_kv_ready, 1)
            norm_pe(pe, 1, h, lambda tt, kt: pe.wait_ge(x_in, 16))
            ffn_pe(pe, 0, S_GU1)
            norm_pe(pe, 2, h, residual_rows(pe, 0))
            mix["pe"](pe)
            norm_pe(pe, 3, h, residual_rows(pe, 1))
            mat["pe"](pe)
            norm_pe(pe, 4, h, residual_rows(pe, 2))
            ffn_pe(pe, 1, S_GU2)


def weight_slabs(w, widths):
    K, N = w.shape
    out, c0 = [], 0
    for wd in widths:
        c = w[:, c0:c0 + wd]
        out.append(c.reshape(K // (2 * P), 2, P, wd).transpose(0, 2, 1, 3).reshape(K // (2 * P), P, 2 * wd))
        c0 += wd
    return out


def down_slabs(w):
    out = np.zeros((4, DOWN, P, SLAB), w.dtype)
    for c in range(4):
        x = w[:, c * NCH:(c + 1) * NCH].reshape(FK, P, NCH)
        out[c, :DOWN - 1] = x[:FK - 1].reshape(DOWN - 1, 2, P, NCH).transpose(0, 2, 1, 3).reshape(DOWN - 1, P, SLAB)
        out[c, DOWN - 1, :, :NCH] = x[FK - 1]
    return out.reshape(2, 2 * DOWN, P, SLAB)


def gate_up_slabs(wg, wu):
    widths = [NCH] * (FFN_PAIRS - 1) + [TAIL_F]
    g, u = weight_slabs(wg, widths), weight_slabs(wu, widths)
    main = np.stack([np.concatenate([a, b]) for a, b in zip(g[:-1], u[:-1])])
    return main, np.concatenate([g[-1], u[-1]])


def channel_columns(parts):
    done = []
    for v, n in parts:
        v = v.reshape(-1)
        x = np.zeros(n * P, v.dtype)
        x[:v.size] = v
        done.append(x.reshape(n, P).T)
    return np.concatenate(done, axis=1)


def kernel(**inputs):
    import concourse.bacc as bacc
    from concourse.bass_utils import run_bass_kernel_spmd

    z = {n: np.asarray(a) for n, a in inputs.items()}
    t = {"x": z["x"], "mem": z["mem"]}
    t["w_kv"] = np.concatenate(weight_slabs(z["mem_w_kv"], [NCH, NCH]))
    t["gu1"], t["gu1_t"] = gate_up_slabs(z["ffn1_w_gate"], z["ffn1_w_up"])
    t["gu2"], t["gu2_t"] = gate_up_slabs(z["ffn2_w_gate"], z["ffn2_w_up"])
    t["dn1"], t["dn2"] = down_slabs(z["ffn1_w_down"]), down_slabs(z["ffn2_w_down"])
    w_in = z["w_in"]
    nsa0 = RW_MAIN + LORA
    w_in = np.concatenate([w_in[:, :RW_MAIN], w_in[:, nsa0:nsa0 + NSA_MAIN], w_in[:, RW_MAIN:nsa0],
                           w_in[:, nsa0 + NSA_MAIN:]], axis=1)
    s = weight_slabs(w_in, [NCH] * 11 + [TAIL_IN])
    t["w_in"] = np.stack([np.concatenate(s[2 * i:2 * i + 2]) for i in range(5)])
    t["w_in5"], t["w_in_t"] = s[10], s[11]
    s = weight_slabs(z["w_out"], [NCH] * 4)
    order = ([(c, 4 + m) for m in range(4) for c in range(3)] + [(c, m) for c in range(3) for m in range(4)]
             + [(3, m) for m in range(8)])
    t["w_out"] = np.stack([s[c][m] for c, m in order]).reshape(2, PAIR, P, SLAB)
    t["w_mq"] = weight_slabs(z["mem_w_q"], [NCH])[0]
    t["w_mo"] = np.concatenate(weight_slabs(z["mem_w_o"], [NCH] * 4))
    t["cols"] = channel_columns([
        (z["mem_norm_g"], 16), (z["ffn1_pre_g"], 16), (z["mix_pre_g"], 16), (z["mem_pre_g"], 16), (z["ffn2_pre_g"], 16),
        (z["cmp_pe_k"], 16), (z["cmp_pe_v"], 16), (z["rw_mu"], 27), (z["rw_w0"], 8), (z["rw_a0"], 8), (z["rw_k_k"], 8),
        (z["rw_k_a"], 8), (z["rw_r_k"], 8), (z["rw_ln_w"], 8), (z["rw_ln_b"], 8)])
    t["ident"] = np.eye(P, dtype=np.float32)
    t["mc"] = shape_constants()
    for a in "kv":
        t["w1_" + a] = np.ascontiguousarray(z["cmp_w1_" + a].reshape(16, P, P).transpose(1, 0, 2))
        t["w2_" + a] = z["cmp_w2_" + a]
    t["loraw_wa"] = np.concatenate([z["rw_w_up"], z["rw_a_up"]])
    t["loraw_g"] = z["rw_g_up"]
    for n, a in enumerate(("ffn1_post_g", "mix_post_g", "mem_post_g", "ffn2_post_g")):
        t[f"post{n + 1}"] = z[a]

    nc = bacc.Bacc("TRN2", target_bir_lowering=False, num_devices=1)
    arrays, drams = {}, {}
    for name, a in t.items():
        a = np.ascontiguousarray(a)
        arrays[f"in_{name}_dram"] = a
        drams[name] = nc.dram_tensor(f"in_{name}_dram", a.shape, mybir.dt.from_np(a.dtype), kind="ExternalInput").ap()
    out = nc.dram_tensor("out_0_dram", (1, S, D), F32, kind="ExternalOutput").ap()
    build(nc, drams, out)
    r = run_bass_kernel_spmd(nc, [arrays], core_ids=[0])
    return r.results[0]["out_0_dram"]
```
